# Optimizing a Trainium2 kernel written in Bass

```python
import math
import jax, jax.numpy as jnp
from jax import lax
import numpy as np

'''One inference step (DEPTH layers) of a hybrid decoder trunk for two request groups sharing weights.

Even layers: one combined input projection feeding two parallel head groups,
  A = gated DeltaNet (short causal conv + SiLU on q/k/v, L2-normed q/k, per-head decay, delta rule, chunked WY form),
  B = differential attention (two softmax maps per head, learned lambda, partial rotary theta=5e5 on first quarter of dims),
  each branch gated by a SiLU path of its own width; outputs concatenated into one output projection.
Odd layers: mLSTM matrix memory (exp input gate, sigmoid forget gate, running-max stabiliser, chunkwise form),
  sigmoid output gate, head RMSNorm, SiLU gate path, output projection.
Pre-RMSNorm before every layer, plain residual adds, one final RMSNorm.

Inputs:
  x_prompt (BATCH, SEQ, D_MODEL); x_sample (DEC_BATCH, DEC_SEQ, D_MODEL)
  cache_k (N_EVEN, N_POOL, PAGE_SIZE, H_B, 2*DQK_B)  paged rotated keys [k1|k2]
  cache_v (N_EVEN, N_POOL, PAGE_SIZE, H_B, DV_B)     paged values
  page_table (DEC_BATCH, N_PAGES) int32, N_PAGES = PAST_LEN // PAGE_SIZE, N_POOL = 5/4 * DEC_BATCH * N_PAGES
  state_gdn_conv (N_EVEN, DEC_BATCH, CONV_W-1, A_CONV_CH); state_gdn_s (N_EVEN, DEC_BATCH, H_A, DK_A, DV_A)
  state_mlstm_c (N_ODD, DEC_BATCH, H_C, DQK_C, DV_C); state_mlstm_n (N_ODD, DEC_BATCH, H_C, DQK_C);
  state_mlstm_m (N_ODD, DEC_BATCH, H_C)
Output tuple:
  y_prompt (BATCH, SEQ, D_MODEL), y_sample (DEC_BATCH, DEC_SEQ, D_MODEL),
  k_rows_prompt (N_EVEN, BATCH, SEQ, H_B, 2*DQK_B), v_rows_prompt (N_EVEN, BATCH, SEQ, H_B, DV_B),
  k_rows_sample (N_EVEN, DEC_BATCH, DEC_SEQ, H_B, 2*DQK_B), v_rows_sample (N_EVEN, DEC_BATCH, DEC_SEQ, H_B, DV_B),
  gdn_conv_prompt (N_EVEN, BATCH, CONV_W-1, A_CONV_CH), gdn_s_prompt (N_EVEN, BATCH, H_A, DK_A, DV_A),
  gdn_conv_sample (N_EVEN, DEC_BATCH, CONV_W-1, A_CONV_CH), gdn_s_sample (N_EVEN, DEC_BATCH, H_A, DK_A, DV_A),
  mlstm_c_prompt (N_ODD, BATCH, H_C, DQK_C, DV_C), mlstm_n_prompt (N_ODD, BATCH, H_C, DQK_C), mlstm_m_prompt (N_ODD, BATCH, H_C),
  mlstm_c_sample (N_ODD, DEC_BATCH, H_C, DQK_C, DV_C), mlstm_n_sample (N_ODD, DEC_BATCH, H_C, DQK_C), mlstm_m_sample (N_ODD, DEC_BATCH, H_C)
'''

D_MODEL = 1024
BATCH = 1
SEQ = 2048
DEPTH = 2
DEC_BATCH = 8
DEC_SEQ = 4
PAST_LEN = 512
PAGE_SIZE = 128

N_EVEN = (DEPTH + 1) // 2
N_ODD = DEPTH // 2
EPS = 1e-6
H_A = 4
DK_A = D_MODEL // 8
DV_A = D_MODEL // 8
CONV_W = 4
CHUNK_A = 64
H_B = 4
DQK_B = D_MODEL // 16
DV_B = 2 * DQK_B
ROPE_DIM = DQK_B // 4
ROPE_THETA = 500000.0
Q_BLOCK = 128
H_C = 4
DQK_C = D_MODEL // 8
DV_C = D_MODEL // 4
CHUNK_C = 64

A_CONV_CH = H_A * (2 * DK_A + DV_A)
W_A = H_A * DV_A
W_B = H_B * DV_B
W_C = H_C * DV_C
EVEN_SPLITS = (A_CONV_CH, W_A, H_A, H_A, H_B * 2 * DQK_B, H_B * 2 * DQK_B, W_B, W_B)
EVEN_IN = sum(EVEN_SPLITS)
ODD_SPLITS = (H_C * DQK_C, H_C * DQK_C, W_C, W_C, W_C, H_C, H_C)
ODD_IN = sum(ODD_SPLITS)

kernel_name = 'hybrid_gdn_diffattn_mlstm_step'

def _split(x, sizes):
    idx = [int(v) for v in np.cumsum(sizes)[:-1]]
    return jnp.split(x, idx, axis=-1)

def _rms_norm(x, w):
    xf = x.astype(jnp.float32)
    y = xf * lax.rsqrt(jnp.mean(xf * xf, axis=-1, keepdims=True) + EPS)
    return (y * w.astype(jnp.float32)).astype(x.dtype)

def _l2norm(x):
    xf = x.astype(jnp.float32)
    return xf * lax.rsqrt(jnp.sum(xf * xf, axis=-1, keepdims=True) + EPS)

def _partial_rope(x, pos):
    half = ROPE_DIM // 2
    inv = jnp.power(ROPE_THETA, -jnp.arange(half, dtype=jnp.float32) / half)
    ang = pos.astype(jnp.float32)[:, None] * inv[None, :]
    shape = (1, pos.shape[0]) + (1,) * (x.ndim - 3) + (half,)
    cos = jnp.cos(ang).reshape(shape)
    sin = jnp.sin(ang).reshape(shape)
    xf = x.astype(jnp.float32)
    x1 = xf[..., :half]
    x2 = xf[..., half:ROPE_DIM]
    rot = jnp.concatenate([x1 * cos - x2 * sin, x2 * cos + x1 * sin, xf[..., ROPE_DIM:]], axis=-1)
    return rot.astype(x.dtype)

def _causal_conv(x, buf, w):
    L = x.shape[1]
    xp = jnp.concatenate([buf.astype(x.dtype), x], axis=1)
    y = xp[:, 0:L] * w[0]
    for j in range(1, CONV_W):
        y = y + xp[:, j:j + L] * w[j]
    return jax.nn.silu(y), xp[:, L:]

def _to_chunks(t, n, c):
    b, _, h, d = t.shape
    return t.astype(jnp.float32).reshape(b, n, c, h, d).transpose(1, 0, 3, 2, 4)

def _gate_chunks(t, n, c):
    b, _, h = t.shape
    return t.astype(jnp.float32).reshape(b, n, c, h).transpose(1, 0, 3, 2)

def _from_chunks(o):
    n, b, h, c, d = o.shape
    return o.transpose(1, 0, 3, 2, 4).reshape(b, n * c, h, d)

def _gated_delta(q, k, v, g, beta, s0):
    L = q.shape[1]
    c = math.gcd(L, CHUNK_A)
    n = L // c
    qc = _to_chunks(q, n, c) * (DK_A ** -0.5)
    kc = _to_chunks(k, n, c)
    vc = _to_chunks(v, n, c)
    gcum = jnp.cumsum(_gate_chunks(g, n, c), axis=-1)
    bc = _gate_chunks(beta, n, c)
    incl = jnp.tril(jnp.ones((c, c), dtype=bool))
    strict = jnp.tril(jnp.ones((c, c), dtype=bool), -1)
    diff = gcum[..., :, None] - gcum[..., None, :]
    decay = jnp.where(incl, jnp.exp(jnp.where(incl, diff, 0.0)), 0.0)
    kk = jnp.einsum('nbhid,nbhjd->nbhij', kc, kc)
    a_low = jnp.where(strict, kk * decay * bc[..., :, None], 0.0)
    lhs = a_low + jnp.eye(c, dtype=jnp.float32)
    rhs = jnp.concatenate([vc * bc[..., None], kc * (bc * jnp.exp(gcum))[..., None]], axis=-1)
    sol = lax.linalg.triangular_solve(lhs, rhs, left_side=True, lower=True, unit_diagonal=True)
    u = sol[..., :DV_A]
    wk = sol[..., DV_A:]
    qk_intra = jnp.einsum('nbhid,nbhjd->nbhij', qc, kc) * decay

    def step(S, xs):
        q_i, k_i, u_i, w_i, g_i, a_i = xs
        v_new = u_i - jnp.einsum('bhcd,bhde->bhce', w_i, S)
        o = jnp.einsum('bhcd,bhde->bhce', q_i * jnp.exp(g_i)[..., None], S) + jnp.einsum('bhij,bhje->bhie', a_i, v_new)
        g_last = g_i[..., -1]
        k_w = k_i * jnp.exp(g_last[..., None] - g_i)[..., None]
        S = S * jnp.exp(g_last)[..., None, None] + jnp.einsum('bhcd,bhce->bhde', k_w, v_new)
        return S, o

    s_fin, o = lax.scan(step, s0.astype(jnp.float32), (qc, kc, u, wk, gcum, qk_intra))
    return _from_chunks(o), s_fin

def _mlstm(q, k, v, log_i, log_f, c0, n0, m0):
    L = q.shape[1]
    c = math.gcd(L, CHUNK_C)
    n = L // c
    qc = _to_chunks(q, n, c) * (DQK_C ** -0.5)
    kc = _to_chunks(k, n, c)
    vc = _to_chunks(v, n, c)
    li = _gate_chunks(log_i, n, c)
    bcum = jnp.cumsum(_gate_chunks(log_f, n, c), axis=-1)
    incl = jnp.tril(jnp.ones((c, c), dtype=bool))
    dmat = jnp.where(incl, bcum[..., :, None] - bcum[..., None, :] + li[..., None, :], -jnp.inf)

    def step(carry, xs):
        cs, ns, ms = carry
        q_i, k_i, v_i, b_i, d_i, l_i = xs
        inter = b_i + ms[..., None]
        m_t = jnp.maximum(inter, jnp.max(d_i, axis=-1))
        w_t = jnp.exp(d_i - m_t[..., None])
        sc = jnp.exp(inter - m_t)
        qk = jnp.einsum('bhid,bhjd->bhij', q_i, k_i) * w_t
        num = sc[..., None] * jnp.einsum('bhcd,bhde->bhce', q_i, cs) + jnp.einsum('bhij,bhje->bhie', qk, v_i)
        den = sc * jnp.einsum('bhcd,bhd->bhc', q_i, ns) + jnp.sum(qk, axis=-1)
        h = num / jnp.maximum(jnp.abs(den), jnp.exp(-m_t))[..., None]
        m_new = m_t[..., -1]
        dec = jnp.exp(b_i[..., -1] + ms - m_new)
        wk = jnp.exp(b_i[..., -1:] - b_i + l_i - m_new[..., None])
        cs = cs * dec[..., None, None] + jnp.einsum('bhcd,bhce->bhde', k_i * wk[..., None], v_i)
        ns = ns * dec[..., None] + jnp.einsum('bhcd,bhc->bhd', k_i, wk)
        return (cs, ns, m_new), h

    carry0 = (c0.astype(jnp.float32), n0.astype(jnp.float32), m0.astype(jnp.float32))
    (c_f, n_f, m_f), h = lax.scan(step, carry0, (qc, kc, vc, bcum, dmat, li))
    return _from_chunks(h), c_f, n_f, m_f

def _diff_attention(q, k, v, lam, start):
    bn, lq = q.shape[0], q.shape[1]
    qb = math.gcd(lq, Q_BLOCK)
    nb = lq // qb
    scale = DQK_B ** -0.5
    kpos = jnp.arange(k.shape[1])
    kf = k.astype(jnp.float32)
    vf = v.astype(jnp.float32)
    q_blocks = q.astype(jnp.float32).reshape(bn, nb, qb, H_B, 2, DQK_B).swapaxes(0, 1)
    starts = start + qb * jnp.arange(nb)

    def block(args):
        qi, s0 = args
        s = jnp.einsum('bqhmd,bkhmd->bhmqk', qi, kf) * scale
        qpos = s0 + jnp.arange(qb)
        s = jnp.where(kpos[None, :] <= qpos[:, None], s, -jnp.inf)
        p = jax.nn.softmax(s, axis=-1)
        a = p[:, :, 0] - lam * p[:, :, 1]
        return jnp.einsum('bhqk,bkhe->bqhe', a, vf)

    o = lax.map(block, (q_blocks, starts))
    return o.swapaxes(0, 1).reshape(bn, lq, H_B, DV_B)

def _even_mixer(h, start, conv_buf, s0, k_past, v_past, w_in, w_out, conv_w, a_log, dt_bias,
                gdn_norm_w, lam_p, diff_norm_w, lambda_init):
    bn, L, _ = h.shape
    proj = h @ w_in
    qkv_a, z_a, b_raw, a_raw, q_b, k_b, v_b, z_b = _split(proj, EVEN_SPLITS)
    qkv_c, new_buf = _causal_conv(qkv_a, conv_buf, conv_w)
    q_a, k_a, v_a = _split(qkv_c, (H_A * DK_A, H_A * DK_A, H_A * DV_A))
    q_a = _l2norm(q_a.reshape(bn, L, H_A, DK_A))
    k_a = _l2norm(k_a.reshape(bn, L, H_A, DK_A))
    v_a = v_a.reshape(bn, L, H_A, DV_A)
    beta = jax.nn.sigmoid(b_raw.astype(jnp.float32))
    g = -jnp.exp(a_log.astype(jnp.float32)) * jax.nn.softplus(a_raw.astype(jnp.float32) + dt_bias.astype(jnp.float32))
    o_a, s_new = _gated_delta(q_a, k_a, v_a, g, beta, s0)
    o_a = _rms_norm(o_a, gdn_norm_w) * jax.nn.silu(z_a.astype(jnp.float32)).reshape(bn, L, H_A, DV_A)
    pos = start + jnp.arange(L)
    q_b = _partial_rope(q_b.reshape(bn, L, H_B, 2, DQK_B), pos)
    k_b = _partial_rope(k_b.reshape(bn, L, H_B, 2, DQK_B), pos)
    v_b = v_b.reshape(bn, L, H_B, DV_B)
    if k_past is None:
        k_all, v_all = k_b, v_b
    else:
        k_all = jnp.concatenate([k_past.astype(k_b.dtype), k_b], axis=1)
        v_all = jnp.concatenate([v_past.astype(v_b.dtype), v_b], axis=1)
    lp = lam_p.astype(jnp.float32)
    lam = jnp.exp(jnp.sum(lp[0] * lp[1])) - jnp.exp(jnp.sum(lp[2] * lp[3])) + lambda_init
    o_b = _diff_attention(q_b, k_all, v_all, lam, start)
    o_b = _rms_norm(o_b, diff_norm_w) * (1.0 - lambda_init) * jax.nn.silu(z_b.astype(jnp.float32)).reshape(bn, L, H_B, DV_B)
    merged = jnp.concatenate([o_a.reshape(bn, L, W_A), o_b.reshape(bn, L, W_B)], axis=-1).astype(h.dtype)
    y = merged @ w_out
    return y, new_buf, s_new, k_b.reshape(bn, L, H_B, 2 * DQK_B), v_b

def _odd_mixer(h, c0, n0, m0, w_in, w_out, b_i, b_f, norm_w):
    bn, L, _ = h.shape
    proj = h @ w_in
    q, k, v, z, o_raw, i_raw, f_raw = _split(proj, ODD_SPLITS)
    q = q.reshape(bn, L, H_C, DQK_C)
    k = k.reshape(bn, L, H_C, DQK_C)
    v = v.reshape(bn, L, H_C, DV_C)
    log_i = i_raw.astype(jnp.float32) + b_i.astype(jnp.float32)
    log_f = jax.nn.log_sigmoid(f_raw.astype(jnp.float32) + b_f.astype(jnp.float32))
    h_t, c_f, n_f, m_f = _mlstm(q, k, v, log_i, log_f, c0, n0, m0)
    h_t = jax.nn.sigmoid(o_raw.astype(jnp.float32)).reshape(bn, L, H_C, DV_C) * h_t
    y = _rms_norm(h_t, norm_w) * jax.nn.silu(z.astype(jnp.float32)).reshape(bn, L, H_C, DV_C)
    return y.reshape(bn, L, W_C).astype(h.dtype) @ w_out, c_f, n_f, m_f

def _trunk(x, start, gdn_conv, gdn_s, ml_c, ml_n, ml_m, cache_k, cache_v, page_table,
           norm_w, final_norm_w, w_in_even, w_out_even, conv_w, a_log, dt_bias, gdn_norm_w,
           lambda_qk, diff_norm_w, w_in_odd, w_out_odd, b_i, b_f, mlstm_norm_w):
    bn = x.shape[0]
    k_rows, v_rows, conv_new, s_new, c_new, n_new, m_new = [], [], [], [], [], [], []
    for layer in range(DEPTH):
        h = _rms_norm(x, norm_w[layer])
        if layer % 2 == 0:
            e = layer // 2
            if page_table is None:
                k_past, v_past = None, None
            else:
                k_past = cache_k[e][page_table].reshape(bn, -1, H_B, 2, DQK_B)
                v_past = cache_v[e][page_table].reshape(bn, -1, H_B, DV_B)
            lambda_init = 0.8 - 0.6 * math.exp(-0.3 * layer)
            y, cb, s, kr, vr = _even_mixer(h, start, gdn_conv[e], gdn_s[e], k_past, v_past,
                                           w_in_even[e], w_out_even[e], conv_w[e], a_log[e], dt_bias[e],
                                           gdn_norm_w[e], lambda_qk[e], diff_norm_w[e], lambda_init)
            k_rows.append(kr)
            v_rows.append(vr)
            conv_new.append(cb)
            s_new.append(s)
        else:
            o = layer // 2
            y, c, n, m = _odd_mixer(h, ml_c[o], ml_n[o], ml_m[o], w_in_odd[o], w_out_odd[o],
                                    b_i[o], b_f[o], mlstm_norm_w[o])
            c_new.append(c)
            n_new.append(n)
            m_new.append(m)
        x = x + y
    states = (jnp.stack(k_rows), jnp.stack(v_rows), jnp.stack(conv_new), jnp.stack(s_new),
              jnp.stack(c_new), jnp.stack(n_new), jnp.stack(m_new))
    return _rms_norm(x, final_norm_w), states

def setup_inputs(seed: int = 0) -> dict:
    key = jax.random.key(seed)
    ks = jax.random.split(key, 26)
    f32 = jnp.float32
    n_pages = PAST_LEN // PAGE_SIZE
    n_pool = (DEC_BATCH * n_pages * 5) // 4

    def nrm(k, shape, s=1.0):
        return jax.random.normal(k, shape, f32) * s

    x_prompt = nrm(ks[0], (BATCH, SEQ, D_MODEL))
    x_sample = nrm(ks[1], (DEC_BATCH, DEC_SEQ, D_MODEL))
    cache_k = nrm(ks[2], (N_EVEN, n_pool, PAGE_SIZE, H_B, 2 * DQK_B))
    cache_v = nrm(ks[3], (N_EVEN, n_pool, PAGE_SIZE, H_B, DV_B))
    page_table = jax.random.permutation(ks[4], n_pool)[: DEC_BATCH * n_pages].reshape(DEC_BATCH, n_pages).astype(jnp.int32)
    state_gdn_conv = nrm(ks[5], (N_EVEN, DEC_BATCH, CONV_W - 1, A_CONV_CH))
    state_gdn_s = nrm(ks[6], (N_EVEN, DEC_BATCH, H_A, DK_A, DV_A), 0.1)
    state_mlstm_c = nrm(ks[7], (N_ODD, DEC_BATCH, H_C, DQK_C, DV_C), 0.1)
    state_mlstm_n = nrm(ks[8], (N_ODD, DEC_BATCH, H_C, DQK_C), 0.1)
    state_mlstm_m = nrm(ks[9], (N_ODD, DEC_BATCH, H_C), 0.5)
    norm_w = 1.0 + nrm(ks[10], (DEPTH, D_MODEL), 0.02)
    final_norm_w = 1.0 + nrm(ks[11], (D_MODEL,), 0.02)
    w_in_even = nrm(ks[12], (N_EVEN, D_MODEL, EVEN_IN), D_MODEL ** -0.5)
    w_out_even = nrm(ks[13], (N_EVEN, W_A + W_B, D_MODEL), (W_A + W_B) ** -0.5)
    conv_w = nrm(ks[14], (N_EVEN, CONV_W, A_CONV_CH), CONV_W ** -0.5)
    a_log = jnp.log(jax.random.uniform(ks[15], (N_EVEN, H_A), f32, 1.0, 16.0))
    dt = jnp.exp(jax.random.uniform(ks[16], (N_EVEN, H_A), f32, math.log(1e-3), math.log(1e-1)))
    dt_bias = dt + jnp.log(-jnp.expm1(-dt))
    gdn_norm_w = 1.0 + nrm(ks[17], (N_EVEN, DV_A), 0.02)
    lambda_qk = nrm(ks[18], (N_EVEN, 4, DQK_B), 0.1)
    diff_norm_w = 1.0 + nrm(ks[19], (N_EVEN, DV_B), 0.02)
    w_in_odd = nrm(ks[20], (N_ODD, D_MODEL, ODD_IN), D_MODEL ** -0.5)
    w_out_odd = nrm(ks[21], (N_ODD, W_C, D_MODEL), W_C ** -0.5)
    b_i = nrm(ks[22], (N_ODD, H_C), 0.1)
    b_f = 3.0 + nrm(ks[23], (N_ODD, H_C), 0.5)
    mlstm_norm_w = 1.0 + nrm(ks[24], (N_ODD, DV_C), 0.02)
    return {'x_prompt': x_prompt, 'x_sample': x_sample, 'cache_k': cache_k, 'cache_v': cache_v,
            'page_table': page_table, 'state_gdn_conv': state_gdn_conv, 'state_gdn_s': state_gdn_s,
            'state_mlstm_c': state_mlstm_c, 'state_mlstm_n': state_mlstm_n, 'state_mlstm_m': state_mlstm_m,
            'norm_w': norm_w, 'final_norm_w': final_norm_w, 'w_in_even': w_in_even, 'w_out_even': w_out_even,
            'conv_w': conv_w, 'a_log': a_log, 'dt_bias': dt_bias, 'gdn_norm_w': gdn_norm_w,
            'lambda_qk': lambda_qk, 'diff_norm_w': diff_norm_w, 'w_in_odd': w_in_odd, 'w_out_odd': w_out_odd,
            'b_i': b_i, 'b_f': b_f, 'mlstm_norm_w': mlstm_norm_w}

def reference(x_prompt, x_sample, cache_k, cache_v, page_table, state_gdn_conv, state_gdn_s,
              state_mlstm_c, state_mlstm_n, state_mlstm_m, norm_w, final_norm_w, w_in_even, w_out_even,
              conv_w, a_log, dt_bias, gdn_norm_w, lambda_qk, diff_norm_w, w_in_odd, w_out_odd,
              b_i, b_f, mlstm_norm_w):
    weights = (norm_w, final_norm_w, w_in_even, w_out_even, conv_w, a_log, dt_bias, gdn_norm_w,
               lambda_qk, diff_norm_w, w_in_odd, w_out_odd, b_i, b_f, mlstm_norm_w)
    bp = x_prompt.shape[0]
    f32 = jnp.float32
    conv0 = jnp.zeros((N_EVEN, bp, CONV_W - 1, A_CONV_CH), x_prompt.dtype)
    s0 = jnp.zeros((N_EVEN, bp, H_A, DK_A, DV_A), f32)
    c0 = jnp.zeros((N_ODD, bp, H_C, DQK_C, DV_C), f32)
    n0 = jnp.zeros((N_ODD, bp, H_C, DQK_C), f32)
    m0 = jnp.zeros((N_ODD, bp, H_C), f32)
    y_prompt, st_p = _trunk(x_prompt, 0, conv0, s0, c0, n0, m0, None, None, None, *weights)
    k_rows_p, v_rows_p, gdn_conv_p, gdn_s_p, ml_c_p, ml_n_p, ml_m_p = st_p
    past_len = page_table.shape[1] * cache_k.shape[2]
    y_sample, st_s = _trunk(x_sample, past_len, state_gdn_conv, state_gdn_s, state_mlstm_c, state_mlstm_n,
                            state_mlstm_m, cache_k, cache_v, page_table, *weights)
    k_rows_s, v_rows_s, gdn_conv_s, gdn_s_s, ml_c_s, ml_n_s, ml_m_s = st_s
    return (y_prompt, y_sample, k_rows_p, v_rows_p, k_rows_s, v_rows_s, gdn_conv_p, gdn_s_p, gdn_conv_s, gdn_s_s,
            ml_c_p, ml_n_p, ml_m_p, ml_c_s, ml_n_s, ml_m_s)


_drawn_inputs = setup_inputs


def setup_inputs(seed=0):
    import zlib

    import numpy as np

    out = dict(_drawn_inputs(seed))
    spreads = {}
    factors = {'final_norm_w': 2.828, 'gdn_norm_w': 4.24, 'diff_norm_w': 4.389, 'mlstm_norm_w': 5.411}
    for name, (base, spread) in spreads.items():
        noise = np.random.default_rng([zlib.crc32(name.encode()), seed]).standard_normal(out[name].shape)
        drawn = base * np.exp(spread * noise) if base else spread * noise
        out[name] = __import__('jax').numpy.asarray(drawn.astype(out[name].dtype))
    for name, factor in factors.items():
        out[name] = (out[name] * factor).astype(out[name].dtype)
    return out
```

```python
from contextlib import ExitStack

import concourse.bass as bass
import numpy as np
from concourse import mybir

F32 = mybir.dt.float32
F32R = mybir.dt.float32r
I32 = mybir.dt.int32
ALU = mybir.AluOpType
ACT = mybir.ActivationFunctionType
AX = mybir.AxisListType

P = 128
D = 1024
KT = D // P
SEQ = 2048
NB = 8
DS = 4
RS = NB * DS
NT = SEQ // P
ROWS = SEQ + RS
H = 4
DK = 128
DV = 256
DQ = 64
ROT = 8
PAST = 512
PAGE = 128
NPG = PAST // PAGE
CONV = 4
CT = 12
WB = 256
EPS = 1e-6
NEG = -1e30
LEVELS = 7
LEVELS_S = 2


class Phase:

    def __init__(self, nc, tag):
        self.nc, self.tag, self.stack, self.sems = nc, tag, ExitStack(), []

    def __enter__(self):
        self.held = self.sem("held")
        return self

    def sb(self, name, shape, dt=F32):
        return self.stack.enter_context(self.nc.sbuf_tensor(name, shape, dt))

    def ps(self, name, shape, dt=F32):
        return self.stack.enter_context(self.nc.psum_tensor(name, shape, dt))

    def sem(self, name):
        s = self.nc.alloc_semaphore(f"{self.tag}_{name}")
        self.sems.append(s)
        return s

    def hold(self, eng, sem, value):
        eng.wait_ge(sem, value)
        if not isinstance(value, int):
            eng.sem_inc(self.held, 1)

    def __exit__(self, *e):
        if e[0] is None:
            self.nc.clear_and_free_semaphores(self.sems)
            self.nc.all_engine_barrier()
        return self.stack.__exit__(*e)


class Chain:

    def __init__(self, eng, sem):
        self.eng, self.sem, self.base, self.n = eng, sem, 0, 0

    def turn(self, base):
        self.base, self.n = base, 0

    def link(self, ins):
        self.n += 1
        ins.then_inc(self.sem, 1)
        self.eng.wait_ge(self.sem, self.base + self.n)


def pairs(eng, count, body):
    with eng.Fori(0, count // 2) as i:
        for s in range(2):
            body(i * 2 + s, s, i)


def turns_of(eng, count, slots, *parts):
    with eng.Fori(0, count // slots) as i:
        for part in parts:
            for s in range(slots):
                part(i * slots + s, s, i)


def load_activations(nc, tag, src, hi, lo, ident_d, norm_d=None):
    N = 4
    with Phase(nc, tag) as ph:
        x = ph.sb(tag + "x", [P, N, D])
        xn = ph.sb(tag + "xn", [P, 2, D])
        junk = ph.sb(tag + "junk", [P, 2, D])
        ms = ph.sb(tag + "ms", [P, N, 3])
        nw = ph.sb(tag + "nw", [P, D])
        ident = ph.sb(tag + "id", [P, P])
        half = ph.sb(tag + "half", [P, 1])
        tp = ph.ps(tag + "tp", [P, N, 2, 4 * P])
        consts_in, halved = ph.sem("consts_in"), ph.sem("halved")
        x_in = [ph.sem(f"x_in{s}") for s in range(N)]
        squares, mean, rstd, normed, transposed, hi_done, lo_done = (
            ph.sem(n) for n in ("squares", "mean", "rstd", "normed", "transposed", "hi_done", "lo_done"))

        def view(s, q, r):
            return tp[:, s, q, :].rearrange("p (k r) -> p k r", k=4)[:, :, :r]

        with nc.Block() as block:

            @block.sync
            def _(sp):
                sp.dma_start(ident[:], ident_d).then_inc(consts_in, 16)
                if norm_d is not None:
                    sp.dma_start(nw[:], norm_d.partition_broadcast(P)).then_inc(consts_in, 16)

                def load(v, s, i, r=P):
                    if norm_d is not None:
                        ph.hold(sp, normed, v + 1)
                    else:
                        ph.hold(sp, transposed, 2 * v + 2)
                    sp.dma_start(x[:r, s, :], src[bass.ds(v * P, r), :]).then_inc(x_in[s], 16)

                turns_of(sp, NT, N, load)
                load(NT, 0, NT // N, RS)

            @block.scalar
            def _(act):
                act.sem_inc(squares, 2)

                def square(v, s, i, r=P):
                    if norm_d is None:
                        return
                    act.wait_ge(x_in[s], i * 16 + 16)
                    act.wait_ge(normed, v + 1)
                    act.wait_ge(squares, v + 1)
                    nc.scalar.activation(junk[:r, s % 2], x[:r, s, :], ACT.Square,
                                         accum_out=ms[:r, s, 0:1]).then_inc(squares, 1)

                def high(v, s, i, r=P):
                    for q in range(2):
                        act.wait_ge(transposed, 2 * (v + N) + q + 1)
                        nc.scalar.activation(hi[:, 4 * q:4 * q + 4, bass.ds(v * P, r)], view(s, q, r), ACT.Copy).then_inc(hi_done, 1)

                turns_of(act, NT, N, square, high)
                square(NT, 0, NT // N, RS)
                high(NT, 0, NT // N, RS)

            @block.gpsimd
            def _(pool):
                if norm_d is None:
                    return
                nc.gpsimd.memset(half[:], -0.5).then_inc(halved, 1)
                pool.wait_ge(halved, 1)

                def root(v, s, i, r=P):
                    ph.hold(pool, mean, v + 1)
                    nc.gpsimd.tensor_tensor(ms[:r, s, 2:3], ms[:r, s, 1:2], half[:r], ALU.pow).then_inc(rstd, 1)

                turns_of(pool, NT, N, root)
                root(NT, 0, NT // N, RS)

            @block.vector
            def _(dve):
                dve.sem_inc(normed, N)
                dve.sem_inc(lo_done, 2 * N)
                dve.wait_ge(consts_in, 16 if norm_d is None else 32)

                def average(v, s, i, r=P):
                    if norm_d is None:
                        return
                    dve.wait_ge(squares, v + 3)
                    nc.vector.tensor_scalar(ms[:r, s, 1:2], ms[:r, s, 0:1], 1.0 / D, EPS,
                                            ALU.mult, ALU.add).then_inc(mean, 1)

                def norm(v, s, i, r=P):
                    if norm_d is None:
                        return
                    dve.wait_ge(rstd, v + 1)
                    dve.wait_ge(transposed, 2 * (v + N - 2) + 2)
                    nc.vector.scalar_tensor_tensor(xn[:r, s % 2, :], x[:r, s, :], ms[:r, s, 2:3], nw[:r],
                                                   ALU.mult, ALU.mult).then_inc(normed, 1)

                def low(v, s, i, r=P):
                    for q in range(2):
                        dve.wait_ge(hi_done, 2 * v + q + 1)
                        part = (slice(None), slice(4 * q, 4 * q + 4), bass.ds(v * P, r))
                        nc.vector.tensor_tensor(lo[part], view(s, q, r), hi[part].bitcast(F32), ALU.subtract).then_inc(lo_done, 1)

                turns_of(dve, NT, N, average, norm, low)
                for part in (average, norm, low):
                    part(NT, 0, NT // N, RS)

            @block.tensor
            def _(pe):
                pe.sem_inc(transposed, 2 * N)
                pe.wait_ge(consts_in, 16 if norm_d is None else 32)

                def transposes(v, s, i, r=P):
                    if norm_d is not None:
                        pe.wait_ge(normed, v + 1 + N)
                    else:
                        pe.wait_ge(x_in[s], i * 16 + 16)
                    rows = x[:r, s] if norm_d is None else xn[:r, s % 2]
                    for q in range(2):
                        pe.wait_ge(lo_done, 2 * v + q + 1)
                        for k in range(4):
                            ins = nc.tensor.transpose(tp[:, s, q, k * P:k * P + r],
                                                      rows[:, (4 * q + k) * P:(4 * q + k + 1) * P], ident[:r, :r])
                        ins.then_inc(transposed, 1)

                turns_of(pe, NT, N, transposes)
                transposes(NT, 0, NT // N, RS)


def project_rows(nc, tag, hi, lo, w, dst, nblocks, residual=None):
    GB = 5
    with Phase(nc, tag) as ph:
        raw = ph.sb(tag + "raw", [P, 2, KT * WB])
        whi = ph.sb(tag + "whi", [P, 2, KT * WB], F32R)
        wlo = ph.sb(tag + "wlo", [P, 2, KT * WB], F32R)
        stage = ph.sb(tag + "stage", [P, 4, 4, WB])
        stage_s = ph.sb(tag + "stage_s", [P, WB])
        acc = ph.ps(tag + "acc", [P, 2, 2, 2, WB])
        acc_s = ph.ps(tag + "acc_s", [P, 2 * WB])
        w_in = [ph.sem("w_in0"), ph.sem("w_in1")]
        w_hi, w_lo, summed, out_a, out_v = (ph.sem(n) for n in ("w_hi", "w_lo", "summed", "out_a", "out_v"))
        stored = [ph.sem(f"stored{g}") for g in range(GB)]
        res_in = [ph.sem(f"res_in{g}") for g in range(GB)]
        dst_t = dst[0:SEQ, :].rearrange("(t p) n -> p t n", p=P)
        res_t = residual[0:SEQ, :].rearrange("(t p) n -> p t n", p=P) if residual is not None else None
        C = 2

        with nc.Block() as block:

            @block.gpsimd
            def _(pool):
                pool.sem_inc(w_lo, C)

                def fetch(n, s, i):
                    ph.hold(pool, w_lo, n + 1)
                    pool.dma_start(raw[:, s, :], w[bass.ds(n, 1)].rearrange("o p n -> (o p) n")).then_inc(w_in[s], 16)

                def split(n, s, i):
                    ph.hold(pool, w_in[s], i * 16 + 16)
                    ph.hold(pool, summed, (n + 1) * GB)
                    nc.gpsimd.tensor_copy(whi[:, s, :], raw[:, s, :]).then_inc(w_hi, 1)
                    ph.hold(pool, w_hi, n + 1)
                    nc.gpsimd.tensor_tensor(wlo[:, s, :], raw[:, s, :], whi[:, s, :].bitcast(F32), ALU.subtract).then_inc(w_lo, 1)

                turns_of(pool, nblocks, 2, fetch, split)

            @block.sync
            def _(sp):
                for g in range(GB):
                    sp.sem_inc(stored[g], 16)

                def blk(n, s, i):
                    cols = bass.ds(n * WB, WB)
                    if residual is not None:
                        for g in range(GB):
                            ph.hold(sp, stored[g], n * 16 + 16)
                            if g < 4:
                                sp.dma_start(stage[:, g], res_t[:, 4 * g:4 * g + 4, cols]).then_inc(res_in[g], 16)
                            else:
                                sp.dma_start(stage_s[:RS], residual[SEQ:ROWS, cols]).then_inc(res_in[g], 16)
                    for g in range(GB):
                        ph.hold(sp, out_v, n * GB + g + 1 + GB)
                        if g < 4:
                            if residual is None:
                                ph.hold(sp, out_a, n * 4 + g + 1 + 4)
                            sp.dma_start(dst_t[:, 4 * g:4 * g + 4, cols], stage[:, g]).then_inc(stored[g], 16)
                        else:
                            sp.dma_start(dst[SEQ:ROWS, cols], stage_s[:RS]).then_inc(stored[g], 16)

                pairs(sp, nblocks, blk)
                for g in range(GB):
                    ph.hold(sp, stored[g], 16 + 16 * nblocks)

            @block.scalar
            def _(act):
                if residual is not None:
                    return
                act.sem_inc(out_a, 4)

                def blk(n, s, i):
                    if residual is None:
                        for g in range(4):
                            act.wait_ge(summed, (n + C) * GB + g + 1)
                            act.wait_ge(stored[g], n * 16 + 16)
                            nc.scalar.activation(stage[:, g, 0:2, :], acc[:, g % 2, 0, :, :], ACT.Copy).then_inc(out_a, 1)

                pairs(act, nblocks, blk)

            @block.vector
            def _(dve):
                dve.sem_inc(out_v, GB)

                def blk(n, s, i):
                    for g in range(GB):
                        dve.wait_ge(summed, (n + C) * GB + g + 1)
                        if residual is not None:
                            dve.wait_ge(res_in[g], n * 16 + 16)
                            if g < 4:
                                nc.vector.tensor_tensor(stage[:, g, 0:2, :], acc[:, g % 2, 0], stage[:, g, 0:2, :], ALU.add)
                                ins = nc.vector.tensor_tensor(stage[:, g, 2:4, :], acc[:, g % 2, 1], stage[:, g, 2:4, :], ALU.add)
                            else:
                                ins = nc.vector.tensor_tensor(stage_s[:RS], acc_s[:RS, :WB], stage_s[:RS], ALU.add)
                        else:
                            dve.wait_ge(stored[g], n * 16 + 16)
                            if g < 4:
                                ins = nc.vector.tensor_copy(stage[:, g, 2:4, :], acc[:, g % 2, 1])
                            else:
                                ins = nc.vector.tensor_copy(stage_s[:RS], acc_s[:RS, :WB])
                        ins.then_inc(out_v, 1)

                pairs(dve, nblocks, blk)

            @block.tensor
            def _(pe):
                pe.sem_inc(summed, C * GB)

                def product(out, v, r, s):
                    for k in range(KT):
                        h = hi[:, k, v * P:v * P + r]
                        l = lo[:, k, v * P:v * P + r]
                        wh = whi[:, s, k * WB:(k + 1) * WB]
                        wl = wlo[:, s, k * WB:(k + 1) * WB]
                        for n, (a, b) in enumerate(((h, wh), (h, wl), (l, wh))):
                            ins = nc.tensor.matmul(out, a, b, start=(k == 0 and n == 0), stop=(k == KT - 1 and n == 2))
                    return ins

                def blk(n, s, i):
                    pe.wait_ge(w_lo, n + 1 + C)
                    for g in range(GB):
                        if g < 4:
                            before = n * GB + g - 2 if g >= 2 else (n - 1) * GB + g + 2
                            before_a = n * 4 + g - 2
                            pe.wait_ge(out_v, before + 1 + GB)
                            if residual is None:
                                pe.wait_ge(out_a, before_a + 1 + 4)
                            for t in range(4):
                                ins = product(acc[:, g % 2, t // 2, t % 2, :], 4 * g + t, P, s)
                        else:
                            pe.wait_ge(out_v, n * GB + g + 1)
                            ins = product(acc_s[:RS, :WB], NT, RS, s)
                        ins.then_inc(summed, 1)

                pairs(pe, nblocks, blk)


def project_conv(nc, hi, lo, w, conv_w, conv_state, conv_t, conv_s, state_p, state_s):
    BL = 4
    TB = SEQ // BL
    HIST = CONV - 1
    with Phase(nc, "conv") as ph:
        wr = ph.sb("cwr", [P, 2, D])
        whi = ph.sb("cwhi", [P, 2, D], F32R)
        wlo = ph.sb("cwlo", [P, 2, D], F32R)
        cw = ph.sb("ccw", [P, CT * CONV])
        cwh = ph.sb("ccwh", [P, CT * CONV])
        x = ph.sb("cx", [P, 2, HIST + SEQ])
        xs = ph.sb("cxs", [P, 2, NB, HIST + DS])
        y = ph.sb("cy", [P, 2, SEQ + RS])
        th = ph.sb("cth", [P, SEQ + RS])
        acc = ph.ps("cacc", [P, BL, TB])
        acc_s = ph.ps("cacc_s", [P, 2, TB])
        w_in = [ph.sem("cw_in0"), ph.sem("cw_in1")]
        small_in, w_hi, w_lo, summed, halves, zeroed = (
            ph.sem(n) for n in ("small_in", "w_hi", "w_lo", "summed", "halves", "zeroed"))
        raw_a, conved, tanhed, siluc, chained = (
            ph.sem(n) for n in ("raw_a", "conved", "tanhed", "siluc", "chained"))
        state_in = [ph.sem("state_in0"), ph.sem("state_in1")]
        stored = [ph.sem("stored0"), ph.sem("stored1")]
        C = 2

        with nc.Block() as block:

            @block.gpsimd
            def _(pool):
                nc.gpsimd.memset(x[:, :, 0:HIST], 0.0).then_inc(zeroed, 1)

                pool.sem_inc(w_lo, C)

                def fetch(n, s, i):
                    ph.hold(pool, w_lo, n + 1)
                    pool.dma_start(wr[:, s, :], w[bass.ds(n, 1)].rearrange("o p n -> (o p) n")).then_inc(w_in[s], 16)

                def split(n, s, i):
                    ph.hold(pool, w_in[s], i * 16 + 16)
                    ph.hold(pool, summed, (n + 1) * (BL + 1))
                    nc.gpsimd.tensor_copy(whi[:, s, :], wr[:, s, :]).then_inc(w_hi, 1)
                    ph.hold(pool, w_hi, n + 1)
                    nc.gpsimd.tensor_tensor(wlo[:, s, :], wr[:, s, :], whi[:, s, :].bitcast(F32), ALU.subtract).then_inc(w_lo, 1)

                turns_of(pool, CT, 2, fetch, split)

            @block.sync
            def _(sp):
                for s in range(2):
                    sp.sem_inc(stored[s], 64)
                sp.dma_start(cw[:], conv_w).then_inc(small_in, 16)

                def load(n, s, i):
                    ph.hold(sp, conved, n + 1)
                    ph.hold(sp, stored[s], i * 64 + 64)
                    sp.dma_start(xs[:, s, :, 0:HIST], conv_state[bass.ds(n, 1)].rearrange("o p b t -> (o p) b t")).then_inc(state_in[s], 16)

                def put(n, s, i):
                    ph.hold(sp, raw_a, (n + 1) * (BL + 1) + BL + 1)
                    sp.dma_start(state_p[bass.ds(n, 1)].rearrange("o p t -> (o p) t"), x[:, s, SEQ:SEQ + HIST],
                                 allow_slow_non_contiguous=True).then_inc(stored[s], 16)
                    sp.dma_start(state_s[bass.ds(n, 1)].rearrange("o p b t -> (o p) b t"), xs[:, s, :, DS:DS + HIST],
                                 allow_slow_non_contiguous=True).then_inc(stored[s], 16)
                    ph.hold(sp, siluc, n + 1)
                    sp.dma_start(conv_t[bass.ds(n * P, P), :], y[:, s, :SEQ]).then_inc(stored[s], 16)
                    sp.dma_start(conv_s[bass.ds(n * P, P), :], y[:, s, SEQ:]).then_inc(stored[s], 16)

                turns_of(sp, CT, 2, load, put)
                for s in range(2):
                    sp.wait_ge(stored[s], 64 + 64 * CT // 2)

            @block.scalar
            def _(act):
                act.sem_inc(raw_a, BL + 1)

                def copies(n, s, i):
                    act.wait_ge(conved, n + 1)
                    act.wait_ge(stored[s], i * 64 + 64)
                    for b in range(BL + 1):
                        act.wait_ge(summed, (n + C) * (BL + 1) + b + 1)
                        if b < BL:
                            nc.scalar.activation(x[:, s, HIST + b * TB:HIST + (b + 1) * TB], acc[:, b], ACT.Copy).then_inc(raw_a, 1)
                        else:
                            nc.scalar.activation(xs[:, s, :, HIST:], acc_s[:, 0, :RS].rearrange("p (b t) -> p b t", b=NB),
                                                 ACT.Copy).then_inc(raw_a, 1)
                    act.wait_ge(conved, n + 1 + C)
                    nc.scalar.activation(th[:], y[:, s], ACT.Tanh).then_inc(tanhed, 1)

                pairs(act, CT, copies)

            @block.vector
            def _(dve):
                dve.sem_inc(conved, C)
                dve.wait_ge(small_in, 16)
                nc.vector.tensor_scalar(cwh[:], cw[:], 0.5, None, ALU.mult).then_inc(halves, 1)
                dve.wait_ge(halves, 1)
                dve.wait_ge(zeroed, 1)
                chain = Chain(dve, chained)

                def ch(n, s, i):
                    chain.turn(n * (2 * (CONV - 1)))
                    dve.wait_ge(raw_a, (n + 1) * (BL + 1) + BL + 1)
                    dve.wait_ge(state_in[s], i * 16 + 16)
                    dve.wait_ge(stored[s], i * 64 + 64)
                    ys = y[:, s, SEQ:].rearrange("p (b t) -> p b t", b=NB)
                    for out, src in ((y[:, s, :SEQ], lambda j: x[:, s, j:j + SEQ]), (ys, lambda j: xs[:, s, :, j:j + DS])):
                        tap = lambda j: cwh[:, bass.ds(n * CONV + j, 1)]
                        chain.link(nc.vector.tensor_scalar(out, src(0), tap(0), None, ALU.mult))
                        for j in range(1, CONV):
                            ins = nc.vector.scalar_tensor_tensor(out, src(j), tap(j), out, ALU.mult, ALU.add)
                            if j < CONV - 1:
                                chain.link(ins)
                    ins.then_inc(conved, 1)
                    dve.wait_ge(tanhed, n + 1)
                    nc.vector.scalar_tensor_tensor(y[:, s], th[:], 1.0, y[:, s], ALU.add, ALU.mult).then_inc(siluc, 1)
                    assert chain.n == 2 * (CONV - 1)

                pairs(dve, CT, ch)

            @block.tensor
            def _(pe):
                pe.sem_inc(summed, C * (BL + 1))

                def ch(n, s, i):
                    pe.wait_ge(w_lo, n + 1 + C)
                    for b in range(BL + 1):
                        pe.wait_ge(raw_a, n * (BL + 1) + b + 1)
                        cols = slice(b * TB, (b + 1) * TB) if b < BL else slice(SEQ, ROWS)
                        out = acc[:, b] if b < BL else acc_s[:, 0, :RS]
                        for k in range(KT):
                            wh, wl = whi[:, s, k * P:(k + 1) * P], wlo[:, s, k * P:(k + 1) * P]
                            for m, (a, z) in enumerate(((wh, hi), (wh, lo), (wl, hi))):
                                ins = nc.tensor.matmul(out, a, z[:, k, cols], start=(k == 0 and m == 0),
                                                       stop=(k == KT - 1 and m == 2))
                        ins.then_inc(summed, 1)

                pairs(pe, CT, ch)


def project_gates(nc, tag, hi, lo, w, vecs, fold_d, gates, kind):
    with Phase(nc, tag + "g") as ph:
        raw = ph.sb(tag + "graw", [P, KT, 8])
        whl = ph.sb(tag + "gwhl", [P, KT, 16], F32R)
        wh0 = ph.sb(tag + "gwh0", [P, KT, 16], F32R)
        g16 = ph.sb(tag + "g16", [16, ROWS])
        fold = ph.sb(tag + "gfold", [16, 8])
        vec = ph.sb(tag + "gvec", [P, 8])
        vecx = ph.sb(tag + "gvecx", [P, 4])
        z = ph.sb(tag + "gz", [P, NT + 1, 8])
        t = [ph.sb(tag + f"gt{j}", [P, NT + 1, 4]) for j in range(4)]
        acc = ph.ps(tag + "gacc", [P, NT + 1, 8])
        gt = [ph.ps(tag + f"gcols{b}", [P, 512]) for b in range(5)]
        w_in, zeroed, w_hi, w_lo, columns, copied, summed, out, act_done, chained = (
            ph.sem(n) for n in ("w_in", "zeroed", "w_hi", "w_lo", "columns", "copied", "summed", "out", "act_done", "chained"))
        with nc.Block() as block:

            @block.sync
            def _(sp):
                sp.dma_start(raw[:].rearrange("p k n -> p (k n)"), w).then_inc(w_in, 16)
                sp.dma_start(fold[:], fold_d).then_inc(w_in, 16)
                sp.dma_start(vec[:], vecs.partition_broadcast(P)).then_inc(w_in, 16)

            @block.tensor
            def _(pe):
                pe.wait_ge(w_lo, 1)
                for b in range(5):
                    cols = slice(b * 512, min(ROWS, (b + 1) * 512))
                    for k in range(KT):
                        nc.tensor.matmul(gt[b][:16, :cols.stop - cols.start], whl[:, k, :], hi[:, k, cols], start=(k == 0), stop=False)
                        ins = nc.tensor.matmul(gt[b][:16, :cols.stop - cols.start], wh0[:, k, :], lo[:, k, cols], start=False, stop=(k == KT - 1))
                    ins.then_inc(columns, 1)
                for v in range(NT + 1):
                    r = P if v < NT else RS
                    pe.wait_ge(copied, v // 4 + 1)
                    ins = nc.tensor.matmul(acc[:r, v, :], g16[:, v * P:v * P + r], fold[:], start=True, stop=True)
                ins.then_inc(summed, 1)

            @block.scalar
            def _(act):
                act.wait_ge(w_in, 48)
                act.wait_ge(zeroed, 1)
                nc.scalar.activation(whl[:, :, 0:8], raw[:], ACT.Copy)
                nc.scalar.activation(wh0[:, :, 0:8], raw[:], ACT.Copy).then_inc(w_hi, 1)
                for b in range(5):
                    act.wait_ge(columns, b + 1)
                    w = min(512, ROWS - b * 512)
                    nc.scalar.activation(g16[:, b * 512:b * 512 + w], gt[b][:16, :w], ACT.Copy).then_inc(copied, 1)
                if kind == "gdn":
                    nc.scalar.activation(vecx[:], vec[:, 0:4], ACT.Exp).then_inc(act_done, 1)
                else:
                    act.sem_inc(act_done, 1)
                act.wait_ge(out, 1)
                if kind == "gdn":
                    nc.scalar.activation(t[3][:], z[:, :, 0:4], ACT.Tanh, scale=0.5).then_inc(act_done, 1)
                else:
                    act.sem_inc(act_done, 1)
                nc.scalar.activation(t[1][:], t[0][:], ACT.Exp, scale=-1.0).then_inc(act_done, 1)
                act.wait_ge(act_done, 3)
                nc.scalar.activation(t[1][:], t[1][:], ACT.Ln, bias=1.0).then_inc(act_done, 1)

            @block.vector
            def _(dve):
                chain = Chain(dve, chained)
                nc.vector.memset(wh0[:].bitcast(F32), 0.0).then_inc(zeroed, 1)
                chain.link(nc.vector.memset(z[:], 0.0))
                dve.wait_ge(w_hi, 1)
                nc.vector.tensor_tensor(whl[:, :, 8:16], raw[:], whl[:, :, 0:8].bitcast(F32), ALU.subtract).then_inc(w_lo, 1)
                dve.wait_ge(summed, 1)
                nc.vector.tensor_copy(z[:, 0:NT, :], acc[:, 0:NT, :])
                chain.link(nc.vector.tensor_copy(z[:RS, NT, :], acc[:RS, NT, :]))
                bias = vec[:, 4:8].rearrange("p (o h) -> p o h", o=1).to_broadcast([P, NT + 1, 4])
                chain.link(nc.vector.tensor_tensor(t[2][:], z[:, :, 4:8], bias, ALU.add))
                sign = 1.0 if kind == "gdn" else -1.0
                if kind != "gdn":
                    chain.link(nc.vector.tensor_scalar(t[2][:], t[2][:], -1.0, None, ALU.mult))
                chain.link(nc.vector.tensor_scalar(t[0][:], t[2][:], -1.0, None, ALU.mult))
                nc.vector.tensor_tensor(t[0][:], t[0][:], t[2][:], ALU.max).then_inc(out, 1)
                dve.wait_ge(act_done, 4)
                chain.link(nc.vector.scalar_tensor_tensor(t[2][:], t[2][:], 0.0, t[1][:], ALU.max, ALU.add))
                if kind == "gdn":
                    rate = vecx[:].rearrange("p (o h) -> p o h", o=1).to_broadcast([P, NT + 1, 4])
                    chain.link(nc.vector.scalar_tensor_tensor(gates[:, :, 0:4], t[2][:], -1.0, rate, ALU.mult, ALU.mult))
                    chain.link(nc.vector.tensor_scalar(gates[:, :, 4:8], t[3][:], 1.0, 0.5, ALU.add, ALU.mult))
                else:
                    bi = vec[:, 0:4].rearrange("p (o h) -> p o h", o=1).to_broadcast([P, NT + 1, 4])
                    chain.link(nc.vector.tensor_scalar(gates[:, :, 0:4], t[2][:], -1.0, None, ALU.mult))
                    chain.link(nc.vector.tensor_tensor(gates[:, :, 4:8], z[:, :, 0:4], bi, ALU.add))


def spread(ap, n):
    return ap.rearrange("p (h o) -> p h o", o=1).to_broadcast([ap.shape[0], ap.shape[1], n])


def repeat(ap, n):
    return ap.rearrange("p (o r) -> p o r", o=1).to_broadcast([ap.shape[0], n, ap.shape[1]])


class Events:

    def __init__(self, ph, names):
        self.ph, self.s = ph, {n: ph.sem(n) for n in names.split()}

    def __getitem__(self, name):
        return self.s[name]

    def open(self, eng, names):
        for n in names.split():
            eng.sem_inc(self.s[n], 1)

    def done(self, eng, name, v):
        self.ph.hold(eng, self.s[name], v + 2)

    def prev(self, eng, name, v):
        self.ph.hold(eng, self.s[name], v + 1)


def gated_delta(nc, a, proj, conv_t, conv_s, gates, merged, out_p, out_s):
    with Phase(nc, "gdn") as ph:
        sb, ps = ph.sb, ph.ps
        ident, ones = sb("d_id", [P, P]), sb("d_ones", [P, P])
        upper, levels = sb("d_up", [P, P]), sb("d_lv", [P, LEVELS, P])
        upper_s, levels_s, same_s = sb("d_ups", [RS, RS]), sb("d_lvs", [RS, LEVELS_S, RS]), sb("d_sms", [RS, RS])
        member, own = sb("d_mem", [RS, NB]), sb("d_own", [P, NB, RS])
        nw, pw = sb("d_nw", [P, DK]), sb("d_pw", [P, 8])
        c = sb("d_c", [P, 2, CT, P])
        z = sb("d_z", [P, 2, 512])
        gt, sm, rn = sb("d_gt", [P, 8]), sb("d_sm", [P, 16]), sb("d_rn", [P, 8])
        kd, egc = sb("d_kd", [P, 8]), sb("d_egc", [P, 4])
        sq, dgn = sb("d_sq", [P, 8, P]), sb("d_dgn", [P, 8, P])
        dgu, dgb = sb("d_dgu", [P, H, P]), sb("d_dgb", [P, H, P])
        eg, dt = sb("d_eg", [P, H, P]), sb("d_dt", [P, H, P])
        qk = sb("d_qk", [P, 8, P])
        kt, vt = sb("d_kt", [P, H, DK]), sb("d_vt", [P, H, DK])
        qt, at = sb("d_qt", [P, H, P]), sb("d_at", [P, H, P])
        mt = sb("d_mt", [P, LEVELS, H, P])
        T, U, Y = sb("d_T", [P, H, P]), sb("d_U", [P, H, P]), sb("d_Y", [P, H, P])
        r1, vn = sb("d_r1", [P, H, DK]), sb("d_vn", [P, H, DK])
        qg, kw = sb("d_qg", [P, H, P]), sb("d_kw", [P, H, DK])
        osq, th, zs, og = (sb("d_" + n, [P, H, DK]) for n in ("osq", "th", "zs", "og"))
        oss, rr = sb("d_oss", [P, 8]), sb("d_rr", [P, 4])
        S, Ss = sb("d_S", [P, H, 1, DK]), sb("d_Ss", [P, H, NB, DK])
        kts, qgs = sb("d_kts", [P, H, NB, RS]), sb("d_qgs", [P, H, NB, RS])
        kws = sb("d_kws", [RS, NB, H, DK])
        bank = [ps(f"d_b{n}", [P, 512]) for n in range(8)]

        consts_in, set_up = ph.sem("consts_in"), ph.sem("set_up")
        c_in, z_in = [ph.sem("c_in0"), ph.sem("c_in1")], [ph.sem("z_in0"), ph.sem("z_in1")]
        NAMES = ("gate sq small smc rn dgs dgn rows bcn eg kd dT DT qk kkq tok tokc qkt kS r vn vnc qg kw o dS "
                 "S osq th ms rr zs og")
        ev = Events(ph, NAMES)
        mts, ys, ycs, tyus, tus = (ph.sem(n) for n in ("mt", "y", "yc", "tyu", "tu"))
        stored, chained, chained_p, freed, batch_dS, batch_S = (
            ph.sem(n) for n in ("stored", "chained", "chained_p", "freed", "batch_dS", "batch_S"))

        def kinds(eng, tile):
            pairs(eng, NT, lambda v, s, i: tile(v, s, i, P, 1, upper, levels, LEVELS, S))
            tile(NT, 0, NT // 2, RS, NB, upper_s, levels_s, LEVELS_S, Ss)

        def v3(b, r, w, rows=None):
            return bank[b][:(rows or P), :H * w].rearrange("p (h r) -> p h r", h=H)

        with nc.Block() as block:

            @block.sync
            def _(sp):
                loads = [(ident[:], a["ident"]), (ones[:], a["same"]), (upper[:], a["upper"]), (levels[:], a["levels"]),
                         (upper_s[:], a["upper_s"]), (levels_s[:], a["levels_s"]), (same_s[:], a["same_s"]),
                         (member[:], a["member"]), (own[:], a["own"].partition_broadcast(P)),
                         (nw[:], a["gdn_norm"].partition_broadcast(P)), (Ss[:], a["gdn_state"])]
                for dst, src in loads:
                    sp.dma_start(dst, src).then_inc(consts_in, 16)
                assert len(loads) == 11
                sp.sem_inc(stored, 16)

                def load(v, s, i, r, n):
                    sp_c = conv_t if n == 1 else conv_s
                    ph.hold(sp, freed, v + 1)
                    cols = bass.ds(v * P, r) if n == 1 else slice(0, RS)
                    sp.dma_start(c[:, s, :, :r], sp_c.rearrange("(c p) t -> p c t", p=P)[:, :, cols]).then_inc(c_in[s], 16)
                    sp.dma_start(z[:r, s, :], proj[bass.ds(v * P, r), 0:512]).then_inc(z_in[s], 16)

                sp.sem_inc(freed, 2)

                def put(v, s, r):
                    ev.done(sp, "og", v)
                    sp.dma_start(merged[bass.ds(v * P, r), 0:512], og[:r].rearrange("p h d -> p (h d)")).then_inc(stored, 16)

                with sp.Fori(0, NT // 2) as i:
                    for s in range(2):
                        load(i * 2 + s, s, i, P, 1)
                    for s in range(2):
                        put(i * 2 + s, s, P)
                load(NT, 0, NT // 2, RS, NB)
                put(NT, 0, RS)
                ev.done(sp, "S", NT - 1)
                sp.dma_start(out_p, S[:, :, 0, :]).then_inc(stored, 16)
                sp.wait_ge(batch_S, NB)
                sp.dma_start(out_s, Ss[:]).then_inc(stored, 16)
                sp.wait_ge(stored, 16 * (NT + 4))

            @block.gpsimd
            def _(pool):
                ev.open(pool, "rn qg kw zs rr")
                pool.sem_inc(mts, 1)
                nc.gpsimd.memset(pw[:], -0.5).then_inc(set_up, 1)
                nc.gpsimd.memset(S[:], 0.0).then_inc(set_up, 1)
                pool.wait_ge(set_up, 2)
                pool.wait_ge(consts_in, 16 * 11)
                chain = Chain(pool, chained_p)

                def tile(v, s, i, r, n, up, lv, L, St):
                    chain.turn(v * 2)
                    lv0 = v * LEVELS
                    ev.done(pool, "smc", v)
                    ev.prev(pool, "dgn", v)
                    nc.gpsimd.tensor_tensor(rn[:r], sm[:r, 0:8], pw[:r], ALU.pow).then_inc(ev["rn"], 1)
                    ev.done(pool, "qk", v)
                    ev.done(pool, "eg", v)
                    ev.prev(pool, "o", v)
                    nc.gpsimd.tensor_tensor(qg[:, :, :r], qk[:, 0:4, :r], eg[:, :, :r], ALU.mult).then_inc(ev["qg"], 1)
                    ev.done(pool, "qkt", v)
                    for l in range(L):
                        nc.gpsimd.tensor_tensor(mt[:r, l, :, :r], at[:r, :, :r], repeat(lv[:r, l, :r], H),
                                                ALU.mult).then_inc(mts, 1)
                    ev.done(pool, "tokc", v)
                    ev.done(pool, "DT", v)
                    ev.prev(pool, "dS", v)
                    nc.gpsimd.tensor_tensor(kw[:r], kt[:r], spread(kd[:r, 4:8], DK), ALU.mult).then_inc(ev["kw"], 1)
                    ev.done(pool, "th", v)
                    ev.prev(pool, "og", v)
                    chain.link(nc.gpsimd.tensor_scalar(zs[:r], th[:r], 1.0, 0.5, ALU.add, ALU.mult))
                    chain.link(nc.gpsimd.tensor_tensor(zs[:r], zs[:r], z[:r, s, :].rearrange("p (h d) -> p h d", h=H), ALU.mult))
                    nc.gpsimd.tensor_tensor(zs[:r], zs[:r], repeat(nw[:r], H), ALU.mult).then_inc(ev["zs"], 1)
                    ev.done(pool, "ms", v)
                    nc.gpsimd.tensor_tensor(rr[:r], oss[:r, 4:8], pw[:r, 0:4], ALU.pow).then_inc(ev["rr"], 1)
                    assert chain.n == 2

                kinds(pool, tile)

            @block.scalar
            def _(act):
                ev.open(act, "sq eg DT tokc vnc th osq")
                act.sem_inc(ycs, 1)

                def tile(v, s, i, r, n, up, lv, L, St):
                    yc0 = v * (LEVELS - 1)
                    act.wait_ge(c_in[s], i * 16 + 16)
                    ev.prev(act, "small", v)
                    nc.scalar.activation(sq[:, :, :r], c[:, s, 0:8, :r], ACT.Square).then_inc(ev["sq"], 1)
                    ev.done(act, "smc", v)
                    ev.prev(act, "S", v)
                    ev.prev(act, "qg", v)
                    nc.scalar.activation(egc[:r], sm[:r, 8:12], ACT.Exp)
                    ev.done(act, "dT", v)
                    nc.scalar.activation(eg[:, :, :r], v3(3, r, r), ACT.Exp).then_inc(ev["eg"], 1)
                    ev.done(act, "kd", v)
                    ev.prev(act, "kw", v)
                    nc.scalar.activation(kd[:r, 4:8], kd[:r, 0:4], ACT.Exp)
                    nc.scalar.activation(dt[:r, :, :r], dt[:r, :, :r], ACT.Exp).then_inc(ev["DT"], 1)
                    ev.done(act, "tok", v)
                    ev.prev(act, "r", v)
                    nc.scalar.activation(kt[:r], v3(5, r, DK, r), ACT.Copy)
                    nc.scalar.activation(vt[:r], v3(6, r, DK, r), ACT.Copy).then_inc(ev["tokc"], 1)
                    for l in range(1, L):
                        act.wait_ge(ys, v * LEVELS + l + 1)
                        nc.scalar.activation(Y[:r, :, :r], v3(7, r, r, r), ACT.Copy).then_inc(ycs, 1)
                    ev.done(act, "vn", v)
                    ev.prev(act, "dS", v)
                    nc.scalar.activation(vn[:r], v3(5, r, DK, r), ACT.Copy).then_inc(ev["vnc"], 1)
                    act.wait_ge(z_in[s], i * 16 + 16)
                    ev.prev(act, "zs", v)
                    nc.scalar.activation(th[:r], z[:r, s, :].rearrange("p (h d) -> p h d", h=H), ACT.Tanh, scale=0.5).then_inc(ev["th"], 1)
                    ev.done(act, "o", v)
                    ev.prev(act, "ms", v)
                    nc.scalar.activation(osq[:r], v3(6, r, DK, r), ACT.Square).then_inc(ev["osq"], 1)

                kinds(act, tile)

            @block.vector
            def _(dve):
                ev.open(dve, "gate smc dgs dgn kd dT qk qkt r S ms og")
                dve.sem_inc(tus, 1)
                dve.wait_ge(consts_in, 16 * 11)
                dve.wait_ge(set_up, 2)
                chain = Chain(dve, chained)
                PER = 6

                def tile(v, s, i, r, n, up, lv, L, St):
                    chain.turn(v * PER)
                    ev.prev(dve, "small", v)
                    nc.vector.tensor_copy(gt[:r], gates[:r, bass.ds(v, 1), :].rearrange("p o h -> p (o h)")).then_inc(ev["gate"], 1)
                    ev.done(dve, "gate", v)
                    ev.prev(dve, "rows", v)
                    nc.vector.tensor_tensor(dgu[:r, :, :r], spread(gt[:r, 0:4], r), repeat(up[:r, :r], H), ALU.mult)
                    nc.vector.tensor_tensor(dgb[:r, :, :r], spread(gt[:r, 4:8], r), repeat(ident[:r, :r], H), ALU.mult).then_inc(ev["dgs"], 1)
                    ev.done(dve, "small", v)
                    ev.prev(dve, "rn", v)
                    nc.vector.tensor_scalar(sm[:r, 0:8], bank[0][:r, 0:8], EPS, None, ALU.add)
                    nc.vector.tensor_copy(sm[:r, 8:16], bank[0][:r, 8:16]).then_inc(ev["smc"], 1)
                    ev.done(dve, "rn", v)
                    ev.prev(dve, "bcn", v)
                    nc.vector.scalar_tensor_tensor(dgn[:r, 0:4, :r], spread(rn[:r, 0:4], r), DK ** -0.5,
                                                   repeat(ident[:r, :r], H), ALU.mult, ALU.mult)
                    nc.vector.tensor_tensor(dgn[:r, 4:8, :r], spread(rn[:r, 4:8], r), repeat(ident[:r, :r], H), ALU.mult).then_inc(ev["dgn"], 1)
                    ev.done(dve, "smc", v)
                    nc.vector.tensor_tensor(kd[:r, 0:4], sm[:r, 12:16], sm[:r, 8:12], ALU.subtract).then_inc(ev["kd"], 1)
                    ev.done(dve, "rows", v)
                    for h in range(H):
                        ins = nc.vector.tensor_scalar(dt[:r, h, :r], bank[3][:r, h * r:(h + 1) * r], sm[:r, 8 + h:9 + h], 0.0,
                                                      ALU.subtract, ALU.min)
                    ins.then_inc(ev["dT"], 1)
                    ev.done(dve, "bcn", v)
                    dve.wait_ge(c_in[s], i * 16 + 16)
                    ev.prev(dve, "kS", v)
                    ev.prev(dve, "qg", v)
                    nc.vector.tensor_tensor(qk[:, 0:4, :r], c[:, s, 0:4, :r], v3(1, r, r), ALU.mult)
                    nc.vector.tensor_tensor(qk[:, 4:8, :r], c[:, s, 4:8, :r], v3(2, r, r), ALU.mult).then_inc(ev["qk"], 1)
                    ev.done(dve, "DT", v)
                    chain.link(nc.vector.tensor_tensor(dt[:r, :, :r], dt[:r, :, :r], repeat(up[:r, :r], H), ALU.mult))
                    ev.done(dve, "kkq", v)
                    ev.prev(dve, "o", v)
                    nc.vector.tensor_tensor(qt[:r, :, :r], v3(2, r, r, r), dt[:r, :, :r], ALU.mult)
                    chain.link(nc.vector.tensor_tensor(at[:r, :, :r], v3(1, r, r, r), dt[:r, :, :r], ALU.mult))
                    nc.vector.tensor_tensor(at[:r, :, :r], at[:r, :, :r], v3(4, r, r, r), ALU.mult).then_inc(ev["qkt"], 1)
                    if n > 1:
                        ev.done(dve, "qk", v)
                        ev.done(dve, "qg", v)
                        for h in range(H):
                            nc.vector.tensor_tensor(kts[:, h], repeat(qk[:, 4 + h, :r], NB), own[:], ALU.mult)
                            ins = nc.vector.tensor_tensor(qgs[:, h], repeat(qg[:, h, :r], NB), own[:], ALU.mult)
                        chain.link(ins)
                    ev.prev(dve, "vn", v)
                    dve.wait_ge(mts, v * LEVELS + 2)
                    dve.wait_ge(ys, v * LEVELS + 1)
                    nc.vector.tensor_tensor(T[:r, :, :r], repeat(ident[:r, :r], H), v3(7, r, r, r), ALU.subtract)
                    nc.vector.tensor_tensor(U[:r, :, :r], repeat(ident[:r, :r], H), mt[:r, 0, :, :r], ALU.subtract).then_inc(tus, 1)
                    for l in range(1, L):
                        dve.wait_ge(tyus, v * (LEVELS - 1) + l)
                        dve.wait_ge(tus, v * LEVELS + l + 1)
                        if l < L - 1:
                            nc.vector.tensor_tensor(T[:r, :, :r], T[:r, :, :r], v3(5, r, r, r), ALU.subtract)
                        nc.vector.tensor_tensor(U[:r, :, :r], U[:r, :, :r], v3(6, r, r, r), ALU.subtract).then_inc(tus, 1)
                    ev.done(dve, "kS", v)
                    ev.done(dve, "eg", v)
                    chain.link(nc.vector.tensor_tensor(r1[:r], v3(7, r, DK, r), spread(egc[:r], DK), ALU.mult))
                    ev.done(dve, "tokc", v)
                    chain.link(nc.vector.tensor_tensor(r1[:r], vt[:r], r1[:r], ALU.subtract))
                    nc.vector.tensor_tensor(r1[:r], r1[:r], spread(gt[:r, 4:8], DK), ALU.mult).then_inc(ev["r"], 1)
                    if n == 1:
                        ev.done(dve, "dS", v)
                        for h in range(H):
                            ins = nc.vector.scalar_tensor_tensor(S[:, h, 0, :], S[:, h, 0, :], eg[:, h, r - 1:r],
                                                                 bank[7][:, h * DK:(h + 1) * DK], ALU.mult, ALU.add)
                        ins.then_inc(ev["S"], 1)
                    else:
                        ev.done(dve, "kw", v)
                        for b in range(NB):
                            ins = nc.vector.tensor_scalar(kws[:, b], kw[:r], member[:, b:b + 1], None, ALU.mult)
                        ins.then_inc(ev["S"], 1)
                        for b in range(NB):
                            dve.wait_ge(batch_dS, b + 1)
                            for h in range(H):
                                ins = nc.vector.scalar_tensor_tensor(
                                    Ss[:, h, b, :], Ss[:, h, b, :], eg[:, h, DS * b + DS - 1:DS * b + DS],
                                    bank[7][:, h * DK:(h + 1) * DK], ALU.mult, ALU.add)
                            ins.then_inc(batch_S, 1)
                    ev.done(dve, "osq", v)
                    chain.link(nc.vector.tensor_reduce(oss[:r, 0:4], osq[:r], AX.X, ALU.add))
                    ev.prev(dve, "rr", v)
                    nc.vector.tensor_scalar(oss[:r, 4:8], oss[:r, 0:4], 1.0 / DK, EPS, ALU.mult, ALU.add).then_inc(ev["ms"], 1)
                    ev.done(dve, "rr", v)
                    dve.wait_ge(stored, v * 16 + 16)
                    chain.link(nc.vector.tensor_tensor(og[:r], v3(6, r, DK, r), spread(rr[:r], DK), ALU.mult))
                    ev.done(dve, "zs", v)
                    nc.vector.tensor_tensor(og[:r], og[:r], zs[:r], ALU.mult).then_inc(ev["og"], 1)
                    ev.done(dve, "tok", v)
                    dve.sem_inc(freed, 1)
                    assert n > 1 or chain.n == PER

                kinds(dve, tile)

            @block.tensor
            def _(pe):
                ev.open(pe, "small rows bcn kkq tok kS vn o dS")
                pe.wait_ge(consts_in, 16 * 11)
                mm = nc.tensor.matmul

                def tile(v, s, i, r, n, up, lv, L, St):
                    ev.done(pe, "sq", v)
                    ev.prev(pe, "smc", v)
                    for j in range(8):
                        mm(bank[0][:r, j:j + 1], sq[:, j, :r], ones[:, 0:1], start=True, stop=True)
                    ev.done(pe, "gate", v)
                    same = ones if n == 1 else same_s
                    mm(bank[0][:r, 8:12], up[:r, :r], gt[:r, 0:4], start=True, stop=True)
                    mm(bank[0][:r, 12:16], same[:r, :r], gt[:r, 0:4], start=True, stop=True).then_inc(ev["small"], 1)
                    ev.done(pe, "dgs", v)
                    ev.prev(pe, "dT", v)
                    ev.prev(pe, "eg", v)
                    ev.prev(pe, "qkt", v)
                    mm(bank[3][:, :H * r], ones[:r, :], dgu[:r, :, :r], start=True, stop=True)
                    mm(bank[4][:r, :H * r], ones[:r, :r], dgb[:r, :, :r], start=True, stop=True).then_inc(ev["rows"], 1)
                    ev.done(pe, "dgn", v)
                    mm(bank[1][:, :H * r], ones[:r, :], dgn[:r, 0:4, :r], start=True, stop=True)
                    mm(bank[2][:, :H * r], ones[:r, :], dgn[:r, 4:8, :r], start=True, stop=True).then_inc(ev["bcn"], 1)
                    ev.done(pe, "qk", v)
                    for h in range(H):
                        mm(bank[1][:r, h * r:(h + 1) * r], qk[:, 4 + h, :r], qk[:, 4 + h, :r], start=True, stop=True)
                        ins = mm(bank[2][:r, h * r:(h + 1) * r], qk[:, 4 + h, :r], qk[:, h, :r], start=True, stop=True)
                    ins.then_inc(ev["kkq"], 1)
                    ev.prev(pe, "vnc", v)
                    ev.prev(pe, "og", v)
                    pe.wait_ge(c_in[s], i * 16 + 16)
                    for h in range(H):
                        nc.tensor.transpose(bank[5][:r, h * DK:(h + 1) * DK], qk[:, 4 + h, :r], ident[:])
                        ins = nc.tensor.transpose(bank[6][:r, h * DK:(h + 1) * DK], c[:, s, 8 + h, :r], ident[:])
                    ins.then_inc(ev["tok"], 1)
                    ev.prev(pe, "S", v)
                    for l in range(L):
                        pe.wait_ge(mts, v * LEVELS + l + 2)
                        if l:
                            pe.wait_ge(tus, v * LEVELS + l + 1)
                        for h in range(H):
                            out, m = bank[7][:r, h * r:(h + 1) * r], mt[:r, l, h, :r]
                            ins = mm(out, m, T[:r, h, :r], start=True, stop=True) if l else nc.tensor.transpose(out, m, ident[:r, :r])
                        ins.then_inc(ys, 1)
                        if l:
                            pe.wait_ge(ycs, v * (LEVELS - 1) + l + 1)
                            if l == 1:
                                ev.done(pe, "tokc", v)
                            for h in range(H):
                                if l < L - 1:
                                    mm(bank[5][:r, h * r:(h + 1) * r], U[:r, h, :r], Y[:r, h, :r], start=True, stop=True)
                                ins = mm(bank[6][:r, h * r:(h + 1) * r], Y[:r, h, :r], U[:r, h, :r], start=True, stop=True)
                            ins.then_inc(tyus, 1)
                    pe.wait_ge(tus, v * LEVELS + L + 1)
                    for h in range(H):
                        for b in range(n):
                            ins = mm(bank[7][:r, h * DK:(h + 1) * DK], qk[:, 4 + h, :r] if n == 1 else kts[:, h, b],
                                     St[:, h, b, :], start=(b == 0), stop=(b == n - 1))
                    ins.then_inc(ev["kS"], 1)
                    ev.done(pe, "r", v)
                    for h in range(H):
                        ins = mm(bank[5][:r, h * DK:(h + 1) * DK], U[:r, h, :r], r1[:r, h, :], start=True, stop=True)
                    ins.then_inc(ev["vn"], 1)
                    ev.done(pe, "vnc", v)
                    ev.done(pe, "qg", v)
                    for h in range(H):
                        for b in range(n):
                            mm(bank[6][:r, h * DK:(h + 1) * DK], qg[:, h, :r] if n == 1 else qgs[:, h, b],
                               St[:, h, b, :], start=(b == 0), stop=False)
                        ins = mm(bank[6][:r, h * DK:(h + 1) * DK], qt[:r, h, :r], vn[:r, h, :], start=False, stop=True)
                    ins.then_inc(ev["o"], 1)
                    ev.done(pe, "kw", v)
                    if n == 1:
                        for h in range(H):
                            ins = mm(bank[7][:, h * DK:(h + 1) * DK], kw[:r, h, :], vn[:r, h, :], start=True, stop=True)
                        ins.then_inc(ev["dS"], 1)
                    else:
                        ev.done(pe, "S", v)
                        for b in range(NB):
                            if b:
                                pe.wait_ge(batch_S, b)
                            for h in range(H):
                                ins = mm(bank[7][:, h * DK:(h + 1) * DK], kws[:, b, h, :], vn[:r, h, :], start=True, stop=True)
                            ins.then_inc(batch_dS, 1)

                kinds(pe, tile)


LAMBDA_INIT = 0.8 - 0.6
KEEP = 1.0 - LAMBDA_INIT
TURNS = 2 * 2 * H


def attention_inputs(nc, a, proj, k_rows, v_rows, qT, kT, V, G, nlam):
    with Phase(nc, "rope") as ph:
        x = ph.sb("r_x", [P, 2, TURNS, DQ])
        cos, sin = ph.sb("r_cos", [P, NT + 1, ROT]), ph.sb("r_sin", [P, NT + 1, ROT])
        t = ph.sb("r_t", [P, 4, TURNS, ROT])
        th = ph.sb("r_th", [P, 512])
        nw, ident = ph.sb("r_nw", [P, DK]), ph.sb("r_id", [P, P])
        lq, lp, le = ph.sb("r_lq", [P, 4, DQ]), ph.sb("r_lp", [P, 2, DQ]), ph.sb("r_le", [P, 4])
        tq = [ph.ps(f"r_tq{s}", [P, 512]) for s in range(2)]
        tk = [ph.ps(f"r_tk{s}", [P, 512]) for s in range(2)]
        consts_in, rows_in, cached, lam_in, lam_exp, chained = (
            ph.sem(n) for n in ("consts_in", "rows_in", "cached", "lam_in", "lam_exp", "chained"))
        x_in = [ph.sem("x_in0"), ph.sem("x_in1")]
        k_out = [ph.sem("k_out0"), ph.sem("k_out1")]
        ev = Events(ph, "turned trans qcopy kcopy th gated")
        with nc.Block() as block:

            @block.sync
            def _(sp):
                for dst, src in ((cos[:], a["cos"]), (sin[:], a["sin"]), (ident[:], a["ident"]),
                                 (nw[:], a["diff_norm"].partition_broadcast(P)),
                                 (lq[:].rearrange("p a b -> p (a b)"), a["lambda_qk"].partition_broadcast(P))):
                    sp.dma_start(dst, src).then_inc(consts_in, 16)
                for dst, c0 in ((V, 1536), (G, 2048)):
                    sp.dma_start(dst[:, 0:NT, :], proj[0:SEQ, c0:c0 + 512].rearrange("(t p) n -> p t n", p=P)).then_inc(rows_in, 16)
                    sp.dma_start(dst[:RS, NT, :], proj[SEQ:ROWS, c0:c0 + 512]).then_inc(rows_in, 16)
                sp.dma_start(v_rows, proj[:, 1536:2048]).then_inc(cached, 16)
                for s in range(2):
                    sp.sem_inc(k_out[s], 16)

                def load(v, s, i, r):
                    ph.hold(sp, ev["trans"], v + 1)
                    ph.hold(sp, k_out[s], i * 16 + 16)
                    sp.dma_start(x[:r, s].rearrange("p a b -> p (a b)"), proj[bass.ds(v * P, r), 512:1536]).then_inc(x_in[s], 16)

                def put(v, s, i, r):
                    ev.done(sp, "turned", v)
                    sp.dma_start(k_rows[bass.ds(v * P, r), :],
                                 x[:r, s, TURNS // 2:, :].rearrange("p a b -> p (a b)")).then_inc(k_out[s], 16)

                with sp.Fori(0, NT // 2) as i:
                    for s in range(2):
                        load(i * 2 + s, s, i, P)
                    for s in range(2):
                        put(i * 2 + s, s, i, P)
                load(NT, 0, NT // 2, RS)
                put(NT, 0, NT // 2, RS)
                sp.wait_ge(cached, 16)
                sp.wait_ge(k_out[0], 16 * (2 + NT // 2))
                sp.wait_ge(k_out[1], 16 * (1 + NT // 2))

            @block.tensor
            def _(pe):
                pe.sem_inc(ev["trans"], 2)
                pe.wait_ge(consts_in, 80)

                def tile(v, s, i, r=P):
                    ev.done(pe, "turned", v)
                    pe.wait_ge(ev["qcopy"], v + 1)
                    pe.wait_ge(ev["kcopy"], v + 1)
                    for h in range(H):
                        nc.tensor.transpose(tq[s][:, h * P:h * P + r], x[:r, s, 2 * h:2 * h + 2, :].rearrange("p a b -> p (a b)"), ident[:r, :r])
                        ins = nc.tensor.transpose(tk[s][:, h * P:h * P + r],
                                                  x[:r, s, TURNS // 2 + 2 * h:TURNS // 2 + 2 * h + 2, :].rearrange("p a b -> p (a b)"), ident[:r, :r])
                    ins.then_inc(ev["trans"], 1)

                pairs(pe, NT, tile)
                tile(NT, 0, NT // 2, RS)

            @block.scalar
            def _(act):
                act.sem_inc(ev["qcopy"], 2)
                act.sem_inc(ev["th"], 1)
                act.wait_ge(lam_in, 1)
                nc.scalar.activation(le[:, 2:4], le[:, 0:2], ACT.Exp).then_inc(lam_exp, 1)
                act.wait_ge(rows_in, 64)

                def tile(v, s, i, r=P):
                    ev.prev(act, "gated", v)
                    nc.scalar.activation(th[:r], G[:r, bass.ds(v, 1), :].rearrange("p o n -> p (o n)"), ACT.Tanh,
                                         scale=0.5).then_inc(ev["th"], 1)
                    act.wait_ge(ev["trans"], v + 3)
                    nc.scalar.activation(qT[:, :, bass.ds(v * P, r)], tq[s][:].rearrange("p (h r) -> p h r", h=H)[:, :, :r],
                                         ACT.Copy, scale=DQ ** -0.5).then_inc(ev["qcopy"], 1)

                pairs(act, NT, tile)
                tile(NT, 0, NT // 2, RS)

            @block.vector
            def _(dve):
                dve.sem_inc(ev["kcopy"], 2)
                ev.open(dve, "turned gated")
                dve.wait_ge(consts_in, 80)
                dve.wait_ge(rows_in, 64)
                chain = Chain(dve, chained)
                lqv = lq[:].rearrange("p (a two) b -> p a two b", two=2)
                chain.link(nc.vector.tensor_tensor(lp[:], lqv[:, :, 0, :], lqv[:, :, 1, :], ALU.mult))
                nc.vector.tensor_reduce(le[:, 0:2], lp[:], AX.X, ALU.add).then_inc(lam_in, 1)
                dve.wait_ge(lam_exp, 1)
                chain.link(nc.vector.tensor_tensor(nlam[:], le[:, 3:4], le[:, 2:3], ALU.subtract))
                chain.link(nc.vector.tensor_scalar(nlam[:], nlam[:], LAMBDA_INIT, None, ALU.subtract))
                first = chain.n
                PER = 3

                def tile(v, s, i, r=P):
                    chain.turn(v * PER + first)
                    dve.wait_ge(x_in[s], i * 16 + 16)
                    cs, sn = (repeat(m[:r, bass.ds(v, 1), :].rearrange("p o f -> p (o f)"), TURNS) for m in (cos, sin))
                    lead, trail = x[:r, s, :, 0:ROT], x[:r, s, :, ROT:2 * ROT]
                    for n, (u, w) in enumerate(((lead, cs), (trail, sn), (trail, cs), (lead, sn))):
                        ins = nc.vector.tensor_tensor(t[:r, n], u, w, ALU.mult)
                    chain.link(ins)
                    nc.vector.tensor_tensor(lead, t[:r, 0], t[:r, 1], ALU.subtract)
                    nc.vector.tensor_tensor(trail, t[:r, 2], t[:r, 3], ALU.add).then_inc(ev["turned"], 1)
                    ev.done(dve, "th", v)
                    g = G[:r, bass.ds(v, 1), :].rearrange("p o n -> p (o n)")
                    gh = G[:r, bass.ds(v, 1), :].rearrange("p o (h n) -> p (o h) n", h=H)
                    chain.link(nc.vector.scalar_tensor_tensor(g, th[:r], 1.0, g, ALU.add, ALU.mult))
                    chain.link(nc.vector.scalar_tensor_tensor(gh, gh, 0.5 * KEEP, repeat(nw[:r], H), ALU.mult, ALU.mult))
                    dve.sem_inc(ev["gated"], 1)
                    dve.wait_ge(ev["trans"], v + 3)
                    nc.vector.tensor_copy(kT[:, :, bass.ds(v * P, r)], tk[s][:].rearrange("p (h r) -> p h r", h=H)[:, :, :r]).then_inc(ev["kcopy"], 1)
                    assert chain.n == PER

                pairs(dve, NT, tile)
                tile(NT, 0, NT // 2, RS)


def prompt_attention(nc, a, merged, qT, kT, V, G, nlam):
    SB = 4
    width = [(qi + 1) * P for qi in range(NT)]
    banks = [-(-w // 512) for w in width]
    first_s = [2 * sum(banks[:qi]) for qi in range(NT)]
    first_a = [sum(banks[:qi]) for qi in range(NT)]
    PS, PA = 2 * sum(banks), sum(banks)
    assert PS % SB == 0 and PA % 2 == 0
    with Phase(nc, "attn") as ph:
        qz = ph.sb("t_qz", [P, 2, 2, P])
        p = ph.sb("t_p", [P, 2, 2, SEQ])
        aT = ph.sb("t_aT", [P, 2, 4, P])
        mx, nm = ph.sb("t_mx", [P, 2, 2, 4]), ph.sb("t_nm", [P, 2, 2])
        ls, lr = ph.sb("t_ls", [P, 2, 2, 4]), ph.sb("t_lr", [P, 2, 4])
        oss, rr = ph.sb("t_oss", [P, 2, 2]), ph.sb("t_rr", [P, 2])
        junk, og = ph.sb("t_junk", [P, 2, DK]), ph.sb("t_og", [P, 2, DK])
        ident, causal, pw = ph.sb("t_id", [P, P]), ph.sb("t_causal", [P, P]), ph.sb("t_pw", [P, 1])
        score = [ph.ps(f"t_s{n}", [P, 512]) for n in range(SB)]
        tps = [ph.ps(f"t_t{n}", [P, 512]) for n in range(2)]
        out = [ph.ps(f"t_o{n}", [P, 512]) for n in range(2)]
        consts_in, set_up, chained = ph.sem("consts_in"), ph.sem("set_up"), ph.sem("chained")
        q_set, maxed, weighted, gathered, squared, mean, rstd, gated = (
            ph.sem(n) for n in ("q_set", "maxed", "weighted", "gathered", "squared", "mean", "rstd", "gated"))
        q_half = ph.sem("q_half")
        scored, expd, turned, copied = (ph.sem(n) for n in ("scored", "expd", "turned", "copied"))
        stored = [ph.sem("stored0"), ph.sem("stored1")]
        PER = NT * (2 * 2 + 3) + sum(banks)

        early = lambda qi: range(0, (banks[qi] + 1) // 2)
        late = lambda qi: range((banks[qi] + 1) // 2, banks[qi])

        def heads(eng, body):
            with eng.Fori(0, H) as h:
                body(h)

        with nc.Block() as block:

            @block.sync
            def _(sp):
                sp.dma_start(ident[:], a["ident"]).then_inc(consts_in, 16)
                sp.dma_start(causal[:], a["causal"]).then_inc(consts_in, 16)
                for s in range(2):
                    sp.sem_inc(stored[s], 16)

                def head(h):
                    for qi in range(NT):
                        ph.hold(sp, gated, h * NT + qi + 1)
                        sp.dma_start(merged[qi * P:(qi + 1) * P, bass.ds(h * DK + 512, DK)], og[:, qi % 2, :]).then_inc(stored[qi % 2], 16)

                heads(sp, head)
                for s in range(2):
                    sp.wait_ge(stored[s], 16 * (1 + H * NT // 2))

            @block.gpsimd
            def _(pool):
                nc.gpsimd.memset(pw[:], -0.5).then_inc(set_up, 1)
                nc.gpsimd.memset(qz[:], 0.0).then_inc(set_up, 1)
                pool.wait_ge(set_up, 2)

                def head(h):
                    def query(qi):
                        before = first_s[qi - 1] if qi >= 2 else [first_s[NT - 1], PS][qi] - PS
                        ph.hold(pool, scored, h * PS + before + PS)
                        nc.gpsimd.tensor_copy(qz[0:DQ, qi % 2, 0, :], qT[0:DQ, bass.ds(h, 1), qi * P:(qi + 1) * P].rearrange("p o r -> p (o r)")).then_inc(q_half, 1)
                        ph.hold(pool, q_half, h * NT + qi + 1)
                        nc.gpsimd.tensor_copy(qz[DQ:P, qi % 2, 1, :], qT[DQ:P, bass.ds(h, 1), qi * P:(qi + 1) * P].rearrange("p o r -> p (o r)")).then_inc(q_set, 1)
                        ph.hold(pool, q_set, h * NT + qi + 1)

                    def root(qi):
                        ph.hold(pool, mean, h * NT + qi + 1)
                        nc.gpsimd.tensor_tensor(rr[:, qi % 2:qi % 2 + 1], oss[:, qi % 2, 1:2], pw[:], ALU.pow).then_inc(rstd, 1)
                        ph.hold(pool, rstd, h * NT + qi + 1)

                    query(0)
                    query(1)
                    for qi in range(NT):
                        if qi + 2 < NT:
                            query(qi + 2)
                        if qi:
                            root(qi - 1)
                    root(NT - 1)

                heads(pool, head)

            @block.scalar
            def _(act):
                act.sem_inc(expd, SB)
                act.sem_inc(copied, 2)

                def head(h):
                    def exps(qi, m):
                        s = qi % 2
                        act.wait_ge(maxed, (h * NT + qi) * 2 + m + 1)
                        if qi >= 2 and m == 0:
                            act.wait_ge(turned, h * PA + first_a[qi - 1])
                        for b in range(banks[qi]):
                            k = first_s[qi] + m * banks[qi] + b
                            w = min(512, width[qi] - b * 512)
                            nc.scalar.activation(p[:, s, m, b * 512:b * 512 + w], score[k % SB][:, :w], ACT.Exp,
                                                 bias=nm[:, s, m:m + 1], accum_out=ls[:, s, m, b:b + 1]).then_inc(expd, 1)

                    def copies(qi, groups):
                        for g in groups:
                            k = first_a[qi] + g
                            n = min(4, qi + 1 - 4 * g)
                            act.wait_ge(turned, h * PA + k + 1)
                            act.wait_ge(gathered, h * PA + k + 1)
                            nc.scalar.activation(aT[:, k % 2, :n, :], tps[k % 2][:, :n * P].rearrange("p (n r) -> p n r", n=n),
                                                 ACT.Copy).then_inc(copied, 1)

                    def square(qi):
                        s = qi % 2
                        act.wait_ge(gathered, h * PA + first_a[qi] + banks[qi] + 2)
                        nc.scalar.activation(junk[:, s, :], out[s][:, :DK], ACT.Square, accum_out=oss[:, s, 0:1]).then_inc(squared, 1)

                    exps(0, 0)
                    exps(0, 1)
                    for qi in range(NT):
                        copies(qi, early(qi))
                        if qi:
                            square(qi - 1)
                        if qi + 1 < NT:
                            exps(qi + 1, 0)
                        copies(qi, late(qi))
                        if qi + 1 < NT:
                            exps(qi + 1, 1)
                    square(NT - 1)

                heads(act, head)

            @block.vector
            def _(dve):
                dve.wait_ge(consts_in, 32)
                chain = Chain(dve, chained)

                def head(h):
                    chain.turn(h * PER)

                    def maxima(qi, m):
                        s = qi % 2
                        for b in range(banks[qi]):
                            k = first_s[qi] + m * banks[qi] + b
                            w = min(512, width[qi] - b * 512)
                            dve.wait_ge(scored, h * PS + k + 1 + PS)
                            if b == banks[qi] - 1:
                                chain.link(nc.vector.tensor_tensor(score[k % SB][:, w - P:w], score[k % SB][:, w - P:w], causal[:], ALU.add))
                            ins = nc.vector.tensor_reduce(mx[:, s, m, b:b + 1], score[k % SB][:, :w], AX.X, ALU.max)
                        chain.link(ins)
                        nc.vector.tensor_reduce(nm[:, s, m:m + 1], mx[:, s, m, :banks[qi]], AX.X, ALU.max,
                                                negate=True).then_inc(maxed, 1)

                    def weights(qi):
                        s, w, n = qi % 2, width[qi], banks[qi]
                        dve.wait_ge(expd, h * PS + first_s[qi] + 2 * n + SB)
                        chain.link(nc.vector.tensor_reduce(lr[:, s, 0:2], ls[:, s, :, :n], AX.X, ALU.add))
                        chain.link(nc.vector.reciprocal(lr[:, s, 2:4], lr[:, s, 0:2]))
                        chain.link(nc.vector.tensor_scalar(lr[:, s, 3:4], lr[:, s, 3:4], nlam[:], None, ALU.mult))
                        for b in range(n):
                            c = slice(b * 512, min(w, b * 512 + 512))
                            chain.link(nc.vector.tensor_scalar(p[:, s, 0, c], p[:, s, 0, c], lr[:, s, 2:3], None, ALU.mult))
                            nc.vector.scalar_tensor_tensor(p[:, s, 0, c], p[:, s, 1, c], lr[:, s, 3:4], p[:, s, 0, c],
                                                           ALU.mult, ALU.add).then_inc(weighted, 1)

                    def square_mean(qi):
                        s = qi % 2
                        dve.wait_ge(squared, h * NT + qi + 1)
                        nc.vector.tensor_scalar(oss[:, s, 1:2], oss[:, s, 0:1], 1.0 / DK, EPS, ALU.mult, ALU.add).then_inc(mean, 1)

                    def gate(qi):
                        s = qi % 2
                        dve.wait_ge(rstd, h * NT + qi + 1)
                        dve.wait_ge(stored[s], (h * (NT // 2) + qi // 2) * 16 + 16)
                        nc.vector.scalar_tensor_tensor(og[:, s, :], out[s][:, :DK], rr[:, s:s + 1],
                                                       G[:, qi, bass.ds(h * DK, DK)], ALU.mult, ALU.mult).then_inc(gated, 1)

                    maxima(0, 0)
                    maxima(0, 1)
                    weights(0)
                    for qi in range(NT):
                        if qi + 1 < NT:
                            maxima(qi + 1, 0)
                        if qi:
                            square_mean(qi - 1)
                        if qi + 1 < NT:
                            maxima(qi + 1, 1)
                        if qi:
                            gate(qi - 1)
                        if qi + 1 < NT:
                            weights(qi + 1)
                    square_mean(NT - 1)
                    gate(NT - 1)
                    assert chain.n == PER

                heads(dve, head)

            @block.tensor
            def _(pe):
                pe.sem_inc(scored, PS)
                pe.sem_inc(gathered, 2)
                pe.wait_ge(consts_in, 32)

                def head(h):
                    def scores(qi, m):
                        if m == 0:
                            pe.wait_ge(q_set, h * NT + qi + 1)
                        for b in range(banks[qi]):
                            k = first_s[qi] + m * banks[qi] + b
                            w = min(512, width[qi] - b * 512)
                            pe.wait_ge(expd, h * PS + k + 1)
                            nc.tensor.matmul(score[k % SB][:, :w], qz[:, qi % 2, m, :],
                                             kT[:, bass.ds(h, 1), b * 512:b * 512 + w].rearrange("p o r -> p (o r)"),
                                             start=True, stop=True).then_inc(scored, 1)

                    def turn(qi, g):
                        k = first_a[qi] + g
                        pe.wait_ge(weighted, h * PA + k + 1)
                        pe.wait_ge(copied, h * PA + k + 1)
                        for t in range(4 * g, min(4 * g + 4, qi + 1)):
                            ins = nc.tensor.transpose(tps[k % 2][:, (t % 4) * P:(t % 4 + 1) * P], p[:, qi % 2, 0, t * P:(t + 1) * P], ident[:])
                        ins.then_inc(turned, 1)

                    def gather(qi, g):
                        k = first_a[qi] + g
                        pe.wait_ge(copied, h * PA + k + 3)
                        if g == 0 and qi >= 2:
                            pe.wait_ge(gated, h * NT + qi - 1)
                        for t in range(4 * g, min(4 * g + 4, qi + 1)):
                            ins = nc.tensor.matmul(out[qi % 2][:, :DK], aT[:, k % 2, t % 4, :], V[:, t, bass.ds(h * DK, DK)],
                                                   start=(t == 0), stop=(t == qi))
                        ins.then_inc(gathered, 1)

                    def groups(qi, some):
                        for g in some:
                            if g == 0:
                                turn(qi, 0)
                            if g + 1 < banks[qi]:
                                turn(qi, g + 1)
                            gather(qi, g)

                    scores(0, 0)
                    scores(0, 1)
                    for qi in range(NT):
                        if qi + 1 < NT:
                            scores(qi + 1, 0)
                        groups(qi, early(qi))
                        if qi + 1 < NT:
                            scores(qi + 1, 1)
                        groups(qi, late(qi))

                heads(pe, head)


def sample_attention(nc, a, merged, qT, kT, V, G, nlam):
    GR, PER = 2, NB // 2
    with Phase(nc, "samp") as ph:
        qs = ph.sb("s_qs", [P, PER * H, P])
        kp = ph.sb("s_kp", [P, NPG, 512])
        vp = ph.sb("s_vp", [P, PER, NPG, 512])
        kTp = ph.sb("s_kTp", [P, 2, H, PAST])
        p = ph.sb("s_p", [P, PAST + RS])
        aT = ph.sb("s_aT", [P, NPG + 1, 64])
        oT = ph.sb("s_oT", [P, H, NB, DS])
        mx, st = ph.sb("s_mx", [P, 4]), ph.sb("s_st", [P, 8])
        ident, fold, map2 = ph.sb("s_id", [P, P]), ph.sb("s_fold", [P, 64]), ph.sb("s_map", [P, 2])
        mask, pg, pw = ph.sb("s_mask", [P, GR, RS]), ph.sb("s_pg", [1, NB * NPG], I32), ph.sb("s_pw", [P, 4])
        osq, oss, og = ph.sb("s_osq", [RS, H, DK]), ph.sb("s_oss", [RS, 12]), ph.sb("s_og", [RS, H, DK])
        score, new, aps, ops = (ph.ps("s_" + n, [P, 512]) for n in ("score", "new", "aps", "ops"))
        tps = [ph.ps(f"s_t{n}", [P, 512]) for n in range(2)]
        back = ph.ps("s_back", [P, 512])
        consts_in, pages_in, zeroed, qset, turned, copied, scored, stat, expd, weighted = (
            ph.sem(n) for n in ("consts_in", "pages_in", "zeroed", "qset", "turned", "copied", "scored", "stat", "expd", "weighted"))
        folded, a_copied, gathered, o_copied, returned, squared, mean, rstd, gated, stored, chained = (
            ph.sem(n) for n in ("folded", "a_copied", "gathered", "o_copied", "returned", "squared", "mean", "rstd", "gated", "stored", "chained"))
        k_in = [ph.sem(f"k_in{n}") for n in range(NPG)]
        v_in = [ph.sem(f"v_in{n}") for n in range(PER)]
        with nc.Block() as block:

            @block.sync
            def _(sp):
                sp.dma_start(pg[:], a["pages"]).then_inc(pages_in, 16)
                for dst, src in ((ident, "ident"), (fold, "fold"), (map2, "map2"), (mask, "new_mask")):
                    sp.dma_start(dst[:], a[src]).then_inc(consts_in, 16)
                sp.wait_ge(pages_in, 16)
                for b in range(NB):
                    for n in range(NPG):
                        u = b * NPG + n
                        page = sp.value_load(pg[0:1, u:u + 1], min_val=0, max_val=a["cache_k"].shape[0] // PAGE - 1)
                        rows = bass.ds(page * PAGE, PAGE)
                        if b:
                            sp.wait_ge(turned, u - NPG + 1)
                        sp.dma_start(kp[:, n, :], a["cache_k"][rows, :]).then_inc(k_in[n], 16)
                        if b >= PER and n == 0:
                            sp.wait_ge(gathered, 1)
                        sp.dma_start(vp[:, b % PER, n, :], a["cache_v"][rows, :]).then_inc(v_in[b % PER], 16)
                sp.wait_ge(gated, 1)
                sp.dma_start(merged[SEQ:ROWS, 512:1024], og[:].rearrange("p h d -> p (h d)")).then_inc(stored, 16)
                sp.wait_ge(stored, 16)

            @block.gpsimd
            def _(pool):
                nc.gpsimd.memset(pw[:], -0.5).then_inc(zeroed, 1)
                nc.gpsimd.memset(qs[:], 0.0).then_inc(zeroed, 1)
                pool.wait_ge(zeroed, 2)
                for g in range(GR):
                    if g:
                        pool.wait_ge(scored, 1)
                    for m in range(2):
                        if m or g:
                            pool.wait_ge(qset, 2 * g + m)
                        for b in range(PER):
                            for h in range(H):
                                col, tok = b * 32 + h * 8 + m * 4, SEQ + (g * PER + b) * DS
                                ins = nc.gpsimd.tensor_copy(qs[m * DQ:(m + 1) * DQ, b * H + h, col:col + DS],
                                                            qT[m * DQ:(m + 1) * DQ, h, tok:tok + DS])
                        ins.then_inc(qset, 1)
                pool.wait_ge(qset, 2 * GR)
                pool.wait_ge(mean, 1)
                nc.gpsimd.tensor_tensor(oss[:, 8:12], oss[:, 4:8], pw[:RS], ALU.pow).then_inc(rstd, 1)

            @block.scalar
            def _(act):
                for g in range(GR):
                    for b in range(PER):
                        for n in range(NPG):
                            u = (g * PER + b) * NPG + n
                            act.wait_ge(turned, u + 1)
                            nc.scalar.activation(kTp[:, b % 2, :, n * PAGE:(n + 1) * PAGE],
                                                 tps[u % 2][:].rearrange("p (h r) -> p h r", h=H), ACT.Copy).then_inc(copied, 1)
                    act.wait_ge(stat, g + 1)
                    nc.scalar.activation(p[:, :PAST], score[:], ACT.Exp, bias=mx[:, 3:4], accum_out=st[:, 0:1])
                    nc.scalar.activation(p[:, PAST:], new[:, :RS], ACT.Exp, bias=mx[:, 3:4], accum_out=st[:, 1:2]).then_inc(expd, 1)
                act.wait_ge(returned, 1)
                nc.scalar.activation(osq[:], back[:RS].rearrange("p (h d) -> p h d", h=H), ACT.Square).then_inc(squared, 1)

            @block.vector
            def _(dve):
                chain = Chain(dve, chained)
                dve.wait_ge(consts_in, 64)
                chain.link(nc.vector.scalar_tensor_tensor(st[:, 4:5], map2[:, 1:2], nlam[:], map2[:, 0:1], ALU.mult, ALU.add))
                for g in range(GR):
                    dve.wait_ge(scored, g + 1)
                    chain.link(nc.vector.tensor_tensor(new[:, :RS], new[:, :RS], mask[:, g, :], ALU.add))
                    nc.vector.tensor_reduce(mx[:, 0:1], score[:], AX.X, ALU.max)
                    chain.link(nc.vector.tensor_reduce(mx[:, 1:2], new[:, :RS], AX.X, ALU.max))
                    nc.vector.tensor_reduce(mx[:, 3:4], mx[:, 0:2], AX.X, ALU.max, negate=True).then_inc(stat, 1)
                    dve.wait_ge(expd, g + 1)
                    chain.link(nc.vector.tensor_tensor(st[:, 2:3], st[:, 0:1], st[:, 1:2], ALU.add))
                    chain.link(nc.vector.reciprocal(st[:, 3:4], st[:, 2:3]))
                    nc.vector.tensor_scalar(p[:], p[:], st[:, 3:4], st[:, 4:5], ALU.mult, ALU.mult).then_inc(weighted, 1)
                    dve.wait_ge(folded, g + 1)
                    nc.vector.tensor_copy(aT[:, 0:NPG, :], aps[:, 0:NPG * 64].rearrange("p (n r) -> p n r", n=NPG))
                    nc.vector.tensor_copy(aT[:RS, NPG, :], aps[:RS, NPG * 64:(NPG + 1) * 64]).then_inc(a_copied, 1)
                    dve.wait_ge(gathered, g + 1)
                    nc.vector.tensor_copy(oT[:, :, g * PER:(g + 1) * PER, :],
                                          ops[:, 0:64].rearrange("p (b h q) -> p h b q", b=PER, h=H)).then_inc(o_copied, 1)
                dve.wait_ge(squared, 1)
                chain.link(nc.vector.tensor_reduce(oss[:, 0:4], osq[:], AX.X, ALU.add))
                nc.vector.tensor_scalar(oss[:, 4:8], oss[:, 0:4], 1.0 / DK, EPS, ALU.mult, ALU.add).then_inc(mean, 1)
                dve.wait_ge(rstd, 1)
                chain.link(nc.vector.tensor_tensor(og[:], back[:RS].rearrange("p (h d) -> p h d", h=H), spread(oss[:, 8:12], DK), ALU.mult))
                nc.vector.tensor_tensor(og[:], og[:], G[:RS, NT, :].rearrange("p (h d) -> p h d", h=H), ALU.mult).then_inc(gated, 1)

            @block.tensor
            def _(pe):
                pe.wait_ge(consts_in, 64)
                mm = nc.tensor.matmul

                def keys(b):
                    for n in range(NPG):
                        u = b * NPG + n
                        pe.wait_ge(k_in[n], 16 * (b + 1))
                        if u >= 2:
                            pe.wait_ge(copied, u - 1)
                        for h in range(H):
                            ins = nc.tensor.transpose(tps[u % 2][:, h * P:(h + 1) * P], kp[:, n, h * P:(h + 1) * P], ident[:])
                        ins.then_inc(turned, 1)

                for g in range(GR):
                    pe.wait_ge(qset, 2 * (g + 1))
                    if g:
                        pe.wait_ge(expd, g)
                    for b in range(PER):
                        keys(g * PER + b)
                        pe.wait_ge(copied, (g * PER + b + 1) * NPG)
                        for h in range(H):
                            edge = dict(start=(b == 0 and h == 0), stop=(b == PER - 1 and h == H - 1))
                            mm(score[:], qs[:, b * H + h, :], kTp[:, b % 2, h, :], **edge)
                            ins = mm(new[:, :RS], qs[:, b * H + h, :], kT[:, h, SEQ:ROWS], **edge)
                    ins.then_inc(scored, 1)
                    pe.wait_ge(weighted, g + 1)
                    if g:
                        pe.wait_ge(a_copied, g)
                    for n in range(NPG + 1):
                        w = PAGE if n < NPG else RS
                        ins = mm(aps[:w, n * 64:(n + 1) * 64], p[:, n * PAGE:n * PAGE + w], fold[:], start=True, stop=True)
                    ins.then_inc(folded, 1)
                    pe.wait_ge(a_copied, g + 1)
                    if g:
                        pe.wait_ge(o_copied, g)
                    for b in range(PER):
                        pe.wait_ge(v_in[b], 16 * NPG * (g + 1))
                        for h in range(H):
                            c0 = (b * H + h) * DS
                            for n in range(NPG):
                                mm(ops[:, c0:c0 + DS], vp[:, b, n, h * DK:(h + 1) * DK], aT[:, n, c0:c0 + DS], start=(n == 0), stop=False)
                            ins = mm(ops[:, c0:c0 + DS], V[:RS, NT, h * DK:(h + 1) * DK], aT[:RS, NPG, c0:c0 + DS], start=False, stop=True)
                    ins.then_inc(gathered, 1)
                pe.wait_ge(o_copied, GR)
                for h in range(H):
                    ins = nc.tensor.transpose(back[:RS, h * DK:(h + 1) * DK], oT[:, h].rearrange("p b q -> p (b q)"), ident[:])
                ins.then_inc(returned, 1)


def mlstm(nc, a, proj, gates, merged, c_out_p, c_out_s, m_out_p, m_out_s):
    W = DV + 1
    with Phase(nc, "mls") as ph:
        sb, ps = ph.sb, ph.ps
        ident, ones, upper = sb("m_id", [P, P]), sb("m_ones", [P, P]), sb("m_up", [P, P])
        last, causal = sb("m_last", [P, P]), sb("m_causal", [P, P])
        upper_s, last_s, causal_s = sb("m_ups", [RS, RS]), sb("m_lasts", [RS, RS]), sb("m_causals", [RS, RS])
        member, own = sb("m_mem", [RS, NB]), sb("m_own", [P, NB, RS])
        nw, pw = sb("m_nw", [P, DV]), sb("m_pw", [P, 4])
        x = sb("m_x", [P, 2, 3072])
        va = sb("m_va", [P, 2, H, W])
        gt, sm, c = sb("m_gt", [P, 8]), sb("m_sm", [P, 4]), sb("m_c", [P, 4])
        M, args, exps = sb("m_M", [P, 4]), sb("m_args", [P, 3, 4]), sb("m_exps", [P, 3, 4])
        mrows, mprev, mprev_s = sb("m_mrows", [P, 4]), sb("m_mprev", [P, 4]), sb("m_mprevs", [RS, 4])
        dgc, dgM, dgs = (sb("m_" + n, [P, H, P]) for n in ("dgc", "dgM", "dgs"))
        cm, wt, pt = (sb("m_" + n, [P, H, P]) for n in ("cm", "wt", "pt"))
        qk, qg, kw = sb("m_qk", [P, 8, P]), sb("m_qg", [P, H, P]), sb("m_kw", [P, H, DK])
        dec = sb("m_dec", [P, H, NB])
        dn, rd = sb("m_dn", [P, 4]), sb("m_rd", [P, 4])
        to, tz, ho, og = (sb("m_" + n, [P, H, DV]) for n in ("to", "tz", "ho", "og"))
        junk, ss, rr = sb("m_junk", [P, H, DV]), sb("m_ss", [P, 8]), sb("m_rr", [P, 4])
        C, Cs = sb("m_C", [P, H, 1, W]), sb("m_Cs", [P, H, NB, W])
        qgs, kws = sb("m_qgs", [P, H, NB, RS]), sb("m_kws", [RS, NB, H, DK])
        bank = [ps(f"m_b{n}", [P, 512]) for n in range(8)]
        NUM, UPD = (1, 2, 5, 6), (0, 3, 4, 7)

        consts_in, set_up, stored, chained, chained_p, freed, batch_dC, batch_C = (
            ph.sem(n) for n in ("consts_in", "set_up", "stored", "chained", "chained_p", "freed", "batch_dC", "batch_C"))
        mcopied = ph.sem("mcopied")
        x_in = [ph.sem("x_in0"), ph.sem("x_in1")]
        ev = Events(ph, "gate small c dgc crow M sc dgM dgs mrow scrow wta wt qkt qkc kq qg pt kw num dC C "
                        "tz to so zs ho sq ms rr og")
        NC = 14

        def kinds(tile):
            def run(eng):
                pairs(eng, NT, lambda v, s, i: tile(v, s, i, P, 1, upper, last, causal, C, mprev))
                tile(NT, 0, NT // 2, RS, NB, upper_s, last_s, causal_s, Cs, mprev_s)
            return run

        def v3(b, r, w, rows=None):
            return bank[b][:(rows or P), :H * w].rearrange("p (h r) -> p h r", h=H)

        with nc.Block() as block:

            @block.sync
            def _(sp):
                loads = [(ident[:], a["ident"]), (ones[:], a["same"]), (upper[:], a["upper"]), (last[:], a["last"]),
                         (causal[:], a["causal"]), (upper_s[:], a["upper_s"]), (last_s[:], a["last_s"]),
                         (causal_s[:], a["causal_s"]), (member[:], a["member"]), (own[:], a["own"].partition_broadcast(P)),
                         (nw[:], a["mlstm_norm"].partition_broadcast(P)), (Cs[:], a["c_state"]), (mprev_s[:], a["m_state"])]
                assert len(loads) == NC - 1
                for dst, src in loads:
                    sp.dma_start(dst, src).then_inc(consts_in, 16)
                sp.sem_inc(stored, 16)
                sp.sem_inc(freed, 2)

                def load(v, s, i, r):
                    ph.hold(sp, freed, v + 1)
                    rows = bass.ds(v * P, r)
                    sp.dma_start(x[:r, s, 0:1024], proj[rows, 0:1024]).then_inc(x_in[s], 16)
                    sp.dma_start(x[:r, s, 1024:3072], proj[rows, 2048:4096]).then_inc(x_in[s], 16)
                    sp.dma_start(va[:r, s, :, 0:DV], proj[rows, 1024:2048].rearrange("p (h d) -> p h d", h=H)).then_inc(x_in[s], 16)

                def put(v, r):
                    ev.done(sp, "og", v)
                    sp.dma_start(merged[bass.ds(v * P, r), :], og[:r].rearrange("p h d -> p (h d)")).then_inc(stored, 16)

                with sp.Fori(0, NT // 2) as i:
                    for s in range(2):
                        load(i * 2 + s, s, i, P)
                    for s in range(2):
                        put(i * 2 + s, P)
                load(NT, 0, NT // 2, RS)
                put(NT, RS)
                ev.done(sp, "C", NT - 1)
                sp.dma_start(c_out_p, C[:, :, 0, :]).then_inc(stored, 16)
                sp.dma_start(m_out_p, mprev[0:1, :]).then_inc(stored, 16)
                ev.done(sp, "M", NT)
                sp.dma_start(m_out_s, mrows[:RS, :]).then_inc(stored, 16)
                sp.wait_ge(batch_C, NB)
                sp.dma_start(c_out_s, Cs[:]).then_inc(stored, 16)
                sp.wait_ge(stored, 16 * (NT + 6))

            @block.gpsimd
            def _(pool):
                ev.open(pool, "kw so zs rr")
                nc.gpsimd.memset(pw[:], -0.5).then_inc(set_up, 1)
                nc.gpsimd.memset(C[:], 0.0).then_inc(set_up, 1)
                nc.gpsimd.memset(mprev[:], 0.0).then_inc(set_up, 1)
                nc.gpsimd.memset(va[:, :, :, DV:W], 1.0).then_inc(set_up, 1)
                pool.wait_ge(set_up, 4)
                pool.wait_ge(consts_in, 16 * (NC - 1))
                chain = Chain(pool, chained_p)

                def tile(v, s, i, r, n, up, la, ca, Ct, mp):
                    chain.turn(v * 2)
                    xz = x[:r, s, 1024:2048].rearrange("p (h d) -> p h d", h=H)
                    ev.done(pool, "to", v)
                    ev.prev(pool, "ho", v)
                    nc.gpsimd.tensor_scalar(to[:r], to[:r], 1.0, 0.5, ALU.add, ALU.mult).then_inc(ev["so"], 1)
                    ev.done(pool, "wt", v)
                    ev.prev(pool, "dC", v)
                    nc.gpsimd.tensor_tensor(kw[:r], x[:r, s, 512:1024].rearrange("p (h d) -> p h d", h=H),
                                            spread(exps[:r, 2, :], DK), ALU.mult).then_inc(ev["kw"], 1)
                    ev.done(pool, "tz", v)
                    chain.link(nc.gpsimd.tensor_scalar(tz[:r], tz[:r], 1.0, 0.5, ALU.add, ALU.mult))
                    chain.link(nc.gpsimd.tensor_tensor(tz[:r], tz[:r], xz, ALU.mult))
                    nc.gpsimd.tensor_tensor(tz[:r], tz[:r], repeat(nw[:r], H), ALU.mult).then_inc(ev["zs"], 1)
                    ev.done(pool, "ms", v)
                    nc.gpsimd.tensor_tensor(rr[:r], ss[:r, 4:8], pw[:r], ALU.pow).then_inc(ev["rr"], 1)
                    assert chain.n == 2

                kinds(tile)(pool)

            @block.scalar
            def _(act):
                ev.open(act, "qkc sc wt to tz sq")

                def tile(v, s, i, r, n, up, la, ca, Ct, mp):
                    ev.done(act, "qkt", v)
                    ev.prev(act, "qg", v)
                    ev.prev(act, "kq", v)
                    nc.scalar.activation(qk[:, 0:4, :r], v3(5, r, r), ACT.Copy, scale=DK ** -0.5)
                    nc.scalar.activation(qk[:, 4:8, :r], v3(6, r, r), ACT.Copy).then_inc(ev["qkc"], 1)
                    ev.done(act, "M", v)
                    nc.scalar.activation(exps[:r, 0:2, :], args[:r, 0:2, :], ACT.Exp).then_inc(ev["sc"], 1)
                    ev.done(act, "wta", v)
                    ev.prev(act, "kw", v)
                    nc.scalar.activation(exps[:r, 2, :], args[:r, 2, :], ACT.Exp)
                    nc.scalar.activation(wt[:r, :, :r], wt[:r, :, :r], ACT.Exp, scale=-1.0).then_inc(ev["wt"], 1)
                    act.wait_ge(x_in[s], i * 48 + 48)
                    ev.prev(act, "ho", v)
                    nc.scalar.activation(to[:r], x[:r, s, 2048:3072].rearrange("p (h d) -> p h d", h=H), ACT.Tanh, scale=0.5).then_inc(ev["to"], 1)
                    ev.prev(act, "og", v)
                    nc.scalar.activation(tz[:r], x[:r, s, 1024:2048].rearrange("p (h d) -> p h d", h=H), ACT.Tanh, scale=0.5).then_inc(ev["tz"], 1)
                    ev.done(act, "ho", v)
                    ev.prev(act, "ms", v)
                    for h in range(H):
                        ins = nc.scalar.activation(junk[:r, h, :], ho[:r, h, :], ACT.Square, accum_out=ss[:r, h:h + 1])
                    ins.then_inc(ev["sq"], 1)

                kinds(tile)(act)

            @block.vector
            def _(dve):
                ev.open(dve, "gate c dgc M dgM dgs wta qg pt C ho ms og")
                dve.wait_ge(consts_in, 16 * (NC - 1))
                dve.wait_ge(set_up, 4)
                chain = Chain(dve, chained)
                PER = 9

                def tile(v, s, i, r, n, up, la, ca, Ct, mp):
                    chain.turn(v * PER)
                    nc.vector.tensor_copy(gt[:r], gates[:r, bass.ds(v, 1), :].rearrange("p o h -> p (o h)")).then_inc(ev["gate"], 1)
                    ev.done(dve, "small", v)
                    nc.vector.tensor_copy(sm[:r], bank[0][:r, 0:4])
                    nc.vector.tensor_tensor(c[:r], gt[:r, 4:8], bank[0][:r, 0:4], ALU.subtract).then_inc(ev["c"], 1)
                    ev.done(dve, "c", v)
                    nc.vector.tensor_tensor(dgc[:r, :, :r], spread(c[:r], r), repeat(ident[:r, :r], H), ALU.mult).then_inc(ev["dgc"], 1)
                    ev.done(dve, "crow", v)
                    chain.link(nc.vector.tensor_tensor(cm[:r, :, :r], v3(1, r, r, r), repeat(ca[:r, :r], H), ALU.add))
                    chain.link(nc.vector.tensor_reduce(M[:r], cm[:r, :, :r], AX.X, ALU.max))
                    chain.link(nc.vector.tensor_tensor(M[:r], M[:r], mp[:r], ALU.max))
                    chain.link(nc.vector.tensor_tensor(mrows[:r], sm[:r], M[:r], ALU.add))
                    nc.vector.tensor_tensor(args[:r, 0, :], mp[:r], M[:r], ALU.subtract)
                    nc.vector.tensor_scalar(args[:r, 1, :], mrows[:r], -1.0, None, ALU.mult).then_inc(ev["M"], 1)
                    nc.vector.tensor_tensor(dgM[:r, :, :r], spread(M[:r], r), repeat(ident[:r, :r], H), ALU.mult).then_inc(ev["dgM"], 1)
                    ev.done(dve, "sc", v)
                    nc.vector.tensor_tensor(dgs[:r, :, :r], spread(exps[:r, 0, :], r), repeat(ident[:r, :r], H), ALU.mult).then_inc(ev["dgs"], 1)
                    ev.done(dve, "mrow", v)
                    nc.vector.tensor_tensor(args[:r, 2, :], c[:r], bank[0][:r, 8:12], ALU.subtract)
                    for h in range(H):
                        ins = nc.vector.tensor_scalar(wt[:r, h, :r], bank[2][:r, h * r:(h + 1) * r], c[:r, h:h + 1], 0.0,
                                                      ALU.subtract, ALU.max)
                    ins.then_inc(ev["wta"], 1)
                    if n == 1:
                        nc.vector.tensor_copy(mp[:], bank[0][:, 8:12]).then_inc(mcopied, 1)
                        dve.wait_ge(mcopied, v + 1)
                        nc.vector.tensor_tensor(mp[:], mp[:], bank[0][:, 4:8], ALU.add)
                    ev.done(dve, "scrow", v)
                    ev.done(dve, "qkc", v)
                    ev.prev(dve, "num", v)
                    per = r // n
                    nc.vector.tensor_copy(dec[:, :, :n], bank[3][:, :H * r].rearrange("p (h b t) -> p h b t", h=H, b=n)[:, :, :, per - 1])
                    nc.vector.tensor_tensor(qg[:, :, :r], qk[:, 0:4, :r], v3(3, r, r), ALU.mult).then_inc(ev["qg"], 1)
                    if n > 1:
                        ev.done(dve, "qg", v)
                        for h in range(H):
                            ins = nc.vector.tensor_tensor(qgs[:, h], repeat(qg[:, h, :r], NB), own[:], ALU.mult)
                        ev.done(dve, "kw", v)
                        for b in range(NB):
                            ins = nc.vector.tensor_scalar(kws[:, b], kw[:r], member[:, b:b + 1], None, ALU.mult)
                    ev.done(dve, "wt", v)
                    chain.link(nc.vector.tensor_tensor(wt[:r, :, :r], wt[:r, :, :r], repeat(up[:r, :r], H), ALU.mult))
                    ev.done(dve, "kq", v)
                    nc.vector.tensor_tensor(pt[:r, :, :r], v3(4, r, r, r), wt[:r, :, :r], ALU.mult).then_inc(ev["pt"], 1)
                    ev.done(dve, "num", v)
                    for h in range(H):
                        ins = nc.vector.tensor_copy(dn[:r, h:h + 1], bank[NUM[h]][:r, DV:W])
                    chain.link(ins)
                    chain.link(nc.vector.scalar_tensor_tensor(dn[:r], dn[:r], -1.0, dn[:r], ALU.mult, ALU.max))
                    chain.link(nc.vector.tensor_tensor(dn[:r], dn[:r], exps[:r, 1, :], ALU.max))
                    chain.link(nc.vector.reciprocal(rd[:r], dn[:r]))
                    ev.done(dve, "so", v)
                    ev.prev(dve, "sq", v)
                    for h in range(H):
                        ins = nc.vector.scalar_tensor_tensor(ho[:r, h, :], bank[NUM[h]][:r, 0:DV], rd[:r, h:h + 1], to[:r, h, :],
                                                             ALU.mult, ALU.mult)
                    ins.then_inc(ev["ho"], 1)
                    if n == 1:
                        ev.done(dve, "dC", v)
                        for h in range(H):
                            ins = nc.vector.scalar_tensor_tensor(C[:, h, 0, :], C[:, h, 0, :], dec[:, h, 0:1],
                                                                 bank[UPD[h]][:, :W], ALU.mult, ALU.add)
                        ins.then_inc(ev["C"], 1)
                    else:
                        for b in range(NB):
                            dve.wait_ge(batch_dC, b + 1)
                            for h in range(H):
                                ins = nc.vector.scalar_tensor_tensor(Cs[:, h, b, :], Cs[:, h, b, :], dec[:, h, b:b + 1],
                                                                     bank[UPD[h]][:, :W], ALU.mult, ALU.add)
                            ins.then_inc(batch_C, 1)
                    ev.done(dve, "sq", v)
                    nc.vector.tensor_scalar(ss[:r, 4:8], ss[:r, 0:4], 1.0 / DV, EPS, ALU.mult, ALU.add).then_inc(ev["ms"], 1)
                    ev.done(dve, "rr", v)
                    ev.done(dve, "zs", v)
                    dve.wait_ge(stored, v * 16 + 16)
                    for h in range(H):
                        ins = nc.vector.scalar_tensor_tensor(og[:r, h, :], ho[:r, h, :], rr[:r, h:h + 1], tz[:r, h, :],
                                                             ALU.mult, ALU.mult)
                    ins.then_inc(ev["og"], 1)
                    ev.done(dve, "dC", v) if n == 1 else None
                    dve.sem_inc(freed, 1)
                    assert n > 1 or chain.n == PER

                kinds(tile)(dve)

            @block.tensor
            def _(pe):
                ev.open(pe, "small crow mrow scrow qkt kq num dC")
                pe.wait_ge(consts_in, 16 * (NC - 1))
                pe.wait_ge(set_up, 4)
                mm = nc.tensor.matmul

                def tile(v, s, i, r, n, up, la, ca, Ct, mp):
                    ev.prev(pe, "C", v)
                    ev.prev(pe, "ho", v)
                    ev.done(pe, "gate", v)
                    mm(bank[0][:r, 0:4], up[:r, :r], gt[:r, 0:4], start=True, stop=True).then_inc(ev["small"], 1)
                    pe.wait_ge(x_in[s], i * 48 + 48)
                    for h in range(H):
                        nc.tensor.transpose(bank[5][:, h * r:(h + 1) * r], x[:r, s, h * P:(h + 1) * P], ident[:r, :r])
                        ins = nc.tensor.transpose(bank[6][:, h * r:(h + 1) * r], x[:r, s, 512 + h * P:512 + (h + 1) * P], ident[:r, :r])
                    ins.then_inc(ev["qkt"], 1)
                    ev.done(pe, "dgc", v)
                    mm(bank[1][:r, :H * r], ones[:r, :r], dgc[:r, :, :r], start=True, stop=True).then_inc(ev["crow"], 1)
                    ev.done(pe, "qkc", v)
                    for h in range(H):
                        ins = mm(bank[4][:r, h * r:(h + 1) * r], qk[:, 4 + h, :r], qk[:, h, :r], start=True, stop=True)
                    ins.then_inc(ev["kq"], 1)
                    ev.done(pe, "dgM", v)
                    mm(bank[0][:, 4:8], ones[:r, :], gt[:r, 0:4], start=True, stop=True)
                    mm(bank[0][:r, 8:12], la[:r, :r], M[:r], start=True, stop=True)
                    mm(bank[2][:r, :H * r], ones[:r, :r], dgM[:r, :, :r], start=True, stop=True).then_inc(ev["mrow"], 1)
                    ev.done(pe, "dgs", v)
                    mm(bank[3][:, :H * r], ones[:r, :], dgs[:r, :, :r], start=True, stop=True).then_inc(ev["scrow"], 1)
                    ev.done(pe, "pt", v)
                    ev.done(pe, "wta", v)
                    for h in range(H):
                        for b in range(n):
                            mm(bank[NUM[h]][:r, :W], qg[:, h, :r] if n == 1 else qgs[:, h, b], Ct[:, h, b, :], start=(b == 0), stop=False)
                        ins = mm(bank[NUM[h]][:r, :W], pt[:r, h, :r], va[:r, s, h, :], start=False, stop=True)
                    ins.then_inc(ev["num"], 1)
                    ev.done(pe, "kw", v)
                    if n == 1:
                        for h in range(H):
                            ins = mm(bank[UPD[h]][:, :W], kw[:r, h, :], va[:r, s, h, :], start=True, stop=True)
                        ins.then_inc(ev["dC"], 1)
                    else:
                        for b in range(NB):
                            if b:
                                pe.wait_ge(batch_C, b)
                            for h in range(H):
                                ins = mm(bank[UPD[h]][:, :W], kws[:, b, h, :], va[:r, s, h, :], start=True, stop=True)
                            ins.then_inc(batch_dC, 1)

                kinds(tile)(pe)


def final_norm(nc, x, norm_d, y):
    with Phase(nc, "fin") as ph:
        xt, out = ph.sb("f_x", [P, 2, D]), ph.sb("f_y", [P, 2, D])
        junk, nw = ph.sb("f_junk", [P, 2, D]), ph.sb("f_nw", [P, D])
        ms, pw = ph.sb("f_ms", [P, 2, 3]), ph.sb("f_pw", [P, 1])
        nw_in, set_up = ph.sem("nw_in"), ph.sem("set_up")
        x_in, stored = [ph.sem("x_in0"), ph.sem("x_in1")], [ph.sem("stored0"), ph.sem("stored1")]
        squares, mean, rstd, normed = (ph.sem(n) for n in ("squares", "mean", "rstd", "normed"))
        with nc.Block() as block:

            @block.sync
            def _(sp):
                sp.dma_start(nw[:], norm_d.partition_broadcast(P)).then_inc(nw_in, 16)

                def load(v, s, i, r):
                    ph.hold(sp, normed, v + 1)
                    sp.dma_start(xt[:r, s, :], x[bass.ds(v * P, r), :]).then_inc(x_in[s], 16)

                def put(v, s, i, r):
                    ph.hold(sp, normed, v + 3)
                    sp.dma_start(y[bass.ds(v * P, r), :], out[:r, s, :]).then_inc(stored[s], 16)

                with sp.Fori(0, NT // 2) as i:
                    for s in range(2):
                        load(i * 2 + s, s, i, P)
                    for s in range(2):
                        put(i * 2 + s, s, i, P)
                load(NT, 0, NT // 2, RS)
                put(NT, 0, NT // 2, RS)
                sp.wait_ge(stored[0], 16 * (2 + NT // 2))
                sp.wait_ge(stored[1], 16 * (1 + NT // 2))

            @block.scalar
            def _(act):
                for s in range(2):
                    act.sem_inc(stored[s], 16)

                def tile(v, s, i, r=P):
                    act.wait_ge(x_in[s], i * 16 + 16)
                    act.wait_ge(normed, v + 1)
                    nc.scalar.activation(junk[:r, s, :], xt[:r, s, :], ACT.Square, accum_out=ms[:r, s, 0:1]).then_inc(squares, 1)

                pairs(act, NT, tile)
                tile(NT, 0, NT // 2, RS)

            @block.gpsimd
            def _(pool):
                nc.gpsimd.memset(pw[:], -0.5).then_inc(set_up, 1)
                pool.wait_ge(set_up, 1)

                def tile(v, s, i, r=P):
                    ph.hold(pool, mean, v + 1)
                    nc.gpsimd.tensor_tensor(ms[:r, s, 2:3], ms[:r, s, 1:2], pw[:r], ALU.pow).then_inc(rstd, 1)

                pairs(pool, NT, tile)
                tile(NT, 0, NT // 2, RS)

            @block.vector
            def _(dve):
                dve.sem_inc(normed, 2)
                dve.wait_ge(nw_in, 16)

                def tile(v, s, i, r=P):
                    dve.wait_ge(squares, v + 1)
                    nc.vector.tensor_scalar(ms[:r, s, 1:2], ms[:r, s, 0:1], 1.0 / D, EPS, ALU.mult, ALU.add).then_inc(mean, 1)
                    dve.wait_ge(rstd, v + 1)
                    dve.wait_ge(stored[s], i * 16 + 16)
                    nc.vector.scalar_tensor_tensor(out[:r, s, :], xt[:r, s, :], ms[:r, s, 2:3], nw[:r], ALU.mult, ALU.mult).then_inc(normed, 1)

                pairs(dve, NT, tile)
                tile(NT, 0, NT // 2, RS)
def build(nc, a, o):
    def scratch(name, shape):
        return nc.dram_tensor(name, shape, F32, kind="Internal").ap()

    proj = scratch("proj", [ROWS, 5 * 512])
    conv_t, conv_s = scratch("conv_t", [CT * P, SEQ]), scratch("conv_s", [CT * P, RS])
    merged = scratch("merged", [ROWS, D])
    x1 = scratch("x1", [ROWS, D])
    proj2 = scratch("proj2", [ROWS, 4096])
    merged2 = scratch("merged2", [ROWS, D])
    x2 = scratch("x2", [ROWS, D])
    with ExitStack() as top:
        gates = top.enter_context(nc.sbuf_tensor("gates", [P, NT + 1, 8], F32))

        def resident(tag):
            st = ExitStack()
            hi = st.enter_context(nc.sbuf_tensor(tag + "act_hi", [P, KT, ROWS], F32R))
            lo = st.enter_context(nc.sbuf_tensor(tag + "act_lo", [P, KT, ROWS], F32R))
            return st, hi, lo

        st, hi, lo = resident("a1")
        with st:
            load_activations(nc, "a1", a["x"], hi, lo, a["ident"], a["norm_w"][0])
            project_conv(nc, hi, lo, a["w_conv"], a["conv_w"], a["conv_state"], conv_t, conv_s,
                         o["conv_p"], o["conv_s"])
            project_gates(nc, "e", hi, lo, a["w_gate_e"], a["gate_vec_e"], a["fold16"], gates, "gdn")
            project_rows(nc, "p1", hi, lo, a["w_rows_e"], proj, 5 * 512 // WB)
        gated_delta(nc, a, proj, conv_t, conv_s, gates, merged, o["gdn_p"], o["gdn_s"])
        with ExitStack() as st:
            def kept(name, shape):
                return st.enter_context(nc.sbuf_tensor(name, shape, F32))

            qT, kT = kept("qT", [P, H, ROWS]), kept("kT", [P, H, ROWS])
            V, G, nlam = kept("V", [P, NT + 1, 512]), kept("G", [P, NT + 1, 512]), kept("nlam", [P, 1])
            attention_inputs(nc, a, proj, o["k_rows"], o["v_rows"], qT, kT, V, G, nlam)
            prompt_attention(nc, a, merged, qT, kT, V, G, nlam)
            sample_attention(nc, a, merged, qT, kT, V, G, nlam)
        st, hi, lo = resident("a2")
        with st:
            load_activations(nc, "a2", merged, hi, lo, a["ident"])
            project_rows(nc, "p2", hi, lo, a["w_out_e"], x1, D // WB, residual=a["x"])

        st, hi, lo = resident("a3")
        with st:
            load_activations(nc, "a3", x1, hi, lo, a["ident"], a["norm_w"][1])
            project_gates(nc, "o", hi, lo, a["w_gate_o"], a["gate_vec_o"], a["fold16"], gates, "mlstm")
            project_rows(nc, "p3", hi, lo, a["w_rows_o"], proj2, 4096 // WB)
        mlstm(nc, a, proj2, gates, merged2, o["c_p"], o["c_s"], o["m_p"], o["m_s"])
        st, hi, lo = resident("a4")
        with st:
            load_activations(nc, "a4", merged2, hi, lo, a["ident"])
            project_rows(nc, "p4", hi, lo, a["w_out_o"], x2, D // WB, residual=x1)
        final_norm(nc, x2, a["final_w"], o["y"])


OUTS = {
    "y": (ROWS, D), "k_rows": (ROWS, 512), "v_rows": (ROWS, 512),
    "conv_p": (CT, P, CONV - 1), "conv_s": (CT, P, NB, CONV - 1),
    "gdn_p": (P, H, P), "gdn_s": (P, H, NB, P),
    "c_p": (P, H, DV + 1), "c_s": (P, H, NB, DV + 1), "m_p": (1, H), "m_s": (RS, H),
}


def constants():
    c = {"ident": np.eye(P, dtype=np.float32)}
    i, j = np.arange(P)[None, :], np.arange(P)[:, None]

    def masks(r, per, levels):
        i, j = np.arange(r)[None, :], np.arange(r)[:, None]
        same = i // per == j // per
        upper = ((j <= i) & same).astype(np.float32)
        level = [((i >> l) ^ 1 == j >> l) & (i > j) for l in range(levels)]
        last = (j == i // per * per + per - 1).astype(np.float32)
        return upper, np.stack(level, 1).astype(np.float32), same.astype(np.float32), last

    c["upper"], c["levels"], c["same"], c["last"] = masks(P, P, LEVELS)
    c["upper_s"], c["levels_s"], c["same_s"], c["last_s"] = masks(RS, DS, LEVELS_S)
    c["causal"] = np.where(j >= i, 0.0, NEG).astype(np.float32)
    c["causal_s"] = np.where(c["upper_s"].T > 0, 0.0, NEG).astype(np.float32)
    c["fold16"] = np.tile(np.eye(8, dtype=np.float32), (2, 1))
    member = np.zeros((RS, NB), np.float32)
    member[np.arange(RS), np.arange(RS) // DS] = 1
    c["own"] = np.repeat(member.T[None], 1, 0).reshape(NB, RS).copy()
    c["member"] = member
    row = np.arange(P)
    seq, hd, mp, q = row // 32, row // 8 % 4, row // 4 % 2, row % 4
    fold = np.zeros((P, 64), np.float32)
    fold[row, (seq * 4 + hd) * 4 + q] = 1
    c["fold"] = fold
    c["map2"] = np.stack([1.0 - mp, mp * 1.0], 1).astype(np.float32)
    new = np.arange(RS)
    ok = (new[None, :] // DS == seq[:, None]) & (new[None, :] % DS <= q[:, None])
    ok2 = (new[None, :] // DS == seq[:, None] + 4) & (new[None, :] % DS <= q[:, None])
    c["new_mask"] = np.stack([np.where(ok, 0, NEG), np.where(ok2, 0, NEG)], 1).astype(np.float32)
    inv = np.power(np.float32(500000.0), -np.arange(ROT, dtype=np.float32) / np.float32(ROT)).astype(np.float32)
    pos = np.concatenate([np.arange(SEQ), PAST + np.tile(np.arange(DS), NB)]).astype(np.float32)
    ang = (pos[:, None] * inv[None, :]).astype(np.float32)
    for name, f in (("cos", np.cos), ("sin", np.sin)):
        t = np.zeros(((NT + 1) * P, ROT), np.float32)
        t[:ROWS] = f(ang)
        c[name] = np.ascontiguousarray(t.reshape(NT + 1, P, ROT).transpose(1, 0, 2))
    return c


def laid_out(inputs):
    f = {k: np.asarray(v) for k, v in inputs.items()}
    blocks = lambda w, n: np.ascontiguousarray(
        w.reshape(KT, P, w.shape[1] // n, n).transpose(2, 1, 0, 3).reshape(-1, P, KT * n))
    we, wo = f["w_in_even"][0], f["w_in_odd"][0]
    a = {
        "x": np.concatenate([f["x_prompt"].reshape(SEQ, D), f["x_sample"].reshape(RS, D)]),
        "norm_w": f["norm_w"], "final_w": f["final_norm_w"],
        "w_conv": blocks(we[:, :1536], P),
        "w_rows_e": blocks(np.concatenate([we[:, 1536:2048], we[:, 2056:]], 1), WB),
        "w_gate_e": blocks(we[:, 2048:2056], 8)[0],
        "gate_vec_e": np.concatenate([f["a_log"][0], f["dt_bias"][0]]),
        "w_out_e": blocks(f["w_out_even"][0], WB),
        "w_rows_o": blocks(wo[:, :4096], WB), "w_gate_o": blocks(wo[:, 4096:], 8)[0],
        "gate_vec_o": np.concatenate([f["b_i"][0], f["b_f"][0]]),
        "w_out_o": blocks(f["w_out_odd"][0], WB),
        "conv_w": f["conv_w"][0].reshape(CONV, CT, P).transpose(2, 1, 0).reshape(P, CT * CONV),
        "conv_state": f["state_gdn_conv"][0].reshape(NB, CONV - 1, CT, P).transpose(2, 3, 0, 1),
        "gdn_state": f["state_gdn_s"][0].transpose(2, 1, 0, 3),
        "c_state": np.concatenate([f["state_mlstm_c"][0], f["state_mlstm_n"][0][..., None]], -1).transpose(2, 1, 0, 3),
        "m_state": np.repeat(f["state_mlstm_m"][0], DS, 0),
        "gdn_norm": f["gdn_norm_w"][0], "diff_norm": f["diff_norm_w"][0], "mlstm_norm": f["mlstm_norm_w"][0],
        "lambda_qk": f["lambda_qk"][0].reshape(-1),
        "pages": f["page_table"].reshape(1, -1),
        "cache_k": f["cache_k"][0].reshape(-1, 512), "cache_v": f["cache_v"][0].reshape(-1, 512),
    }
    return {k: np.ascontiguousarray(v) for k, v in a.items()}


def kernel(**inputs):
    import concourse.bacc as _bacc
    from concourse.bass_utils import run_bass_kernel_spmd as _run

    nc = _bacc.Bacc("TRN2", target_bir_lowering=False, num_devices=1)
    arrays, a, o = {}, {}, {}
    for name, x in {**laid_out(inputs), **constants()}.items():
        arrays[f"in_{name}"] = x
        a[name] = nc.dram_tensor(f"in_{name}", x.shape, mybir.dt.from_np(x.dtype), kind="ExternalInput").ap()
    for name, shape in OUTS.items():
        o[name] = nc.dram_tensor(f"out_{name}", shape, F32, kind="ExternalOutput").ap()
    build(nc, a, o)
    r = _run(nc, [arrays], core_ids=[0]).results[0]
    g = {name: r[f"out_{name}"] for name in OUTS}
    k, v = (g[n].reshape(ROWS, H, P) for n in ("k_rows", "v_rows"))
    cp = g["c_p"].transpose(1, 0, 2)
    cs = g["c_s"].transpose(2, 1, 0, 3)
    return (
        g["y"][:SEQ].reshape(1, SEQ, D), g["y"][SEQ:].reshape(NB, DS, D),
        k[:SEQ].reshape(1, 1, SEQ, H, P), v[:SEQ].reshape(1, 1, SEQ, H, P),
        k[SEQ:].reshape(1, NB, DS, H, P), v[SEQ:].reshape(1, NB, DS, H, P),
        g["conv_p"].transpose(2, 0, 1).reshape(1, 1, CONV - 1, CT * P),
        g["gdn_p"].transpose(1, 0, 2).reshape(1, 1, H, P, P),
        g["conv_s"].transpose(2, 3, 0, 1).reshape(1, NB, CONV - 1, CT * P),
        g["gdn_s"].transpose(2, 1, 0, 3).reshape(1, NB, H, P, P),
        cp[..., :DV].reshape(1, 1, H, P, DV), cp[..., DV].reshape(1, 1, H, P), g["m_p"].reshape(1, 1, H),
        cs[..., :DV].reshape(1, NB, H, P, DV), cs[..., DV].reshape(1, NB, H, P), g["m_s"][DS - 1::DS].reshape(1, NB, H),
    )
```

```python
from contextlib import ExitStack

import concourse.bass as bass
import numpy as np
from concourse import mybir

F32 = mybir.dt.float32
F32R = mybir.dt.float32r
I32 = mybir.dt.int32
ALU = mybir.AluOpType
ACT = mybir.ActivationFunctionType
AX = mybir.AxisListType

P = 128
D = 1024
KT = D // P
SEQ = 2048
NB = 8
DS = 4
RS = NB * DS
NT = SEQ // P
ROWS = SEQ + RS
H = 4
DK = 128
DV = 256
DQ = 64
ROT = 8
PAST = 512
PAGE = 128
NPG = PAST // PAGE
CONV = 4
CT = 12
WB = 256
EPS = 1e-6
NEG = -1e30
LEVELS = 7
LEVELS_S = 2


class Phase:

    def __init__(self, nc, tag):
        self.nc, self.tag, self.stack, self.sems = nc, tag, ExitStack(), []

    def __enter__(self):
        self.held = self.sem("held")
        return self

    def sb(self, name, shape, dt=F32):
        return self.stack.enter_context(self.nc.sbuf_tensor(name, shape, dt))

    def ps(self, name, shape, dt=F32):
        return self.stack.enter_context(self.nc.psum_tensor(name, shape, dt))

    def sem(self, name):
        s = self.nc.alloc_semaphore(f"{self.tag}_{name}")
        self.sems.append(s)
        return s

    def hold(self, eng, sem, value):
        eng.wait_ge(sem, value)
        if not isinstance(value, int):
            eng.sem_inc(self.held, 1)

    def __exit__(self, *e):
        if e[0] is None:
            self.nc.clear_and_free_semaphores(self.sems)
            self.nc.all_engine_barrier()
        return self.stack.__exit__(*e)


class Chain:

    def __init__(self, eng, sem):
        self.eng, self.sem, self.base, self.n = eng, sem, 0, 0

    def turn(self, base):
        self.base, self.n = base, 0

    def link(self, ins):
        self.n += 1
        ins.then_inc(self.sem, 1)
        self.eng.wait_ge(self.sem, self.base + self.n)


def pairs(eng, count, body):
    with eng.Fori(0, count // 2) as i:
        for s in range(2):
            body(i * 2 + s, s, i)


def turns_of(eng, count, slots, *parts):
    with eng.Fori(0, count // slots) as i:
        for part in parts:
            for s in range(slots):
                part(i * slots + s, s, i)


def loads_and_stores(eng, load, put):
    for v in range(4):
        load(v, v, 0, P)
    put(0, 0, 0, P)
    put(1, 1, 0, P)
    with eng.Fori(0, NT // 4 - 1) as i:
        for s in range(4):
            load(i * 4 + (4 + s), s, i + 1, P)
            put(i * 4 + (2 + s), (s + 2) % 4, i, P)
    load(NT, 0, NT // 4, RS)
    put(NT - 2, 2, NT // 4 - 1, P)
    put(NT - 1, 3, NT // 4 - 1, P)
    put(NT, 0, NT // 4, RS)


def load_activations(nc, tag, src, hi, lo, ident_d, norm_d=None):
    N = 4
    with Phase(nc, tag) as ph:
        x = ph.sb(tag + "x", [P, N, D])
        xn = ph.sb(tag + "xn", [P, 2, D])
        junk = ph.sb(tag + "junk", [P, 2, D])
        ms = ph.sb(tag + "ms", [P, N, 3])
        nw = ph.sb(tag + "nw", [P, D])
        ident = ph.sb(tag + "id", [P, P])
        half = ph.sb(tag + "half", [P, 1])
        tp = ph.ps(tag + "tp", [P, N, 2, 4 * P])
        consts_in, halved = ph.sem("consts_in"), ph.sem("halved")
        x_in = [ph.sem(f"x_in{s}") for s in range(N)]
        squares, mean, rstd, normed, transposed, hi_done, lo_done = (
            ph.sem(n) for n in ("squares", "mean", "rstd", "normed", "transposed", "hi_done", "lo_done"))

        def view(s, q, r):
            return tp[:, s, q, :].rearrange("p (k r) -> p k r", k=4)[:, :, :r]

        with nc.Block() as block:

            @block.sync
            def _(sp):
                sp.dma_start(ident[:], ident_d).then_inc(consts_in, 16)
                if norm_d is not None:
                    sp.dma_start(nw[:], norm_d.partition_broadcast(P)).then_inc(consts_in, 16)

                def load(v, s, i, r=P):
                    if norm_d is not None:
                        ph.hold(sp, normed, v + 1)
                    else:
                        ph.hold(sp, transposed, 2 * v + 2)
                    sp.dma_start(x[:r, s, :], src[bass.ds(v * P, r), :]).then_inc(x_in[s], 16)

                turns_of(sp, NT, N, load)
                load(NT, 0, NT // N, RS)

            @block.scalar
            def _(act):
                act.sem_inc(squares, 2)

                def square(v, s, i, r=P):
                    if norm_d is None:
                        return
                    act.wait_ge(x_in[s], i * 16 + 16)
                    act.wait_ge(normed, v + 1)
                    act.wait_ge(squares, v + 1)
                    nc.scalar.activation(junk[:r, s % 2], x[:r, s, :], ACT.Square,
                                         accum_out=ms[:r, s, 0:1]).then_inc(squares, 1)

                def high(v, s, i, r=P):
                    for q in range(2):
                        act.wait_ge(transposed, 2 * (v + N) + q + 1)
                        nc.scalar.activation(hi[:, 4 * q:4 * q + 4, bass.ds(v * P, r)], view(s, q, r), ACT.Copy).then_inc(hi_done, 1)

                turns_of(act, NT, N, square, high)
                square(NT, 0, NT // N, RS)
                high(NT, 0, NT // N, RS)

            @block.gpsimd
            def _(pool):
                if norm_d is None:
                    return
                nc.gpsimd.memset(half[:], -0.5).then_inc(halved, 1)
                pool.wait_ge(halved, 1)

                def root(v, s, i, r=P):
                    ph.hold(pool, mean, v + 1)
                    nc.gpsimd.tensor_tensor(ms[:r, s, 2:3], ms[:r, s, 1:2], half[:r], ALU.pow).then_inc(rstd, 1)

                turns_of(pool, NT, N, root)
                root(NT, 0, NT // N, RS)

            @block.vector
            def _(dve):
                dve.sem_inc(normed, N)
                dve.sem_inc(lo_done, 2 * N)
                dve.wait_ge(consts_in, 16 if norm_d is None else 32)

                def average(v, s, i, r=P):
                    if norm_d is None:
                        return
                    dve.wait_ge(squares, v + 3)
                    nc.vector.tensor_scalar(ms[:r, s, 1:2], ms[:r, s, 0:1], 1.0 / D, EPS,
                                            ALU.mult, ALU.add).then_inc(mean, 1)

                def norm(v, s, i, r=P):
                    if norm_d is None:
                        return
                    dve.wait_ge(rstd, v + 1)
                    dve.wait_ge(transposed, 2 * (v + N - 2) + 2)
                    nc.vector.scalar_tensor_tensor(xn[:r, s % 2, :], x[:r, s, :], ms[:r, s, 2:3], nw[:r],
                                                   ALU.mult, ALU.mult).then_inc(normed, 1)

                def low(v, s, i, r=P):
                    for q in range(2):
                        dve.wait_ge(hi_done, 2 * v + q + 1)
                        part = (slice(None), slice(4 * q, 4 * q + 4), bass.ds(v * P, r))
                        nc.vector.tensor_tensor(lo[part], view(s, q, r), hi[part].bitcast(F32), ALU.subtract).then_inc(lo_done, 1)

                turns_of(dve, NT, N, average, norm, low)
                for part in (average, norm, low):
                    part(NT, 0, NT // N, RS)

            @block.tensor
            def _(pe):
                pe.sem_inc(transposed, 2 * N)
                pe.wait_ge(consts_in, 16 if norm_d is None else 32)

                def transposes(v, s, i, r=P):
                    if norm_d is not None:
                        pe.wait_ge(normed, v + 1 + N)
                    else:
                        pe.wait_ge(x_in[s], i * 16 + 16)
                    rows = x[:r, s] if norm_d is None else xn[:r, s % 2]
                    for q in range(2):
                        pe.wait_ge(lo_done, 2 * v + q + 1)
                        for k in range(4):
                            ins = nc.tensor.transpose(tp[:, s, q, k * P:k * P + r],
                                                      rows[:, (4 * q + k) * P:(4 * q + k + 1) * P], ident[:r, :r])
                        ins.then_inc(transposed, 1)

                turns_of(pe, NT, N, transposes)
                transposes(NT, 0, NT // N, RS)


def project_rows(nc, tag, hi, lo, w, dst, nblocks, residual=None):
    GB = 5
    with Phase(nc, tag) as ph:
        raw = ph.sb(tag + "raw", [P, 2, KT * WB])
        whi = ph.sb(tag + "whi", [P, 2, KT * WB], F32R)
        wlo = ph.sb(tag + "wlo", [P, 2, KT * WB], F32R)
        stage = ph.sb(tag + "stage", [P, 4, 4, WB])
        stage_s = ph.sb(tag + "stage_s", [P, WB])
        acc = ph.ps(tag + "acc", [P, 2, 2, 2, WB])
        acc_s = ph.ps(tag + "acc_s", [P, 2 * WB])
        w_in = [ph.sem("w_in0"), ph.sem("w_in1")]
        w_hi, w_lo, summed, out_a, out_v = (ph.sem(n) for n in ("w_hi", "w_lo", "summed", "out_a", "out_v"))
        stored = [ph.sem(f"stored{g}") for g in range(GB)]
        res_in = [ph.sem(f"res_in{g}") for g in range(GB)]
        dst_t = dst[0:SEQ, :].rearrange("(t p) n -> p t n", p=P)
        res_t = residual[0:SEQ, :].rearrange("(t p) n -> p t n", p=P) if residual is not None else None
        C = 2

        with nc.Block() as block:

            @block.gpsimd
            def _(pool):
                pool.sem_inc(w_lo, C)

                def fetch(n, s, i):
                    ph.hold(pool, w_lo, n + 1)
                    pool.dma_start(raw[:, s, :], w[bass.ds(n, 1)].rearrange("o p n -> (o p) n")).then_inc(w_in[s], 16)

                def split(n, s, i):
                    ph.hold(pool, w_in[s], i * 16 + 16)
                    ph.hold(pool, summed, (n + 1) * GB)
                    nc.gpsimd.tensor_copy(whi[:, s, :], raw[:, s, :]).then_inc(w_hi, 1)
                    ph.hold(pool, w_hi, n + 1)
                    nc.gpsimd.tensor_tensor(wlo[:, s, :], raw[:, s, :], whi[:, s, :].bitcast(F32), ALU.subtract).then_inc(w_lo, 1)

                turns_of(pool, nblocks, 2, fetch, split)

            @block.sync
            def _(sp):
                for g in range(GB):
                    sp.sem_inc(stored[g], 16)

                def blk(n, s, i):
                    cols = bass.ds(n * WB, WB)
                    if residual is not None:
                        for g in range(GB):
                            ph.hold(sp, stored[g], n * 16 + 16)
                            if g < 4:
                                sp.dma_start(stage[:, g], res_t[:, 4 * g:4 * g + 4, cols]).then_inc(res_in[g], 16)
                            else:
                                sp.dma_start(stage_s[:RS], residual[SEQ:ROWS, cols]).then_inc(res_in[g], 16)
                    for g in range(GB):
                        ph.hold(sp, out_v, n * GB + g + 1 + GB)
                        if g < 4:
                            if residual is None:
                                ph.hold(sp, out_a, n * 4 + g + 1 + 4)
                            sp.dma_start(dst_t[:, 4 * g:4 * g + 4, cols], stage[:, g]).then_inc(stored[g], 16)
                        else:
                            sp.dma_start(dst[SEQ:ROWS, cols], stage_s[:RS]).then_inc(stored[g], 16)

                pairs(sp, nblocks, blk)
                for g in range(GB):
                    ph.hold(sp, stored[g], 16 + 16 * nblocks)

            @block.scalar
            def _(act):
                if residual is not None:
                    return
                act.sem_inc(out_a, 4)

                def blk(n, s, i):
                    if residual is None:
                        for g in range(4):
                            act.wait_ge(summed, (n + C) * GB + g + 1)
                            act.wait_ge(stored[g], n * 16 + 16)
                            nc.scalar.activation(stage[:, g, 0:2, :], acc[:, g % 2, 0, :, :], ACT.Copy).then_inc(out_a, 1)

                pairs(act, nblocks, blk)

            @block.vector
            def _(dve):
                dve.sem_inc(out_v, GB)

                def blk(n, s, i):
                    for g in range(GB):
                        dve.wait_ge(summed, (n + C) * GB + g + 1)
                        if residual is not None:
                            dve.wait_ge(res_in[g], n * 16 + 16)
                            if g < 4:
                                nc.vector.tensor_tensor(stage[:, g, 0:2, :], acc[:, g % 2, 0], stage[:, g, 0:2, :], ALU.add)
                                ins = nc.vector.tensor_tensor(stage[:, g, 2:4, :], acc[:, g % 2, 1], stage[:, g, 2:4, :], ALU.add)
                            else:
                                ins = nc.vector.tensor_tensor(stage_s[:RS], acc_s[:RS, :WB], stage_s[:RS], ALU.add)
                        else:
                            dve.wait_ge(stored[g], n * 16 + 16)
                            if g < 4:
                                ins = nc.vector.tensor_copy(stage[:, g, 2:4, :], acc[:, g % 2, 1])
                            else:
                                ins = nc.vector.tensor_copy(stage_s[:RS], acc_s[:RS, :WB])
                        ins.then_inc(out_v, 1)

                pairs(dve, nblocks, blk)

            @block.tensor
            def _(pe):
                pe.sem_inc(summed, C * GB)

                def product(out, v, r, s):
                    for k in range(KT):
                        h = hi[:, k, v * P:v * P + r]
                        l = lo[:, k, v * P:v * P + r]
                        wh = whi[:, s, k * WB:(k + 1) * WB]
                        wl = wlo[:, s, k * WB:(k + 1) * WB]
                        for n, (a, b) in enumerate(((h, wh), (h, wl), (l, wh))):
                            ins = nc.tensor.matmul(out, a, b, start=(k == 0 and n == 0), stop=(k == KT - 1 and n == 2))
                    return ins

                def blk(n, s, i):
                    pe.wait_ge(w_lo, n + 1 + C)
                    for g in range(GB):
                        if g < 4:
                            before = n * GB + g - 2 if g >= 2 else (n - 1) * GB + g + 2
                            before_a = n * 4 + g - 2
                            pe.wait_ge(out_v, before + 1 + GB)
                            if residual is None:
                                pe.wait_ge(out_a, before_a + 1 + 4)
                            for t in range(4):
                                ins = product(acc[:, g % 2, t // 2, t % 2, :], 4 * g + t, P, s)
                        else:
                            pe.wait_ge(out_v, n * GB + g + 1)
                            ins = product(acc_s[:RS, :WB], NT, RS, s)
                        ins.then_inc(summed, 1)

                pairs(pe, nblocks, blk)


def project_conv(nc, hi, lo, w, conv_w, conv_state, conv_t, conv_s, state_p, state_s):
    BL = 4
    TB = SEQ // BL
    HIST = CONV - 1
    with Phase(nc, "conv") as ph:
        wr = ph.sb("cwr", [P, 2, D])
        whi = ph.sb("cwhi", [P, 2, D], F32R)
        wlo = ph.sb("cwlo", [P, 2, D], F32R)
        cw = ph.sb("ccw", [P, CT * CONV])
        cwh = ph.sb("ccwh", [P, CT * CONV])
        x = ph.sb("cx", [P, 2, HIST + SEQ])
        xs = ph.sb("cxs", [P, 2, NB, HIST + DS])
        y = ph.sb("cy", [P, 2, SEQ + RS])
        th = ph.sb("cth", [P, SEQ + RS])
        acc = ph.ps("cacc", [P, BL, TB])
        acc_s = ph.ps("cacc_s", [P, 2, TB])
        w_in = [ph.sem("cw_in0"), ph.sem("cw_in1")]
        small_in, w_hi, w_lo, summed, halves, zeroed = (
            ph.sem(n) for n in ("small_in", "w_hi", "w_lo", "summed", "halves", "zeroed"))
        raw_a, conved, tanhed, siluc, chained = (
            ph.sem(n) for n in ("raw_a", "conved", "tanhed", "siluc", "chained"))
        state_in = [ph.sem("state_in0"), ph.sem("state_in1")]
        stored = [ph.sem("stored0"), ph.sem("stored1")]
        C = 2

        with nc.Block() as block:

            @block.gpsimd
            def _(pool):
                nc.gpsimd.memset(x[:, :, 0:HIST], 0.0).then_inc(zeroed, 1)

                pool.sem_inc(w_lo, C)

                def fetch(n, s, i):
                    ph.hold(pool, w_lo, n + 1)
                    pool.dma_start(wr[:, s, :], w[bass.ds(n, 1)].rearrange("o p n -> (o p) n")).then_inc(w_in[s], 16)

                def split(n, s, i):
                    ph.hold(pool, w_in[s], i * 16 + 16)
                    ph.hold(pool, summed, (n + 1) * (BL + 1))
                    nc.gpsimd.tensor_copy(whi[:, s, :], wr[:, s, :]).then_inc(w_hi, 1)
                    ph.hold(pool, w_hi, n + 1)
                    nc.gpsimd.tensor_tensor(wlo[:, s, :], wr[:, s, :], whi[:, s, :].bitcast(F32), ALU.subtract).then_inc(w_lo, 1)

                turns_of(pool, CT, 2, fetch, split)

            @block.sync
            def _(sp):
                for s in range(2):
                    sp.sem_inc(stored[s], 64)
                sp.dma_start(cw[:], conv_w).then_inc(small_in, 16)

                def load(n, s, i):
                    ph.hold(sp, conved, n + 1)
                    ph.hold(sp, stored[s], i * 64 + 64)
                    sp.dma_start(xs[:, s, :, 0:HIST], conv_state[bass.ds(n, 1)].rearrange("o p b t -> (o p) b t")).then_inc(state_in[s], 16)

                def put(n, s, i):
                    ph.hold(sp, raw_a, (n + 1) * (BL + 1) + BL + 1)
                    sp.dma_start(state_p[bass.ds(n, 1)].rearrange("o p t -> (o p) t"), x[:, s, SEQ:SEQ + HIST],
                                 allow_slow_non_contiguous=True).then_inc(stored[s], 16)
                    sp.dma_start(state_s[bass.ds(n, 1)].rearrange("o p b t -> (o p) b t"), xs[:, s, :, DS:DS + HIST],
                                 allow_slow_non_contiguous=True).then_inc(stored[s], 16)
                    ph.hold(sp, siluc, n + 1)
                    sp.dma_start(conv_t[bass.ds(n * P, P), :], y[:, s, :SEQ]).then_inc(stored[s], 16)
                    sp.dma_start(conv_s[bass.ds(n * P, P), :], y[:, s, SEQ:]).then_inc(stored[s], 16)

                turns_of(sp, CT, 2, load, put)
                for s in range(2):
                    sp.wait_ge(stored[s], 64 + 64 * CT // 2)

            @block.scalar
            def _(act):
                act.sem_inc(raw_a, BL + 1)

                def copies(n, s, i):
                    act.wait_ge(conved, n + 1)
                    act.wait_ge(stored[s], i * 64 + 64)
                    for b in range(BL + 1):
                        act.wait_ge(summed, (n + C) * (BL + 1) + b + 1)
                        if b < BL:
                            nc.scalar.activation(x[:, s, HIST + b * TB:HIST + (b + 1) * TB], acc[:, b], ACT.Copy).then_inc(raw_a, 1)
                        else:
                            nc.scalar.activation(xs[:, s, :, HIST:], acc_s[:, 0, :RS].rearrange("p (b t) -> p b t", b=NB),
                                                 ACT.Copy).then_inc(raw_a, 1)
                    act.wait_ge(conved, n + 1 + C)
                    nc.scalar.activation(th[:], y[:, s], ACT.Tanh).then_inc(tanhed, 1)

                pairs(act, CT, copies)

            @block.vector
            def _(dve):
                dve.sem_inc(conved, C)
                dve.wait_ge(small_in, 16)
                nc.vector.tensor_scalar(cwh[:], cw[:], 0.5, None, ALU.mult).then_inc(halves, 1)
                dve.wait_ge(halves, 1)
                dve.wait_ge(zeroed, 1)
                chain = Chain(dve, chained)

                def ch(n, s, i):
                    chain.turn(n * (2 * (CONV - 1)))
                    dve.wait_ge(raw_a, (n + 1) * (BL + 1) + BL + 1)
                    dve.wait_ge(state_in[s], i * 16 + 16)
                    dve.wait_ge(stored[s], i * 64 + 64)
                    ys = y[:, s, SEQ:].rearrange("p (b t) -> p b t", b=NB)
                    for out, src in ((y[:, s, :SEQ], lambda j: x[:, s, j:j + SEQ]), (ys, lambda j: xs[:, s, :, j:j + DS])):
                        tap = lambda j: cwh[:, bass.ds(n * CONV + j, 1)]
                        chain.link(nc.vector.tensor_scalar(out, src(0), tap(0), None, ALU.mult))
                        for j in range(1, CONV):
                            ins = nc.vector.scalar_tensor_tensor(out, src(j), tap(j), out, ALU.mult, ALU.add)
                            if j < CONV - 1:
                                chain.link(ins)
                    ins.then_inc(conved, 1)
                    dve.wait_ge(tanhed, n + 1)
                    nc.vector.scalar_tensor_tensor(y[:, s], th[:], 1.0, y[:, s], ALU.add, ALU.mult).then_inc(siluc, 1)
                    assert chain.n == 2 * (CONV - 1)

                pairs(dve, CT, ch)

            @block.tensor
            def _(pe):
                pe.sem_inc(summed, C * (BL + 1))

                def ch(n, s, i):
                    pe.wait_ge(w_lo, n + 1 + C)
                    for b in range(BL + 1):
                        pe.wait_ge(raw_a, n * (BL + 1) + b + 1)
                        cols = slice(b * TB, (b + 1) * TB) if b < BL else slice(SEQ, ROWS)
                        out = acc[:, b] if b < BL else acc_s[:, 0, :RS]
                        for k in range(KT):
                            wh, wl = whi[:, s, k * P:(k + 1) * P], wlo[:, s, k * P:(k + 1) * P]
                            for m, (a, z) in enumerate(((wh, hi), (wh, lo), (wl, hi))):
                                ins = nc.tensor.matmul(out, a, z[:, k, cols], start=(k == 0 and m == 0),
                                                       stop=(k == KT - 1 and m == 2))
                        ins.then_inc(summed, 1)

                pairs(pe, CT, ch)


def project_gates(nc, tag, hi, lo, w, vecs, fold_d, gates, kind):
    with Phase(nc, tag + "g") as ph:
        raw = ph.sb(tag + "graw", [P, KT, 8])
        whl = ph.sb(tag + "gwhl", [P, KT, 16], F32R)
        wh0 = ph.sb(tag + "gwh0", [P, KT, 16], F32R)
        g16 = ph.sb(tag + "g16", [16, ROWS])
        fold = ph.sb(tag + "gfold", [16, 8])
        vec = ph.sb(tag + "gvec", [P, 8])
        vecx = ph.sb(tag + "gvecx", [P, 4])
        z = ph.sb(tag + "gz", [P, NT + 1, 8])
        t = [ph.sb(tag + f"gt{j}", [P, NT + 1, 4]) for j in range(4)]
        acc = ph.ps(tag + "gacc", [P, NT + 1, 8])
        gt = [ph.ps(tag + f"gcols{b}", [P, 512]) for b in range(5)]
        w_in, zeroed, w_hi, w_lo, columns, copied, summed, out, act_done, chained = (
            ph.sem(n) for n in ("w_in", "zeroed", "w_hi", "w_lo", "columns", "copied", "summed", "out", "act_done", "chained"))
        with nc.Block() as block:

            @block.sync
            def _(sp):
                sp.dma_start(raw[:].rearrange("p k n -> p (k n)"), w).then_inc(w_in, 16)
                sp.dma_start(fold[:], fold_d).then_inc(w_in, 16)
                sp.dma_start(vec[:], vecs.partition_broadcast(P)).then_inc(w_in, 16)

            @block.tensor
            def _(pe):
                pe.wait_ge(w_lo, 1)
                for b in range(5):
                    cols = slice(b * 512, min(ROWS, (b + 1) * 512))
                    for k in range(KT):
                        nc.tensor.matmul(gt[b][:16, :cols.stop - cols.start], whl[:, k, :], hi[:, k, cols], start=(k == 0), stop=False)
                        ins = nc.tensor.matmul(gt[b][:16, :cols.stop - cols.start], wh0[:, k, :], lo[:, k, cols], start=False, stop=(k == KT - 1))
                    ins.then_inc(columns, 1)
                for v in range(NT + 1):
                    r = P if v < NT else RS
                    pe.wait_ge(copied, v // 4 + 1)
                    ins = nc.tensor.matmul(acc[:r, v, :], g16[:, v * P:v * P + r], fold[:], start=True, stop=True)
                ins.then_inc(summed, 1)

            @block.scalar
            def _(act):
                act.wait_ge(w_in, 48)
                act.wait_ge(zeroed, 1)
                nc.scalar.activation(whl[:, :, 0:8], raw[:], ACT.Copy)
                nc.scalar.activation(wh0[:, :, 0:8], raw[:], ACT.Copy).then_inc(w_hi, 1)
                for b in range(5):
                    act.wait_ge(columns, b + 1)
                    w = min(512, ROWS - b * 512)
                    nc.scalar.activation(g16[:, b * 512:b * 512 + w], gt[b][:16, :w], ACT.Copy).then_inc(copied, 1)
                if kind == "gdn":
                    nc.scalar.activation(vecx[:], vec[:, 0:4], ACT.Exp).then_inc(act_done, 1)
                else:
                    act.sem_inc(act_done, 1)
                act.wait_ge(out, 1)
                if kind == "gdn":
                    nc.scalar.activation(t[3][:], z[:, :, 0:4], ACT.Tanh, scale=0.5).then_inc(act_done, 1)
                else:
                    act.sem_inc(act_done, 1)
                nc.scalar.activation(t[1][:], t[0][:], ACT.Exp, scale=-1.0).then_inc(act_done, 1)
                act.wait_ge(act_done, 3)
                nc.scalar.activation(t[1][:], t[1][:], ACT.Ln, bias=1.0).then_inc(act_done, 1)

            @block.vector
            def _(dve):
                chain = Chain(dve, chained)
                nc.vector.memset(wh0[:].bitcast(F32), 0.0).then_inc(zeroed, 1)
                chain.link(nc.vector.memset(z[:], 0.0))
                dve.wait_ge(w_hi, 1)
                nc.vector.tensor_tensor(whl[:, :, 8:16], raw[:], whl[:, :, 0:8].bitcast(F32), ALU.subtract).then_inc(w_lo, 1)
                dve.wait_ge(summed, 1)
                nc.vector.tensor_copy(z[:, 0:NT, :], acc[:, 0:NT, :])
                chain.link(nc.vector.tensor_copy(z[:RS, NT, :], acc[:RS, NT, :]))
                bias = vec[:, 4:8].rearrange("p (o h) -> p o h", o=1).to_broadcast([P, NT + 1, 4])
                chain.link(nc.vector.tensor_tensor(t[2][:], z[:, :, 4:8], bias, ALU.add))
                sign = 1.0 if kind == "gdn" else -1.0
                if kind != "gdn":
                    chain.link(nc.vector.tensor_scalar(t[2][:], t[2][:], -1.0, None, ALU.mult))
                chain.link(nc.vector.tensor_scalar(t[0][:], t[2][:], -1.0, None, ALU.mult))
                nc.vector.tensor_tensor(t[0][:], t[0][:], t[2][:], ALU.max).then_inc(out, 1)
                dve.wait_ge(act_done, 4)
                chain.link(nc.vector.scalar_tensor_tensor(t[2][:], t[2][:], 0.0, t[1][:], ALU.max, ALU.add))
                if kind == "gdn":
                    rate = vecx[:].rearrange("p (o h) -> p o h", o=1).to_broadcast([P, NT + 1, 4])
                    chain.link(nc.vector.scalar_tensor_tensor(gates[:, :, 0:4], t[2][:], -1.0, rate, ALU.mult, ALU.mult))
                    chain.link(nc.vector.tensor_scalar(gates[:, :, 4:8], t[3][:], 1.0, 0.5, ALU.add, ALU.mult))
                else:
                    bi = vec[:, 0:4].rearrange("p (o h) -> p o h", o=1).to_broadcast([P, NT + 1, 4])
                    chain.link(nc.vector.tensor_scalar(gates[:, :, 0:4], t[2][:], -1.0, None, ALU.mult))
                    chain.link(nc.vector.tensor_tensor(gates[:, :, 4:8], z[:, :, 0:4], bi, ALU.add))


def spread(ap, n):
    return ap.rearrange("p (h o) -> p h o", o=1).to_broadcast([ap.shape[0], ap.shape[1], n])


def repeat(ap, n):
    return ap.rearrange("p (o r) -> p o r", o=1).to_broadcast([ap.shape[0], n, ap.shape[1]])


class Events:

    def __init__(self, ph, names, first=1):
        self.ph, self.first, self.s = ph, first, {n: ph.sem(n) for n in names.split()}

    def __getitem__(self, name):
        return self.s[name]

    def open(self, eng, names):
        for n in names.split():
            eng.sem_inc(self.s[n], self.first)

    def done(self, eng, name, v):
        self.ph.hold(eng, self.s[name], v + 1 + self.first)

    def ago(self, eng, name, v, k):
        assert k <= self.first
        self.ph.hold(eng, self.s[name], v + (1 + self.first - k))

    def prev(self, eng, name, v):
        self.ago(eng, name, v, 1)


def gated_delta(nc, a, proj, conv_t, conv_s, gates, merged, out_p, out_s):
    with Phase(nc, "gdn") as ph:
        sb, ps = ph.sb, ph.ps
        ident, ones = sb("d_id", [P, P]), sb("d_ones", [P, P])
        upper, levels = sb("d_up", [P, P]), sb("d_lv", [P, LEVELS, P])
        upper_s, levels_s, same_s = sb("d_ups", [RS, RS]), sb("d_lvs", [RS, LEVELS_S, RS]), sb("d_sms", [RS, RS])
        member, own = sb("d_mem", [RS, NB]), sb("d_own", [P, NB, RS])
        nw, pw = sb("d_nw", [P, DK]), sb("d_pw", [P, 8])
        c = sb("d_c", [P, 2, CT, P])
        z = sb("d_z", [P, 2, 512])
        gt, sm, rn = sb("d_gt", [P, 2, 8]), sb("d_sm", [P, 16]), sb("d_rn", [P, 8])
        bt, kd, egc = sb("d_bt", [P, 2, 4]), sb("d_kd", [P, 8]), sb("d_egc", [P, 2, 4])
        sq, dgn = sb("d_sq", [P, 8, P]), sb("d_dgn", [P, 8, P])
        dgu, dgb = sb("d_dgu", [P, H, P]), sb("d_dgb", [P, H, P])
        eg, dt = sb("d_eg", [P, 2, H, P]), sb("d_dt", [P, H, P])
        qk = sb("d_qk", [P, 2, 8, P])
        kt, vt = sb("d_kt", [P, H, DK]), sb("d_vt", [P, 2, H, DK])
        qt, at = sb("d_qt", [P, 2, H, P]), sb("d_at", [P, H, P])
        mt = sb("d_mt", [P, 2, LEVELS, H, P])
        T, U, Y = sb("d_T", [P, H, P]), sb("d_U", [P, 2, H, P]), sb("d_Y", [P, H, P])
        r1, vn = sb("d_r1", [P, H, DK]), sb("d_vn", [P, H, DK])
        qg, kw = sb("d_qg", [P, 2, H, P]), sb("d_kw", [P, 2, H, DK])
        osq, th, zs, og = (sb("d_" + n, [P, H, DK]) for n in ("osq", "th", "zs", "og"))
        oss, rr = sb("d_oss", [P, 8]), sb("d_rr", [P, 4])
        S, Ss = sb("d_S", [P, H, 1, DK]), sb("d_Ss", [P, H, NB, DK])
        kts, qgs = sb("d_kts", [P, H, NB, RS]), sb("d_qgs", [P, H, NB, RS])
        kws = sb("d_kws", [RS, NB, H, DK])
        q_b, k_b, row_b, beta_b, y_b, u_b, s_b, o_b = (
            ps("d_" + n, [P, 512]) for n in ("qb", "kb", "row", "beta", "yb", "ub", "sb", "ob"))

        consts_in, set_up = ph.sem("consts_in"), ph.sem("set_up")
        c_in, z_in = [ph.sem("c_in0"), ph.sem("c_in1")], [ph.sem("z_in0"), ph.sem("z_in1")]
        ev = Events(ph, "gate sq small smc rn dgs dgn rows bcn eg kd dT DT qk kkq tok tokc qkt kS r vn vnc qg kw o dS "
                        "S osq th ms rr zs og", first=2)
        mts, ys, ycs, tys, yus, tts, tus = (ph.sem(n) for n in ("mt", "y", "yc", "ty", "yu", "tt", "tu"))
        TU0 = LEVELS + 1
        stored, chained, chained_p, batch_dS, batch_S = (
            ph.sem(n) for n in ("stored", "chained", "chained_p", "batch_dS", "batch_S"))
        PROMPT, SAMPLE = (P, 1, upper, levels, LEVELS, S), (RS, NB, upper_s, levels_s, LEVELS_S, Ss)

        LEVEL_COUNT = 7

        def staged(eng, front, inverse, back, chain=None, per=0):

            def f(n, t):
                if t and front[n]:
                    front[n](*t)

            def lv(l, t):
                if inverse and l < t[LEVEL_COUNT]:
                    inverse(l, *t)

            def b(n, t):
                if t and back[n]:
                    back[n](*t)

            def step(mid, nxt, old):
                for l in range(LEVELS):
                    lv(l, mid)
                    f(l, nxt)
                    b(l, old)

            def tile(v, s, i, kind=PROMPT):
                return (v, s, i, *kind)

            for n in range(LEVELS):
                f(n, tile(0, 0, 0))
            step(tile(0, 0, 0), tile(1, 1, 0), None)
            before = chain.n if chain else 0
            with eng.Fori(0, NT // 2 - 1) as i:
                if chain:
                    chain.turn(i * per + before)
                step(tile(i * 2 + 1, 1, i), tile(i * 2 + 2, 0, i + 1), tile(i * 2, 0, i))
                step(tile(i * 2 + 2, 0, i + 1), tile(i * 2 + 3, 1, i + 1), tile(i * 2 + 1, 1, i))
                assert not chain or chain.n == per
            if chain:
                chain.turn((NT // 2 - 1) * per + before)
            i = NT // 2 - 1
            step(tile(NT - 1, 1, i), tile(NT, 0, i + 1, SAMPLE), tile(NT - 2, 0, i))
            step(tile(NT, 0, i + 1, SAMPLE), None, tile(NT - 1, 1, i))
            for n in range(LEVELS):
                b(n, tile(NT, 0, i + 1, SAMPLE))

        def v3(b, w, rows=P):
            return b[:rows, :H * w].rearrange("p (h r) -> p h r", h=H)

        with nc.Block() as block:

            @block.sync
            def _(sp):
                loads = [(ident[:], a["ident"]), (ones[:], a["same"]), (upper[:], a["upper"]), (levels[:], a["levels"]),
                         (upper_s[:], a["upper_s"]), (levels_s[:], a["levels_s"]), (same_s[:], a["same_s"]),
                         (member[:], a["member"]), (own[:], a["own"].partition_broadcast(P)),
                         (nw[:], a["gdn_norm"].partition_broadcast(P)), (Ss[:], a["gdn_state"])]
                assert len(loads) == 11

                def channels(v, s, r=P):
                    ev.ago(sp, "tok", v, 2)
                    src, cols = (conv_t, bass.ds(v * P, r)) if r == P else (conv_s, slice(0, RS))
                    sp.dma_start(c[:, s, :, :r], src.rearrange("(c p) t -> p c t", p=P)[:, :, cols]).then_inc(c_in[s], 16)

                def gate(v, s, r=P):
                    ev.ago(sp, "zs", v, 2)
                    sp.dma_start(z[:r, s, :], proj[bass.ds(v * P, r), 0:512]).then_inc(z_in[s], 16)

                def put(v, r=P):
                    ev.done(sp, "og", v)
                    sp.dma_start(merged[bass.ds(v * P, r), 0:512], og[:r].rearrange("p h d -> p (h d)")).then_inc(stored, 16)

                channels(0, 0)
                for dst, src in loads:
                    sp.dma_start(dst, src).then_inc(consts_in, 16)
                sp.sem_inc(stored, 16)
                channels(1, 1)
                gate(0, 0)
                channels(2, 0)
                gate(1, 1)
                channels(3, 1)
                gate(2, 0)
                put(0)
                with sp.Fori(0, NT // 2 - 2) as i:
                    for s in range(2):
                        v = i * 2 + (4 + s)
                        channels(v, s)
                        gate(v - 1, 1 - s)
                        put(v - 3)
                channels(NT, 0, RS)
                gate(NT - 1, 1)
                put(NT - 3)
                gate(NT, 0, RS)
                put(NT - 2)
                put(NT - 1)
                put(NT, RS)
                ev.done(sp, "S", NT - 1)
                sp.dma_start(out_p, S[:, :, 0, :]).then_inc(stored, 16)
                sp.wait_ge(batch_S, NB)
                sp.dma_start(out_s, Ss[:]).then_inc(stored, 16)
                sp.wait_ge(stored, 16 * (NT + 4))

            @block.gpsimd
            def _(pool):
                ev.open(pool, "rn qg kw zs rr")
                nc.gpsimd.memset(pw[:], -0.5).then_inc(set_up, 1)
                nc.gpsimd.memset(S[:], 0.0).then_inc(set_up, 1)
                pool.wait_ge(set_up, 2)
                pool.wait_ge(consts_in, 16 * 11)
                pool.sem_inc(mts, 1)
                chain = Chain(pool, chained_p)

                def roots(v, s, i, r, n, up, lv, L, St):
                    ev.done(pool, "smc", v)
                    ev.ago(pool, "dgn", v, 1)
                    nc.gpsimd.tensor_tensor(rn[:r], sm[:r, 0:8], pw[:r], ALU.pow).then_inc(ev["rn"], 1)

                def decayed(v, s, i, r, n, up, lv, L, St):
                    ev.done(pool, "qk", v)
                    ev.done(pool, "eg", v)
                    ev.ago(pool, "o", v, 2)
                    nc.gpsimd.tensor_tensor(qg[:, s, :, :r], qk[:, s, 0:4, :r], eg[:, s, :, :r], ALU.mult).then_inc(ev["qg"], 1)

                def joins(v, s, i, r, n, up, lv, L, St):
                    ev.done(pool, "qkt", v)
                    ph.hold(pool, tus, (v - 1) * LEVELS + TU0)
                    for l in range(L):
                        nc.gpsimd.tensor_tensor(mt[:r, s, l, :, :r], at[:r, :, :r], repeat(lv[:r, l, :r], H),
                                                ALU.mult).then_inc(mts, 1)

                def keys(v, s, i, r, n, up, lv, L, St):
                    decayed(v, s, i, r, n, up, lv, L, St)
                    ev.done(pool, "tokc", v)
                    ev.done(pool, "DT", v)
                    ev.ago(pool, "dS", v, 2)
                    nc.gpsimd.tensor_tensor(kw[:r, s], kt[:r], spread(kd[:r, 4:8], DK), ALU.mult).then_inc(ev["kw"], 1)

                def gate(v, s, i, r, n, up, lv, L, St):
                    ev.done(pool, "th", v)
                    ev.ago(pool, "og", v, 1)
                    chain.link(nc.gpsimd.tensor_scalar(zs[:r], th[:r], 1.0, 0.5, ALU.add, ALU.mult))
                    chain.link(nc.gpsimd.tensor_tensor(zs[:r], zs[:r], z[:r, s, :].rearrange("p (h d) -> p h d", h=H), ALU.mult))
                    nc.gpsimd.tensor_tensor(zs[:r], zs[:r], repeat(nw[:r], H), ALU.mult).then_inc(ev["zs"], 1)

                def root(v, s, i, r, n, up, lv, L, St):
                    ev.done(pool, "ms", v)
                    nc.gpsimd.tensor_tensor(rr[:r], oss[:r, 4:8], pw[:r, 0:4], ALU.pow).then_inc(ev["rr"], 1)

                staged(pool, [None, None, roots, None, None, joins, keys], None,
                       [gate, None, None, None, root, None, None], chain, 4)

            @block.scalar
            def _(act):
                ev.open(act, "sq eg DT tokc vnc th osq")
                act.sem_inc(ycs, 1)

                def squares(v, s, i, r, n, up, lv, L, St):
                    act.wait_ge(c_in[s], i * 16 + 16)
                    ev.ago(act, "small", v, 1)
                    nc.scalar.activation(sq[:, :, :r], c[:, s, 0:8, :r], ACT.Square).then_inc(ev["sq"], 1)

                def decays(v, s, i, r, n, up, lv, L, St):
                    ev.done(act, "kd", v)
                    ev.ago(act, "kw", v, 1)
                    nc.scalar.activation(kd[:r, 4:8], kd[:r, 0:4], ACT.Exp)
                    ev.done(act, "dT", v)
                    nc.scalar.activation(dt[:r, :, :r], dt[:r, :, :r], ACT.Exp).then_inc(ev["DT"], 1)

                def row_decays(v, s, i, r, n, up, lv, L, St):
                    ev.done(act, "smc", v)
                    ev.ago(act, "S", v, 2)
                    ev.ago(act, "qg", v, 2)
                    nc.scalar.activation(egc[:r, s], sm[:r, 8:12], ACT.Exp)
                    nc.scalar.activation(eg[:, s, :, :r], v3(row_b, r), ACT.Exp).then_inc(ev["eg"], 1)

                def tokens(v, s, i, r, n, up, lv, L, St):
                    ev.done(act, "tok", v)
                    ev.ago(act, "kw", v, 1)
                    ev.ago(act, "r", v, 2)
                    nc.scalar.activation(kt[:r], v3(row_b, DK, r), ACT.Copy)
                    nc.scalar.activation(vt[:r, s], v3(beta_b, DK, r), ACT.Copy).then_inc(ev["tokc"], 1)

                def level(l, v, s, i, r, n, up, lv, L, St):
                    if l:
                        act.wait_ge(ys, v * LEVELS + l + 1)
                        nc.scalar.activation(Y[:r, :, :r], v3(y_b, r, r), ACT.Copy).then_inc(ycs, 1)

                def gate(v, s, i, r, n, up, lv, L, St):
                    act.wait_ge(z_in[s], i * 16 + 16)
                    ev.ago(act, "zs", v, 1)
                    nc.scalar.activation(th[:r], z[:r, s, :].rearrange("p (h d) -> p h d", h=H), ACT.Tanh, scale=0.5).then_inc(ev["th"], 1)

                def values(v, s, i, r, n, up, lv, L, St):
                    ev.done(act, "vn", v)
                    ev.ago(act, "dS", v, 1)
                    nc.scalar.activation(vn[:r], v3(s_b, DK, r), ACT.Copy).then_inc(ev["vnc"], 1)

                def output_squares(v, s, i, r, n, up, lv, L, St):
                    ev.done(act, "o", v)
                    ev.ago(act, "ms", v, 1)
                    nc.scalar.activation(osq[:r], v3(o_b, DK, r), ACT.Square).then_inc(ev["osq"], 1)

                staged(act, [squares, None, None, decays, None, row_decays, tokens], level,
                       [gate, None, values, output_squares, None, None, None])

            @block.vector
            def _(dve):
                ev.open(dve, "gate smc dgs dgn kd dT qk qkt r S ms og")
                dve.sem_inc(tus, TU0)
                dve.sem_inc(tts, 1)
                dve.wait_ge(consts_in, 16 * 11)
                dve.wait_ge(set_up, 2)
                chain = Chain(dve, chained)

                def diagonals(v, s, i, r, n, up, lv, L, St):
                    ev.ago(dve, "small", v, 2)
                    nc.vector.tensor_copy(gt[:r, s], gates[:r, bass.ds(v, 1), :].rearrange("p o h -> p (o h)")).then_inc(ev["gate"], 1)
                    ev.done(dve, "gate", v)
                    ev.ago(dve, "rows", v, 1)
                    nc.vector.tensor_tensor(dgu[:r, :, :r], spread(gt[:r, s, 0:4], r), repeat(up[:r, :r], H), ALU.mult)
                    nc.vector.tensor_tensor(dgb[:r, :, :r], spread(gt[:r, s, 4:8], r), repeat(ident[:r, :r], H), ALU.mult).then_inc(ev["dgs"], 1)

                def sums(v, s, i, r, n, up, lv, L, St):
                    ev.done(dve, "small", v)
                    ev.ago(dve, "rn", v, 1)
                    ev.ago(dve, "eg", v, 1)
                    nc.vector.tensor_scalar(sm[:r, 0:8], q_b[:r, 0:8], EPS, None, ALU.add)
                    ev.ago(dve, "r", v, 2)
                    nc.vector.tensor_copy(bt[:r, s], gt[:r, s, 4:8])
                    nc.vector.tensor_copy(sm[:r, 8:16], q_b[:r, 8:16]).then_inc(ev["smc"], 1)

                def norms(v, s, i, r, n, up, lv, L, St):
                    ev.done(dve, "rn", v)
                    ev.ago(dve, "bcn", v, 1)
                    nc.vector.scalar_tensor_tensor(dgn[:r, 0:4, :r], spread(rn[:r, 0:4], r), DK ** -0.5,
                                                   repeat(ident[:r, :r], H), ALU.mult, ALU.mult)
                    nc.vector.tensor_tensor(dgn[:r, 4:8, :r], spread(rn[:r, 4:8], r), repeat(ident[:r, :r], H), ALU.mult).then_inc(ev["dgn"], 1)
                    ev.done(dve, "smc", v)
                    ev.ago(dve, "DT", v, 1)
                    nc.vector.tensor_tensor(kd[:r, 0:4], sm[:r, 12:16], sm[:r, 8:12], ALU.subtract).then_inc(ev["kd"], 1)
                    ev.done(dve, "rows", v)
                    for h in range(H):
                        ins = nc.vector.tensor_scalar(dt[:r, h, :r], row_b[:r, h * r:(h + 1) * r], sm[:r, 8 + h:9 + h], 0.0,
                                                      ALU.subtract, ALU.min)
                    ins.then_inc(ev["dT"], 1)

                def normed(v, s, i, r, n, up, lv, L, St):
                    ev.done(dve, "bcn", v)
                    dve.wait_ge(c_in[s], i * 16 + 16)
                    ev.ago(dve, "kS", v, 2)
                    ev.ago(dve, "qg", v, 2)
                    nc.vector.tensor_tensor(qk[:, s, 0:4, :r], c[:, s, 0:4, :r], v3(q_b, r), ALU.mult)
                    nc.vector.tensor_tensor(qk[:, s, 4:8, :r], c[:, s, 4:8, :r], v3(k_b, r), ALU.mult).then_inc(ev["qk"], 1)
                    ev.done(dve, "DT", v)
                    chain.link(nc.vector.tensor_tensor(dt[:r, :, :r], dt[:r, :, :r], repeat(up[:r, :r], H), ALU.mult))

                def products(v, s, i, r, n, up, lv, L, St):
                    ev.done(dve, "kkq", v)
                    dve.wait_ge(mts, v * LEVELS + 1)
                    ev.ago(dve, "o", v, 2)
                    chain.link(nc.vector.tensor_tensor(at[:r, :, :r], v3(q_b, r, r), dt[:r, :, :r], ALU.mult))
                    nc.vector.tensor_tensor(qt[:r, s, :, :r], v3(k_b, r, r), dt[:r, :, :r], ALU.mult)
                    nc.vector.tensor_tensor(at[:r, :, :r], at[:r, :, :r], v3(beta_b, r, r), ALU.mult).then_inc(ev["qkt"], 1)
                    if n > 1:
                        ev.done(dve, "qk", v)
                        ev.done(dve, "qg", v)
                        for h in range(H):
                            nc.vector.tensor_tensor(kts[:, h], repeat(qk[:, s, 4 + h, :r], NB), own[:], ALU.mult)
                            nc.vector.tensor_tensor(qgs[:, h], repeat(qg[:, s, h, :r], NB), own[:], ALU.mult)

                def level(l, v, s, i, r, n, up, lv, L, St):
                    if l == 0:
                        dve.wait_ge(mts, v * LEVELS + 2)
                        dve.wait_ge(ys, v * LEVELS + 1)
                        dve.wait_ge(tts, v * (LEVELS - 1) + 1)
                        nc.vector.tensor_tensor(T[:r, :, :r], repeat(ident[:r, :r], H), v3(y_b, r, r), ALU.subtract).then_inc(tts, 1)
                        ev.ago(dve, "vn", v, 2)
                        dve.wait_ge(tus, v * LEVELS + TU0)
                        nc.vector.tensor_tensor(U[:r, s, :, :r], repeat(ident[:r, :r], H), mt[:r, s, 0, :, :r], ALU.subtract).then_inc(tus, 1)
                    else:
                        if l < L - 1:
                            dve.wait_ge(tys, v * (LEVELS - 2) + l)
                            dve.wait_ge(tts, v * (LEVELS - 1) + l + 1)
                            nc.vector.tensor_tensor(T[:r, :, :r], T[:r, :, :r], v3(y_b, r, r), ALU.subtract).then_inc(tts, 1)
                        dve.wait_ge(yus, v * (LEVELS - 1) + l)
                        dve.wait_ge(tus, v * LEVELS + l + TU0)
                        nc.vector.tensor_tensor(U[:r, s, :, :r], U[:r, s, :, :r], v3(u_b, r, r), ALU.subtract).then_inc(tus, 1)

                def residual(v, s, i, r, n, up, lv, L, St):
                    ev.done(dve, "kS", v)
                    ev.done(dve, "eg", v)
                    ev.ago(dve, "vn", v, 1)
                    chain.link(nc.vector.tensor_tensor(r1[:r], v3(s_b, DK, r), spread(egc[:r, s], DK), ALU.mult))
                    ev.done(dve, "tokc", v)
                    chain.link(nc.vector.tensor_tensor(r1[:r], vt[:r, s], r1[:r], ALU.subtract))
                    nc.vector.tensor_tensor(r1[:r], r1[:r], spread(bt[:r, s], DK), ALU.mult).then_inc(ev["r"], 1)

                def states(v, s, i, r, n, up, lv, L, St):
                    means(v, s, i, r, n, up, lv, L, St)
                    if n == 1:
                        ev.done(dve, "dS", v)
                        ev.prev(dve, "S", v)
                        for h in range(H):
                            ins = nc.vector.scalar_tensor_tensor(S[:, h, 0, :], S[:, h, 0, :], eg[:, s, h, r - 1:r],
                                                                 s_b[:, h * DK:(h + 1) * DK], ALU.mult, ALU.add)
                        ins.then_inc(ev["S"], 1)
                    else:
                        ev.done(dve, "kw", v)
                        for b in range(NB):
                            ins = nc.vector.tensor_scalar(kws[:, b], kw[:r, s], member[:, b:b + 1], None, ALU.mult)
                        ins.then_inc(ev["S"], 1)
                        for b in range(NB):
                            dve.wait_ge(batch_dS, b + 1)
                            for h in range(H):
                                ins = nc.vector.scalar_tensor_tensor(
                                    Ss[:, h, b, :], Ss[:, h, b, :], eg[:, s, h, DS * b + DS - 1:DS * b + DS],
                                    s_b[:, h * DK:(h + 1) * DK], ALU.mult, ALU.add)
                            ins.then_inc(batch_S, 1)

                def means(v, s, i, r, n, up, lv, L, St):
                    ev.done(dve, "osq", v)
                    ev.ago(dve, "rr", v, 1)
                    chain.link(nc.vector.tensor_reduce(oss[:r, 0:4], osq[:r], AX.X, ALU.add))
                    nc.vector.tensor_scalar(oss[:r, 4:8], oss[:r, 0:4], 1.0 / DK, EPS, ALU.mult, ALU.add).then_inc(ev["ms"], 1)

                def outputs(v, s, i, r, n, up, lv, L, St):
                    ev.done(dve, "rr", v)
                    dve.wait_ge(stored, v * 16 + 16)
                    chain.link(nc.vector.tensor_tensor(og[:r], v3(o_b, DK, r), spread(rr[:r], DK), ALU.mult))
                    ev.done(dve, "zs", v)
                    nc.vector.tensor_tensor(og[:r], og[:r], zs[:r], ALU.mult).then_inc(ev["og"], 1)

                staged(dve, [diagonals, None, sums, norms, normed, products, None], level,
                       [None, residual, None, None, states, None, outputs], chain, 12)

            @block.tensor
            def _(pe):
                ev.open(pe, "small rows bcn kkq tok kS vn o dS")
                pe.wait_ge(consts_in, 16 * 11)
                mm = nc.tensor.matmul

                def sums(v, s, i, r, n, up, lv, L, St):
                    ev.done(pe, "sq", v)
                    ev.ago(pe, "qkt", v, 1)
                    for j in range(8):
                        mm(q_b[:r, j:j + 1], sq[:, j, :r], ones[:, 0:1], start=True, stop=True)
                    ev.done(pe, "gate", v)
                    same = ones if n == 1 else same_s
                    mm(q_b[:r, 8:12], up[:r, :r], gt[:r, s, 0:4], start=True, stop=True)
                    mm(q_b[:r, 12:16], same[:r, :r], gt[:r, s, 0:4], start=True, stop=True).then_inc(ev["small"], 1)
                    ev.done(pe, "dgs", v)
                    ev.ago(pe, "tokc", v, 1)
                    mm(row_b[:, :H * r], ones[:r, :], dgu[:r, :, :r], start=True, stop=True)
                    mm(beta_b[:r, :H * r], ones[:r, :r], dgb[:r, :, :r], start=True, stop=True).then_inc(ev["rows"], 1)

                def norms(v, s, i, r, n, up, lv, L, St):
                    ev.done(pe, "dgn", v)
                    mm(q_b[:, :H * r], ones[:r, :], dgn[:r, 0:4, :r], start=True, stop=True)
                    mm(k_b[:, :H * r], ones[:r, :], dgn[:r, 4:8, :r], start=True, stop=True).then_inc(ev["bcn"], 1)

                def products(v, s, i, r, n, up, lv, L, St):
                    ev.done(pe, "qk", v)
                    for h in range(H):
                        mm(q_b[:r, h * r:(h + 1) * r], qk[:, s, 4 + h, :r], qk[:, s, 4 + h, :r], start=True, stop=True)
                        ins = mm(k_b[:r, h * r:(h + 1) * r], qk[:, s, 4 + h, :r], qk[:, s, h, :r], start=True, stop=True)
                    ins.then_inc(ev["kkq"], 1)

                def tokens(v, s, i, r, n, up, lv, L, St):
                    ev.done(pe, "eg", v)
                    ev.done(pe, "qkt", v)
                    for h in range(H):
                        nc.tensor.transpose(row_b[:r, h * DK:(h + 1) * DK], qk[:, s, 4 + h, :r], ident[:])
                        ins = nc.tensor.transpose(beta_b[:r, h * DK:(h + 1) * DK], c[:, s, 8 + h, :r], ident[:])
                    ins.then_inc(ev["tok"], 1)

                def level(l, v, s, i, r, n, up, lv, L, St):
                    pe.wait_ge(mts, v * LEVELS + l + 2)
                    pe.wait_ge(tts, v * (LEVELS - 1) + l + 1)
                    for h in range(H):
                        out, m = y_b[:r, h * r:(h + 1) * r], mt[:r, s, l, h, :r]
                        ins = mm(out, m, T[:r, h, :r], start=True, stop=True) if l else nc.tensor.transpose(out, m, ident[:r, :r])
                    ins.then_inc(ys, 1)
                    if l:
                        pe.wait_ge(ycs, v * (LEVELS - 1) + l + 1)
                        pe.wait_ge(tus, v * LEVELS + l + TU0)
                        if l < L - 1:
                            for h in range(H):
                                ins = mm(y_b[:r, h * r:(h + 1) * r], U[:r, s, h, :r], Y[:r, h, :r], start=True, stop=True)
                            ins.then_inc(tys, 1)
                        for h in range(H):
                            ins = mm(u_b[:r, h * r:(h + 1) * r], Y[:r, h, :r], U[:r, s, h, :r], start=True, stop=True)
                        ins.then_inc(yus, 1)

                def residual(v, s, i, r, n, up, lv, L, St):
                    ev.ago(pe, "S", v, 1)
                    for h in range(H):
                        for b in range(n):
                            ins = mm(s_b[:r, h * DK:(h + 1) * DK], qk[:, s, 4 + h, :r] if n == 1 else kts[:, h, b],
                                     St[:, h, b, :], start=(b == 0), stop=(b == n - 1))
                    ins.then_inc(ev["kS"], 1)

                def values(v, s, i, r, n, up, lv, L, St):
                    ev.done(pe, "r", v)
                    pe.wait_ge(tus, v * LEVELS + L + TU0)
                    for h in range(H):
                        ins = mm(s_b[:r, h * DK:(h + 1) * DK], U[:r, s, h, :r], r1[:r, h, :], start=True, stop=True)
                    ins.then_inc(ev["vn"], 1)

                def outputs(v, s, i, r, n, up, lv, L, St):
                    ev.done(pe, "vnc", v)
                    ev.done(pe, "qg", v)
                    ev.ago(pe, "og", v, 1)
                    for h in range(H):
                        for b in range(n):
                            mm(o_b[:r, h * DK:(h + 1) * DK], qg[:, s, h, :r] if n == 1 else qgs[:, h, b],
                               St[:, h, b, :], start=(b == 0), stop=False)
                        ins = mm(o_b[:r, h * DK:(h + 1) * DK], qt[:r, s, h, :r], vn[:r, h, :], start=False, stop=True)
                    ins.then_inc(ev["o"], 1)
                    ev.done(pe, "kw", v)
                    if n == 1:
                        for h in range(H):
                            ins = mm(s_b[:, h * DK:(h + 1) * DK], kw[:r, s, h, :], vn[:r, h, :], start=True, stop=True)
                        ins.then_inc(ev["dS"], 1)
                    else:
                        ev.done(pe, "S", v)
                        for b in range(NB):
                            if b:
                                pe.wait_ge(batch_S, b)
                            for h in range(H):
                                ins = mm(s_b[:, h * DK:(h + 1) * DK], kws[:, b, h, :], vn[:r, h, :], start=True, stop=True)
                            ins.then_inc(batch_dS, 1)

                staged(pe, [None, sums, None, None, norms, products, tokens], level,
                       [residual, None, values, outputs, None, None, None])


LAMBDA_INIT = 0.8 - 0.6
KEEP = 1.0 - LAMBDA_INIT
TURNS = 2 * 2 * H


def attention_inputs(nc, a, proj, k_rows, v_rows, qT, kT, V, G, nlam):
    with Phase(nc, "rope") as ph:
        x = ph.sb("r_x", [P, 4, TURNS, DQ])
        cos, sin = ph.sb("r_cos", [P, NT + 1, ROT]), ph.sb("r_sin", [P, NT + 1, ROT])
        t = ph.sb("r_t", [P, 4, TURNS, ROT])
        th = ph.sb("r_th", [P, 512])
        nw, ident = ph.sb("r_nw", [P, DK]), ph.sb("r_id", [P, P])
        lq, lp, le = ph.sb("r_lq", [P, 4, DQ]), ph.sb("r_lp", [P, 2, DQ]), ph.sb("r_le", [P, 4])
        tq = [ph.ps(f"r_tq{s}", [P, 512]) for s in range(2)]
        tk = [ph.ps(f"r_tk{s}", [P, 512]) for s in range(2)]
        consts_in, rows_in, cached, lam_in, lam_exp, chained = (
            ph.sem(n) for n in ("consts_in", "rows_in", "cached", "lam_in", "lam_exp", "chained"))
        x_in, k_out = [ph.sem(f"x_in{s}") for s in range(4)], [ph.sem(f"k_out{s}") for s in range(4)]
        ev = Events(ph, "turned trans qcopy kcopy th gated")
        with nc.Block() as block:

            @block.sync
            def _(sp):
                for dst, src in ((cos[:], a["cos"]), (sin[:], a["sin"]), (ident[:], a["ident"]),
                                 (nw[:], a["diff_norm"].partition_broadcast(P)),
                                 (lq[:].rearrange("p a b -> p (a b)"), a["lambda_qk"].partition_broadcast(P))):
                    sp.dma_start(dst, src).then_inc(consts_in, 16)
                for dst, c0 in ((V, 1536), (G, 2048)):
                    sp.dma_start(dst[:, 0:NT, :], proj[0:SEQ, c0:c0 + 512].rearrange("(t p) n -> p t n", p=P)).then_inc(rows_in, 16)
                    sp.dma_start(dst[:RS, NT, :], proj[SEQ:ROWS, c0:c0 + 512]).then_inc(rows_in, 16)
                sp.dma_start(v_rows, proj[:, 1536:2048]).then_inc(cached, 16)
                for s in range(4):
                    sp.sem_inc(k_out[s], 16)

                def load(v, s, i, r):
                    ph.hold(sp, ev["trans"], v + 1)
                    ph.hold(sp, k_out[s], i * 16 + 16)
                    sp.dma_start(x[:r, s].rearrange("p a b -> p (a b)"), proj[bass.ds(v * P, r), 512:1536]).then_inc(x_in[s], 16)

                def put(v, s, i, r):
                    ev.done(sp, "turned", v)
                    sp.dma_start(k_rows[bass.ds(v * P, r), :],
                                 x[:r, s, TURNS // 2:, :].rearrange("p a b -> p (a b)")).then_inc(k_out[s], 16)

                loads_and_stores(sp, load, put)
                sp.wait_ge(cached, 16)
                for s in range(4):
                    sp.wait_ge(k_out[s], 16 * (1 + NT // 4 + (s == 0)))

            @block.tensor
            def _(pe):
                pe.sem_inc(ev["trans"], 4)
                pe.wait_ge(consts_in, 80)

                def tile(v, s, i, r=P):
                    ev.done(pe, "turned", v)
                    pe.wait_ge(ev["qcopy"], v + 1)
                    pe.wait_ge(ev["kcopy"], v + 1)
                    for h in range(H):
                        nc.tensor.transpose(tq[s % 2][:, h * P:h * P + r], x[:r, s, 2 * h:2 * h + 2, :].rearrange("p a b -> p (a b)"), ident[:r, :r])
                        ins = nc.tensor.transpose(tk[s % 2][:, h * P:h * P + r],
                                                  x[:r, s, TURNS // 2 + 2 * h:TURNS // 2 + 2 * h + 2, :].rearrange("p a b -> p (a b)"), ident[:r, :r])
                    ins.then_inc(ev["trans"], 1)

                turns_of(pe, NT, 4, tile)
                tile(NT, 0, NT // 4, RS)

            @block.scalar
            def _(act):
                act.sem_inc(ev["qcopy"], 2)
                act.sem_inc(ev["th"], 1)
                act.wait_ge(lam_in, 1)
                nc.scalar.activation(le[:, 2:4], le[:, 0:2], ACT.Exp).then_inc(lam_exp, 1)
                act.wait_ge(rows_in, 64)

                def tile(v, s, i, r=P):
                    ev.prev(act, "gated", v)
                    nc.scalar.activation(th[:r], G[:r, bass.ds(v, 1), :].rearrange("p o n -> p (o n)"), ACT.Tanh,
                                         scale=0.5).then_inc(ev["th"], 1)
                    act.wait_ge(ev["trans"], v + 5)
                    nc.scalar.activation(qT[:, :, bass.ds(v * P, r)], tq[s % 2][:].rearrange("p (h r) -> p h r", h=H)[:, :, :r],
                                         ACT.Copy, scale=DQ ** -0.5).then_inc(ev["qcopy"], 1)

                turns_of(act, NT, 4, tile)
                tile(NT, 0, NT // 4, RS)

            @block.vector
            def _(dve):
                dve.sem_inc(ev["kcopy"], 2)
                ev.open(dve, "turned gated")
                dve.wait_ge(consts_in, 80)
                dve.wait_ge(rows_in, 64)
                chain = Chain(dve, chained)
                lqv = lq[:].rearrange("p (a two) b -> p a two b", two=2)
                chain.link(nc.vector.tensor_tensor(lp[:], lqv[:, :, 0, :], lqv[:, :, 1, :], ALU.mult))
                nc.vector.tensor_reduce(le[:, 0:2], lp[:], AX.X, ALU.add).then_inc(lam_in, 1)
                dve.wait_ge(lam_exp, 1)
                chain.link(nc.vector.tensor_tensor(nlam[:], le[:, 3:4], le[:, 2:3], ALU.subtract))
                chain.link(nc.vector.tensor_scalar(nlam[:], nlam[:], LAMBDA_INIT, None, ALU.subtract))
                first = chain.n
                PER = 3

                def tile(v, s, i, r=P):
                    chain.turn(v * PER + first)
                    dve.wait_ge(x_in[s], i * 16 + 16)
                    cs, sn = (repeat(m[:r, bass.ds(v, 1), :].rearrange("p o f -> p (o f)"), TURNS) for m in (cos, sin))
                    lead, trail = x[:r, s, :, 0:ROT], x[:r, s, :, ROT:2 * ROT]
                    for n, (u, w) in enumerate(((lead, cs), (trail, sn), (trail, cs), (lead, sn))):
                        ins = nc.vector.tensor_tensor(t[:r, n], u, w, ALU.mult)
                    chain.link(ins)
                    nc.vector.tensor_tensor(lead, t[:r, 0], t[:r, 1], ALU.subtract)
                    nc.vector.tensor_tensor(trail, t[:r, 2], t[:r, 3], ALU.add).then_inc(ev["turned"], 1)
                    ev.done(dve, "th", v)
                    g = G[:r, bass.ds(v, 1), :].rearrange("p o n -> p (o n)")
                    gh = G[:r, bass.ds(v, 1), :].rearrange("p o (h n) -> p (o h) n", h=H)
                    chain.link(nc.vector.scalar_tensor_tensor(g, th[:r], 1.0, g, ALU.add, ALU.mult))
                    chain.link(nc.vector.scalar_tensor_tensor(gh, gh, 0.5 * KEEP, repeat(nw[:r], H), ALU.mult, ALU.mult))
                    dve.sem_inc(ev["gated"], 1)
                    dve.wait_ge(ev["trans"], v + 5)
                    nc.vector.tensor_copy(kT[:, :, bass.ds(v * P, r)], tk[s % 2][:].rearrange("p (h r) -> p h r", h=H)[:, :, :r]).then_inc(ev["kcopy"], 1)
                    assert chain.n == PER

                turns_of(dve, NT, 4, tile)
                tile(NT, 0, NT // 4, RS)


def prompt_attention(nc, a, merged, qT, kT, V, G, nlam):
    SB = 4
    width = [(qi + 1) * P for qi in range(NT)]
    banks = [-(-w // 512) for w in width]
    first_s = [2 * sum(banks[:qi]) for qi in range(NT)]
    first_a = [sum(banks[:qi]) for qi in range(NT)]
    PS, PA = 2 * sum(banks), sum(banks)
    assert PS % SB == 0 and PA % 2 == 0
    with Phase(nc, "attn") as ph:
        qz = ph.sb("t_qz", [P, 2, 2, P])
        p = ph.sb("t_p", [P, 2, 2, SEQ])
        aT = ph.sb("t_aT", [P, 2, 4, P])
        mx, nm = ph.sb("t_mx", [P, 2, 2, 4]), ph.sb("t_nm", [P, 2, 2])
        ls, lr = ph.sb("t_ls", [P, 2, 2, 4]), ph.sb("t_lr", [P, 2, 4])
        oss, rr = ph.sb("t_oss", [P, 2, 2]), ph.sb("t_rr", [P, 2])
        junk, og = ph.sb("t_junk", [P, 2, DK]), ph.sb("t_og", [P, 2, DK])
        ident, causal, pw = ph.sb("t_id", [P, P]), ph.sb("t_causal", [P, P]), ph.sb("t_pw", [P, 1])
        score = [ph.ps(f"t_s{n}", [P, 512]) for n in range(SB)]
        tps = [ph.ps(f"t_t{n}", [P, 512]) for n in range(2)]
        out = [ph.ps(f"t_o{n}", [P, 512]) for n in range(2)]
        consts_in, set_up, chained = ph.sem("consts_in"), ph.sem("set_up"), ph.sem("chained")
        q_set, maxed, weighted, gathered, squared, mean, rstd, gated = (
            ph.sem(n) for n in ("q_set", "maxed", "weighted", "gathered", "squared", "mean", "rstd", "gated"))
        q_half = ph.sem("q_half")
        scored, expd, turned, copied = (ph.sem(n) for n in ("scored", "expd", "turned", "copied"))
        stored = [ph.sem("stored0"), ph.sem("stored1")]
        PER = NT * (2 * 2 + 3 + 2)

        early = lambda qi: range(0, (banks[qi] + 1) // 2)
        late = lambda qi: range((banks[qi] + 1) // 2, banks[qi])

        def heads(eng, body):
            with eng.Fori(0, H) as h:
                body(h)

        with nc.Block() as block:

            @block.sync
            def _(sp):
                sp.dma_start(ident[:], a["ident"]).then_inc(consts_in, 16)
                sp.dma_start(causal[:], a["causal"]).then_inc(consts_in, 16)
                for s in range(2):
                    sp.sem_inc(stored[s], 16)

                def head(h):
                    for qi in range(NT):
                        ph.hold(sp, gated, h * NT + qi + 1)
                        sp.dma_start(merged[qi * P:(qi + 1) * P, bass.ds(h * DK + 512, DK)], og[:, qi % 2, :]).then_inc(stored[qi % 2], 16)

                heads(sp, head)
                for s in range(2):
                    sp.wait_ge(stored[s], 16 * (1 + H * NT // 2))

            @block.gpsimd
            def _(pool):
                nc.gpsimd.memset(pw[:], -0.5).then_inc(set_up, 1)
                nc.gpsimd.memset(qz[:], 0.0).then_inc(set_up, 1)
                pool.wait_ge(set_up, 2)

                def head(h):
                    def query(qi):
                        before = first_s[qi - 1] if qi >= 2 else [first_s[NT - 1], PS][qi] - PS
                        ph.hold(pool, scored, h * PS + before + PS)
                        nc.gpsimd.tensor_copy(qz[0:DQ, qi % 2, 0, :], qT[0:DQ, bass.ds(h, 1), qi * P:(qi + 1) * P].rearrange("p o r -> p (o r)")).then_inc(q_half, 1)
                        ph.hold(pool, q_half, h * NT + qi + 1)
                        nc.gpsimd.tensor_copy(qz[DQ:P, qi % 2, 1, :], qT[DQ:P, bass.ds(h, 1), qi * P:(qi + 1) * P].rearrange("p o r -> p (o r)")).then_inc(q_set, 1)
                        ph.hold(pool, q_set, h * NT + qi + 1)

                    def root(qi):
                        ph.hold(pool, mean, h * NT + qi + 1)
                        nc.gpsimd.tensor_tensor(rr[:, qi % 2:qi % 2 + 1], oss[:, qi % 2, 1:2], pw[:], ALU.pow).then_inc(rstd, 1)
                        ph.hold(pool, rstd, h * NT + qi + 1)

                    query(0)
                    query(1)
                    for qi in range(NT):
                        if qi + 2 < NT:
                            query(qi + 2)
                        if qi:
                            root(qi - 1)
                    root(NT - 1)

                heads(pool, head)

            @block.scalar
            def _(act):
                act.sem_inc(expd, SB)
                act.sem_inc(copied, 2)

                def head(h):
                    def exps(qi, m):
                        s = qi % 2
                        act.wait_ge(maxed, (h * NT + qi) * 2 + m + 1)
                        if qi >= 2 and m == 0:
                            act.wait_ge(turned, h * PA + first_a[qi - 1])
                        for b in range(banks[qi]):
                            k = first_s[qi] + m * banks[qi] + b
                            w = min(512, width[qi] - b * 512)
                            nc.scalar.activation(p[:, s, m, b * 512:b * 512 + w], score[k % SB][:, :w], ACT.Exp,
                                                 bias=nm[:, s, m:m + 1], accum_out=ls[:, s, m, b:b + 1]).then_inc(expd, 1)

                    def copies(qi, groups):
                        for g in groups:
                            k = first_a[qi] + g
                            n = min(4, qi + 1 - 4 * g)
                            act.wait_ge(turned, h * PA + k + 1)
                            act.wait_ge(gathered, h * PA + k + 1)
                            nc.scalar.activation(aT[:, k % 2, :n, :], tps[k % 2][:, :n * P].rearrange("p (n r) -> p n r", n=n),
                                                 ACT.Copy).then_inc(copied, 1)

                    def square(qi):
                        s = qi % 2
                        act.wait_ge(gathered, h * PA + first_a[qi] + banks[qi] + 2)
                        nc.scalar.activation(junk[:, s, :], out[s][:, :DK], ACT.Square, accum_out=oss[:, s, 0:1]).then_inc(squared, 1)

                    exps(0, 0)
                    exps(0, 1)
                    for qi in range(NT):
                        copies(qi, early(qi))
                        if qi:
                            square(qi - 1)
                        if qi + 1 < NT:
                            exps(qi + 1, 0)
                        copies(qi, late(qi))
                        if qi + 1 < NT:
                            exps(qi + 1, 1)
                    square(NT - 1)

                heads(act, head)

            @block.vector
            def _(dve):
                dve.wait_ge(consts_in, 32)
                chain = Chain(dve, chained)

                def head(h):
                    chain.turn(h * PER)

                    def maxima(qi, m):
                        s = qi % 2
                        for b in range(banks[qi]):
                            k = first_s[qi] + m * banks[qi] + b
                            w = min(512, width[qi] - b * 512)
                            dve.wait_ge(scored, h * PS + k + 1 + PS)
                            if b == banks[qi] - 1:
                                chain.link(nc.vector.tensor_tensor(score[k % SB][:, w - P:w], score[k % SB][:, w - P:w], causal[:], ALU.add))
                            ins = nc.vector.tensor_reduce(mx[:, s, m, b:b + 1], score[k % SB][:, :w], AX.X, ALU.max)
                        chain.link(ins)
                        nc.vector.tensor_reduce(nm[:, s, m:m + 1], mx[:, s, m, :banks[qi]], AX.X, ALU.max,
                                                negate=True).then_inc(maxed, 1)

                    def weights(qi):
                        s, w, n = qi % 2, width[qi], banks[qi]
                        dve.wait_ge(expd, h * PS + first_s[qi] + 2 * n + SB)
                        chain.link(nc.vector.tensor_reduce(lr[:, s, 0:2], ls[:, s, :, :n], AX.X, ALU.add))
                        chain.link(nc.vector.reciprocal(lr[:, s, 2:4], lr[:, s, 0:2]))
                        chain.link(nc.vector.tensor_scalar(lr[:, s, 3:4], lr[:, s, 3:4], nlam[:], lr[:, s, 0:1], ALU.mult, ALU.mult))
                        for b in range(n):
                            c = slice(b * 512, min(w, b * 512 + 512))
                            nc.vector.scalar_tensor_tensor(p[:, s, 0, c], p[:, s, 1, c], lr[:, s, 3:4], p[:, s, 0, c],
                                                           ALU.mult, ALU.add).then_inc(weighted, 1)

                    def square_mean(qi):
                        s = qi % 2
                        dve.wait_ge(squared, h * NT + qi + 1)
                        chain.link(nc.vector.tensor_scalar(oss[:, s, 0:1], oss[:, s, 0:1], lr[:, s, 2:3], lr[:, s, 2:3], ALU.mult, ALU.mult))
                        nc.vector.tensor_scalar(oss[:, s, 1:2], oss[:, s, 0:1], 1.0 / DK, EPS, ALU.mult, ALU.add).then_inc(mean, 1)

                    def gate(qi):
                        s = qi % 2
                        dve.wait_ge(rstd, h * NT + qi + 1)
                        chain.link(nc.vector.tensor_scalar(lr[:, s, 2:3], lr[:, s, 2:3], rr[:, s:s + 1], None, ALU.mult))
                        dve.wait_ge(stored[s], (h * (NT // 2) + qi // 2) * 16 + 16)
                        nc.vector.scalar_tensor_tensor(og[:, s, :], out[s][:, :DK], lr[:, s, 2:3],
                                                       G[:, qi, bass.ds(h * DK, DK)], ALU.mult, ALU.mult).then_inc(gated, 1)

                    maxima(0, 0)
                    maxima(0, 1)
                    weights(0)
                    for qi in range(NT):
                        if qi + 1 < NT:
                            maxima(qi + 1, 0)
                        if qi:
                            square_mean(qi - 1)
                        if qi + 1 < NT:
                            maxima(qi + 1, 1)
                        if qi:
                            gate(qi - 1)
                        if qi + 1 < NT:
                            weights(qi + 1)
                    square_mean(NT - 1)
                    gate(NT - 1)
                    assert chain.n == PER

                heads(dve, head)

            @block.tensor
            def _(pe):
                pe.sem_inc(scored, PS)
                pe.sem_inc(gathered, 2)
                pe.wait_ge(consts_in, 32)

                def head(h):
                    def scores(qi, m):
                        if m == 0:
                            pe.wait_ge(q_set, h * NT + qi + 1)
                        for b in range(banks[qi]):
                            k = first_s[qi] + m * banks[qi] + b
                            w = min(512, width[qi] - b * 512)
                            pe.wait_ge(expd, h * PS + k + 1)
                            nc.tensor.matmul(score[k % SB][:, :w], qz[:, qi % 2, m, :],
                                             kT[:, bass.ds(h, 1), b * 512:b * 512 + w].rearrange("p o r -> p (o r)"),
                                             start=True, stop=True).then_inc(scored, 1)

                    def turn(qi, g):
                        k = first_a[qi] + g
                        pe.wait_ge(weighted, h * PA + k + 1)
                        pe.wait_ge(copied, h * PA + k + 1)
                        for t in range(4 * g, min(4 * g + 4, qi + 1)):
                            ins = nc.tensor.transpose(tps[k % 2][:, (t % 4) * P:(t % 4 + 1) * P], p[:, qi % 2, 0, t * P:(t + 1) * P], ident[:])
                        ins.then_inc(turned, 1)

                    def gather(qi, g):
                        k = first_a[qi] + g
                        pe.wait_ge(copied, h * PA + k + 3)
                        if g == 0 and qi >= 2:
                            pe.wait_ge(gated, h * NT + qi - 1)
                        for t in range(4 * g, min(4 * g + 4, qi + 1)):
                            ins = nc.tensor.matmul(out[qi % 2][:, :DK], aT[:, k % 2, t % 4, :], V[:, t, bass.ds(h * DK, DK)],
                                                   start=(t == 0), stop=(t == qi))
                        ins.then_inc(gathered, 1)

                    def groups(qi, some):
                        for g in some:
                            if g == 0:
                                turn(qi, 0)
                            if g + 1 < banks[qi]:
                                turn(qi, g + 1)
                            gather(qi, g)

                    scores(0, 0)
                    scores(0, 1)
                    for qi in range(NT):
                        if qi + 1 < NT:
                            scores(qi + 1, 0)
                        groups(qi, early(qi))
                        if qi + 1 < NT:
                            scores(qi + 1, 1)
                        groups(qi, late(qi))

                heads(pe, head)


def sample_attention(nc, a, merged, qT, kT, V, G, nlam):
    GR, PER = 2, NB // 2
    with Phase(nc, "samp") as ph:
        qs = ph.sb("s_qs", [P, PER * H, P])
        kp = ph.sb("s_kp", [P, NPG, 512])
        vp = ph.sb("s_vp", [P, PER, NPG, 512])
        kTp = ph.sb("s_kTp", [P, 2, H, PAST])
        p = ph.sb("s_p", [P, PAST + RS])
        aT = ph.sb("s_aT", [P, NPG + 1, 64])
        oT = ph.sb("s_oT", [P, H, NB, DS])
        mx, st = ph.sb("s_mx", [P, 4]), ph.sb("s_st", [P, 8])
        ident, fold, map2 = ph.sb("s_id", [P, P]), ph.sb("s_fold", [P, 64]), ph.sb("s_map", [P, 2])
        mask, pg, pw = ph.sb("s_mask", [P, GR, RS]), ph.sb("s_pg", [1, NB * NPG], I32), ph.sb("s_pw", [P, 4])
        osq, oss, og = ph.sb("s_osq", [RS, H, DK]), ph.sb("s_oss", [RS, 12]), ph.sb("s_og", [RS, H, DK])
        score, new, aps, ops = (ph.ps("s_" + n, [P, 512]) for n in ("score", "new", "aps", "ops"))
        tps = [ph.ps(f"s_t{n}", [P, 512]) for n in range(2)]
        back = ph.ps("s_back", [P, 512])
        consts_in, pages_in, zeroed, qset, turned, copied, scored, stat, expd, weighted = (
            ph.sem(n) for n in ("consts_in", "pages_in", "zeroed", "qset", "turned", "copied", "scored", "stat", "expd", "weighted"))
        folded, a_copied, gathered, o_copied, returned, squared, mean, rstd, gated, stored, chained = (
            ph.sem(n) for n in ("folded", "a_copied", "gathered", "o_copied", "returned", "squared", "mean", "rstd", "gated", "stored", "chained"))
        k_in = [ph.sem(f"k_in{n}") for n in range(NPG)]
        v_in = [ph.sem(f"v_in{n}") for n in range(PER)]
        with nc.Block() as block:

            @block.sync
            def _(sp):
                sp.dma_start(pg[:], a["pages"]).then_inc(pages_in, 16)
                for dst, src in ((ident, "ident"), (fold, "fold"), (map2, "map2"), (mask, "new_mask")):
                    sp.dma_start(dst[:], a[src]).then_inc(consts_in, 16)
                sp.wait_ge(pages_in, 16)

                def rows(u):
                    page = sp.value_load(pg[0:1, u:u + 1], min_val=0, max_val=a["cache_k"].shape[0] // PAGE - 1)
                    return bass.ds(page * PAGE, PAGE)

                def keys(b, n):
                    if b:
                        sp.wait_ge(turned, (b - 1) * NPG + n + 1)
                    sp.dma_start(kp[:, n, :], a["cache_k"][rows(b * NPG + n), :]).then_inc(k_in[n], 16)

                def values(b, n):
                    sp.dma_start(vp[:, b % PER, n, :], a["cache_v"][rows(b * NPG + n), :]).then_inc(v_in[b % PER], 16)

                for b in range(PER):
                    for n in range(NPG):
                        keys(b, n)
                        values(b, n)
                for b in range(PER, NB):
                    for n in range(NPG):
                        keys(b, n)
                sp.wait_ge(gathered, 1)
                for b in range(PER, NB):
                    for n in range(NPG):
                        values(b, n)
                sp.wait_ge(gated, 1)
                sp.dma_start(merged[SEQ:ROWS, 512:1024], og[:].rearrange("p h d -> p (h d)")).then_inc(stored, 16)
                sp.wait_ge(stored, 16)

            @block.gpsimd
            def _(pool):
                nc.gpsimd.memset(pw[:], -0.5).then_inc(zeroed, 1)
                nc.gpsimd.memset(qs[:], 0.0).then_inc(zeroed, 1)
                pool.wait_ge(zeroed, 2)
                for g in range(GR):
                    if g:
                        pool.wait_ge(scored, 1)
                    for m in range(2):
                        if m or g:
                            pool.wait_ge(qset, 2 * g + m)
                        for b in range(PER):
                            for h in range(H):
                                col, tok = b * 32 + h * 8 + m * 4, SEQ + (g * PER + b) * DS
                                ins = nc.gpsimd.tensor_copy(qs[m * DQ:(m + 1) * DQ, b * H + h, col:col + DS],
                                                            qT[m * DQ:(m + 1) * DQ, h, tok:tok + DS])
                        ins.then_inc(qset, 1)
                pool.wait_ge(qset, 2 * GR)
                pool.wait_ge(mean, 1)
                nc.gpsimd.tensor_tensor(oss[:, 8:12], oss[:, 4:8], pw[:RS], ALU.pow).then_inc(rstd, 1)

            @block.scalar
            def _(act):
                def keys(b):
                    for n in range(NPG):
                        u = b * NPG + n
                        act.wait_ge(turned, u + 1)
                        nc.scalar.activation(kTp[:, b % 2, :, n * PAGE:(n + 1) * PAGE],
                                             tps[u % 2][:].rearrange("p (h r) -> p h r", h=H), ACT.Copy).then_inc(copied, 1)

                keys(0)
                for g in range(GR):
                    for b in range(g * PER + 1, min((g + 1) * PER + 1, NB)):
                        keys(b)
                    act.wait_ge(stat, g + 1)
                    nc.scalar.activation(p[:, :PAST], score[:], ACT.Exp, bias=mx[:, 3:4], accum_out=st[:, 0:1])
                    nc.scalar.activation(p[:, PAST:], new[:, :RS], ACT.Exp, bias=mx[:, 3:4], accum_out=st[:, 1:2]).then_inc(expd, 1)
                act.wait_ge(returned, 1)
                nc.scalar.activation(osq[:], back[:RS].rearrange("p (h d) -> p h d", h=H), ACT.Square).then_inc(squared, 1)

            @block.vector
            def _(dve):
                chain = Chain(dve, chained)
                dve.wait_ge(consts_in, 64)
                chain.link(nc.vector.scalar_tensor_tensor(st[:, 4:5], map2[:, 1:2], nlam[:], map2[:, 0:1], ALU.mult, ALU.add))
                for g in range(GR):
                    dve.wait_ge(scored, g + 1)
                    chain.link(nc.vector.tensor_tensor(new[:, :RS], new[:, :RS], mask[:, g, :], ALU.add))
                    nc.vector.tensor_reduce(mx[:, 0:1], score[:], AX.X, ALU.max)
                    chain.link(nc.vector.tensor_reduce(mx[:, 1:2], new[:, :RS], AX.X, ALU.max))
                    nc.vector.tensor_reduce(mx[:, 3:4], mx[:, 0:2], AX.X, ALU.max, negate=True).then_inc(stat, 1)
                    dve.wait_ge(expd, g + 1)
                    chain.link(nc.vector.tensor_tensor(st[:, 2:3], st[:, 0:1], st[:, 1:2], ALU.add))
                    chain.link(nc.vector.reciprocal(st[:, 3:4], st[:, 2:3]))
                    nc.vector.tensor_scalar(p[:], p[:], st[:, 3:4], st[:, 4:5], ALU.mult, ALU.mult).then_inc(weighted, 1)
                    dve.wait_ge(folded, g + 1)
                    nc.vector.tensor_copy(aT[:, 0:NPG, :], aps[:, 0:NPG * 64].rearrange("p (n r) -> p n r", n=NPG))
                    nc.vector.tensor_copy(aT[:RS, NPG, :], aps[:RS, NPG * 64:(NPG + 1) * 64]).then_inc(a_copied, 1)
                    dve.wait_ge(gathered, g + 1)
                    nc.vector.tensor_copy(oT[:, :, g * PER:(g + 1) * PER, :],
                                          ops[:, 0:64].rearrange("p (b h q) -> p h b q", b=PER, h=H)).then_inc(o_copied, 1)
                dve.wait_ge(squared, 1)
                chain.link(nc.vector.tensor_reduce(oss[:, 0:4], osq[:], AX.X, ALU.add))
                nc.vector.tensor_scalar(oss[:, 4:8], oss[:, 0:4], 1.0 / DK, EPS, ALU.mult, ALU.add).then_inc(mean, 1)
                dve.wait_ge(rstd, 1)
                chain.link(nc.vector.tensor_tensor(og[:], back[:RS].rearrange("p (h d) -> p h d", h=H), spread(oss[:, 8:12], DK), ALU.mult))
                nc.vector.tensor_tensor(og[:], og[:], G[:RS, NT, :].rearrange("p (h d) -> p h d", h=H), ALU.mult).then_inc(gated, 1)

            @block.tensor
            def _(pe):
                pe.wait_ge(consts_in, 64)
                mm = nc.tensor.matmul

                def keys(b):
                    for n in range(NPG):
                        u = b * NPG + n
                        pe.wait_ge(k_in[n], 16 * (b + 1))
                        if u >= 2:
                            pe.wait_ge(copied, u - 1)
                        for h in range(H):
                            ins = nc.tensor.transpose(tps[u % 2][:, h * P:(h + 1) * P], kp[:, n, h * P:(h + 1) * P], ident[:])
                        ins.then_inc(turned, 1)

                keys(0)
                for g in range(GR):
                    pe.wait_ge(qset, 2 * (g + 1))
                    if g:
                        pe.wait_ge(expd, g)
                    for b in range(PER):
                        if g * PER + b + 1 < NB:
                            keys(g * PER + b + 1)
                        pe.wait_ge(copied, (g * PER + b + 1) * NPG)
                        for h in range(H):
                            edge = dict(start=(b == 0 and h == 0), stop=(b == PER - 1 and h == H - 1))
                            mm(score[:], qs[:, b * H + h, :], kTp[:, b % 2, h, :], **edge)
                            ins = mm(new[:, :RS], qs[:, b * H + h, :], kT[:, h, SEQ:ROWS], **edge)
                    ins.then_inc(scored, 1)
                    pe.wait_ge(weighted, g + 1)
                    if g:
                        pe.wait_ge(a_copied, g)
                    for n in range(NPG + 1):
                        w = PAGE if n < NPG else RS
                        ins = mm(aps[:w, n * 64:(n + 1) * 64], p[:, n * PAGE:n * PAGE + w], fold[:], start=True, stop=True)
                    ins.then_inc(folded, 1)
                    pe.wait_ge(a_copied, g + 1)
                    if g:
                        pe.wait_ge(o_copied, g)
                    for b in range(PER):
                        pe.wait_ge(v_in[b], 16 * NPG * (g + 1))
                        for h in range(H):
                            c0 = (b * H + h) * DS
                            for n in range(NPG):
                                mm(ops[:, c0:c0 + DS], vp[:, b, n, h * DK:(h + 1) * DK], aT[:, n, c0:c0 + DS], start=(n == 0), stop=False)
                            ins = mm(ops[:, c0:c0 + DS], V[:RS, NT, h * DK:(h + 1) * DK], aT[:RS, NPG, c0:c0 + DS], start=False, stop=True)
                    ins.then_inc(gathered, 1)
                pe.wait_ge(o_copied, GR)
                for h in range(H):
                    ins = nc.tensor.transpose(back[:RS, h * DK:(h + 1) * DK], oT[:, h].rearrange("p b q -> p (b q)"), ident[:])
                ins.then_inc(returned, 1)


def mlstm(nc, a, proj, gates, merged, c_out_p, c_out_s, m_out_p, m_out_s):
    W = DV + 1
    with Phase(nc, "mls") as ph:
        sb, ps = ph.sb, ph.ps
        ident, ones, upper = sb("m_id", [P, P]), sb("m_ones", [P, P]), sb("m_up", [P, P])
        last, causal = sb("m_last", [P, P]), sb("m_causal", [P, P])
        upper_s, last_s, causal_s = sb("m_ups", [RS, RS]), sb("m_lasts", [RS, RS]), sb("m_causals", [RS, RS])
        member, own = sb("m_mem", [RS, NB]), sb("m_own", [P, NB, RS])
        nw, pw = sb("m_nw", [P, DV]), sb("m_pw", [P, 4])
        x = sb("m_x", [P, 2, 3072])
        va = sb("m_va", [P, 2, H, W])
        gt, sm, c = sb("m_gt", [P, 8]), sb("m_sm", [P, 4]), sb("m_c", [P, 4])
        M, args, exps = sb("m_M", [P, 4]), sb("m_args", [P, 3, 4]), sb("m_exps", [P, 2, 3, 4])
        mrows, mprev, mprev_s = sb("m_mrows", [P, 4]), sb("m_mprev", [P, 4]), sb("m_mprevs", [RS, 4])
        dgc, dgM, dgs = (sb("m_" + n, [P, H, P]) for n in ("dgc", "dgM", "dgs"))
        cm, wt, qk = sb("m_cm", [P, H, P]), sb("m_wt", [P, H, P]), sb("m_qk", [P, 8, P])
        pt, qg, kw = sb("m_pt", [P, 2, H, P]), sb("m_qg", [P, 2, H, P]), sb("m_kw", [P, 2, H, DK])
        dec = sb("m_dec", [P, 2, H, NB])
        dn, rd = sb("m_dn", [P, 4]), sb("m_rd", [P, 4])
        to, tz = sb("m_to", [P, 2, H, DV]), sb("m_tz", [P, 2, H, DV])
        ho, og = sb("m_ho", [P, H, DV]), sb("m_og", [P, H, DV])
        junk, ss, rr = sb("m_junk", [P, H, DV]), sb("m_ss", [P, 8]), sb("m_rr", [P, 4])
        C, Cs = sb("m_C", [P, H, 1, W]), sb("m_Cs", [P, H, NB, W])
        qgs, kws = sb("m_qgs", [P, H, NB, RS]), sb("m_kws", [RS, NB, H, DK])
        small_b, row_b, q_b, k_b = (ps("m_" + n, [P, 512]) for n in ("small", "row", "qb", "kb"))
        head_b = [ps(f"m_head{h}", [P, 512]) for h in range(H)]

        consts_in, set_up, stored, chained, chained_p, batch_dC, batch_C, mcopied = (
            ph.sem(n) for n in ("consts_in", "set_up", "stored", "chained", "chained_p", "batch_dC", "batch_C", "mcopied"))
        x_in, va_in = [ph.sem("x_in0"), ph.sem("x_in1")], [ph.sem("va_in0"), ph.sem("va_in1")]
        ev = Events(ph, "gate small c dgc crow M sc dgM dgs mrow scrow wta wt qkt qkc kq qg pt kw num dC C "
                        "tz to so zs ho sq ms rr og", first=2)
        NC = 14
        PROMPT, SAMPLE = (P, 1, upper, last, causal, C, mprev), (RS, NB, upper_s, last_s, causal_s, Cs, mprev_s)

        def interleaved(eng, front, back, base=None):
            def step(v, s, i, kind, s1, i1, kind1):
                ahead, behind = (v + 1, s1, i1, *kind1), (v, s, i, *kind)
                for piece, tile in ((front[0], ahead), (front[1], ahead), (back[0], behind), (front[2], ahead),
                                    (back[1], behind), (front[3], ahead), (back[2], behind), (back[3], behind)):
                    if piece:
                        piece(*tile)

            for f in front:
                if f:
                    f(0, 0, 0, *PROMPT)
            base and base(None)
            with eng.Fori(0, NT // 2 - 1) as i:
                base and base(i)
                step(i * 2, 0, i, PROMPT, 1, i, PROMPT)
                step(i * 2 + 1, 1, i, PROMPT, 0, i + 1, PROMPT)
            base and base(NT // 2 - 1)
            i = NT // 2 - 1
            step(NT - 2, 0, i, PROMPT, 1, i, PROMPT)
            step(NT - 1, 1, i, PROMPT, 0, i + 1, SAMPLE)
            for b in back:
                if b:
                    b(NT, 0, i + 1, *SAMPLE)

        def heads(b, r, rows=None):
            return b[:(rows or P), :H * r].rearrange("p (h r) -> p h r", h=H)

        with nc.Block() as block:

            @block.sync
            def _(sp):
                loads = [(ident[:], a["ident"]), (ones[:], a["same"]), (upper[:], a["upper"]), (last[:], a["last"]),
                         (causal[:], a["causal"]), (upper_s[:], a["upper_s"]), (last_s[:], a["last_s"]),
                         (causal_s[:], a["causal_s"]), (member[:], a["member"]), (own[:], a["own"].partition_broadcast(P)),
                         (nw[:], a["mlstm_norm"].partition_broadcast(P)), (Cs[:], a["c_state"]), (mprev_s[:], a["m_state"])]
                assert len(loads) == NC - 1
                for dst, src in loads:
                    sp.dma_start(dst, src).then_inc(consts_in, 16)
                sp.sem_inc(stored, 16)

                def load(v, s, r=P):
                    ev.ago(sp, "qkt", v, 2)
                    ev.ago(sp, "kw", v, 2)
                    rows = bass.ds(v * P, r)
                    sp.dma_start(x[:r, s, 0:1024], proj[rows, 0:1024]).then_inc(x_in[s], 16)
                    sp.dma_start(x[:r, s, 1024:3072], proj[rows, 2048:4096]).then_inc(x_in[s], 16)

                def values(v, s, r=P):
                    ev.ago(sp, "dC", v, 2)
                    sp.dma_start(va[:r, s, :, 0:DV], proj[bass.ds(v * P, r), 1024:2048].rearrange("p (h d) -> p h d", h=H)).then_inc(va_in[s], 16)

                def put(v, r=P):
                    ev.done(sp, "og", v)
                    sp.dma_start(merged[bass.ds(v * P, r), :], og[:r].rearrange("p h d -> p (h d)")).then_inc(stored, 16)

                load(0, 0)
                load(1, 1)
                values(0, 0)
                with sp.Fori(0, NT // 2 - 1) as i:
                    for s in range(2):
                        v = i * 2 + (2 + s)
                        load(v, s)
                        values(v - 1, 1 - s)
                        put(v - 2)
                load(NT, 0, RS)
                values(NT - 1, 1)
                put(NT - 2)
                values(NT, 0, RS)
                put(NT - 1)
                put(NT, RS)
                ev.done(sp, "C", NT - 1)
                sp.dma_start(c_out_p, C[:, :, 0, :]).then_inc(stored, 16)
                sp.dma_start(m_out_p, mprev[0:1, :]).then_inc(stored, 16)
                ev.done(sp, "M", NT)
                sp.dma_start(m_out_s, mrows[:RS, :]).then_inc(stored, 16)
                sp.wait_ge(batch_C, NB)
                sp.dma_start(c_out_s, Cs[:]).then_inc(stored, 16)
                sp.wait_ge(stored, 16 * (NT + 6))

            @block.gpsimd
            def _(pool):
                ev.open(pool, "kw so zs rr")
                nc.gpsimd.memset(pw[:], -0.5).then_inc(set_up, 1)
                nc.gpsimd.memset(C[:], 0.0).then_inc(set_up, 1)
                nc.gpsimd.memset(mprev[:], 0.0).then_inc(set_up, 1)
                nc.gpsimd.memset(va[:, :, :, DV:W], 1.0).then_inc(set_up, 1)
                pool.wait_ge(set_up, 4)
                pool.wait_ge(consts_in, 16 * (NC - 1))
                chain = Chain(pool, chained_p)

                def gate(v, s, i, r, *_):
                    xz = x[:r, s, 1024:2048].rearrange("p (h d) -> p h d", h=H)
                    ev.done(pool, "to", v)
                    nc.gpsimd.tensor_scalar(to[:r, s], to[:r, s], 1.0, 0.5, ALU.add, ALU.mult).then_inc(ev["so"], 1)
                    ev.done(pool, "tz", v)
                    chain.link(nc.gpsimd.tensor_scalar(tz[:r, s], tz[:r, s], 1.0, 0.5, ALU.add, ALU.mult))
                    chain.link(nc.gpsimd.tensor_tensor(tz[:r, s], tz[:r, s], xz, ALU.mult))
                    nc.gpsimd.tensor_tensor(tz[:r, s], tz[:r, s], repeat(nw[:r], H), ALU.mult).then_inc(ev["zs"], 1)

                def keys(v, s, i, r, *_):
                    ev.done(pool, "wt", v)
                    ev.ago(pool, "dC", v, 2)
                    nc.gpsimd.tensor_tensor(kw[:r, s], x[:r, s, 512:1024].rearrange("p (h d) -> p h d", h=H),
                                            spread(exps[:r, s, 2, :], DK), ALU.mult).then_inc(ev["kw"], 1)

                def root(v, s, i, r, *_):
                    ev.done(pool, "ms", v)
                    nc.gpsimd.tensor_tensor(rr[:r], ss[:r, 4:8], pw[:r], ALU.pow).then_inc(ev["rr"], 1)

                def base(i):
                    if i is None:
                        base.first = chain.n
                    else:
                        chain.turn(i * 4 + base.first)

                interleaved(pool, [gate, None, None, keys], [None, root, None, None], base)

            @block.scalar
            def _(act):
                ev.open(act, "qkc sc wt to tz sq")

                def turned(v, s, i, r, *_):
                    ev.done(act, "qkt", v)
                    ev.ago(act, "qg", v, 1)
                    ev.ago(act, "kq", v, 1)
                    nc.scalar.activation(qk[:, 0:4, :r], heads(q_b, r), ACT.Copy, scale=DK ** -0.5)
                    nc.scalar.activation(qk[:, 4:8, :r], heads(k_b, r), ACT.Copy).then_inc(ev["qkc"], 1)

                def gate_tanhs(v, s, i, r, *_):
                    act.wait_ge(x_in[s], i * 32 + 32)
                    ev.ago(act, "og", v, 2)
                    nc.scalar.activation(to[:r, s], x[:r, s, 2048:3072].rearrange("p (h d) -> p h d", h=H), ACT.Tanh, scale=0.5).then_inc(ev["to"], 1)
                    nc.scalar.activation(tz[:r, s], x[:r, s, 1024:2048].rearrange("p (h d) -> p h d", h=H), ACT.Tanh, scale=0.5).then_inc(ev["tz"], 1)

                def shares(v, s, i, r, *_):
                    ev.done(act, "M", v)
                    ev.ago(act, "ho", v, 2)
                    nc.scalar.activation(exps[:r, s, 0:2, :], args[:r, 0:2, :], ACT.Exp).then_inc(ev["sc"], 1)

                def weights(v, s, i, r, *_):
                    ev.done(act, "wta", v)
                    ev.ago(act, "kw", v, 2)
                    nc.scalar.activation(exps[:r, s, 2, :], args[:r, 2, :], ACT.Exp)
                    nc.scalar.activation(wt[:r, :, :r], wt[:r, :, :r], ACT.Exp, scale=-1.0).then_inc(ev["wt"], 1)

                def squares(v, s, i, r, *_):
                    ev.done(act, "ho", v)
                    ev.ago(act, "ms", v, 1)
                    for h in range(H):
                        ins = nc.scalar.activation(junk[:r, h, :], ho[:r, h, :], ACT.Square, accum_out=ss[:r, h:h + 1])
                    ins.then_inc(ev["sq"], 1)

                interleaved(act, [turned, shares, gate_tanhs, weights], [None, squares, None, None])

            @block.vector
            def _(dve):
                ev.open(dve, "gate c dgc M dgM dgs wta qg pt C ho ms og")
                dve.wait_ge(consts_in, 16 * (NC - 1))
                dve.wait_ge(set_up, 4)
                chain = Chain(dve, chained)

                def decays(v, s, i, r, *_):
                    ev.ago(dve, "mrow", v, 1)
                    nc.vector.tensor_copy(gt[:r], gates[:r, bass.ds(v, 1), :].rearrange("p o h -> p (o h)")).then_inc(ev["gate"], 1)
                    ev.done(dve, "small", v)
                    nc.vector.tensor_copy(sm[:r], small_b[:r, 0:4])
                    nc.vector.tensor_tensor(c[:r], gt[:r, 4:8], small_b[:r, 0:4], ALU.subtract).then_inc(ev["c"], 1)
                    ev.done(dve, "c", v)
                    nc.vector.tensor_tensor(dgc[:r, :, :r], spread(c[:r], r), repeat(ident[:r, :r], H), ALU.mult).then_inc(ev["dgc"], 1)

                def maxima(v, s, i, r, n, up, la, ca, Ct, mp):
                    ev.done(dve, "crow", v)
                    chain.link(nc.vector.tensor_tensor(cm[:r, :, :r], heads(row_b, r, r), repeat(ca[:r, :r], H), ALU.add))
                    chain.link(nc.vector.tensor_reduce(M[:r], cm[:r, :, :r], AX.X, ALU.max))
                    chain.link(nc.vector.tensor_tensor(M[:r], M[:r], mp[:r], ALU.max))
                    ev.ago(dve, "wt", v, 1)
                    chain.link(nc.vector.tensor_tensor(mrows[:r], sm[:r], M[:r], ALU.add))
                    nc.vector.tensor_tensor(args[:r, 0, :], mp[:r], M[:r], ALU.subtract)
                    nc.vector.tensor_scalar(args[:r, 1, :], mrows[:r], -1.0, None, ALU.mult).then_inc(ev["M"], 1)
                    nc.vector.tensor_tensor(dgM[:r, :, :r], spread(M[:r], r), repeat(ident[:r, :r], H), ALU.mult).then_inc(ev["dgM"], 1)
                    ev.done(dve, "sc", v)
                    nc.vector.tensor_tensor(dgs[:r, :, :r], spread(exps[:r, s, 0, :], r), repeat(ident[:r, :r], H), ALU.mult).then_inc(ev["dgs"], 1)

                def spreads(v, s, i, r, n, up, la, ca, Ct, mp):
                    ev.done(dve, "mrow", v)
                    nc.vector.tensor_tensor(args[:r, 2, :], c[:r], small_b[:r, 8:12], ALU.subtract)
                    for h in range(H):
                        ins = nc.vector.tensor_scalar(wt[:r, h, :r], row_b[:r, h * r:(h + 1) * r], c[:r, h:h + 1], 0.0,
                                                      ALU.subtract, ALU.max)
                    ins.then_inc(ev["wta"], 1)
                    if n == 1:
                        nc.vector.tensor_copy(mp[:], small_b[:, 8:12]).then_inc(mcopied, 1)
                        dve.wait_ge(mcopied, v + 1)
                        nc.vector.tensor_tensor(mp[:], mp[:], small_b[:, 4:8], ALU.add)
                    ev.done(dve, "scrow", v)
                    ev.done(dve, "qkc", v)
                    ev.ago(dve, "num", v, 2)
                    per = r // n
                    nc.vector.tensor_copy(dec[:, s, :, :n], q_b[:, :H * r].rearrange("p (h b t) -> p h b t", h=H, b=n)[:, :, :, per - 1])
                    nc.vector.tensor_tensor(qg[:, s, :, :r], qk[:, 0:4, :r], heads(q_b, r), ALU.mult).then_inc(ev["qg"], 1)

                def products(v, s, i, r, n, up, la, ca, Ct, mp):
                    if n > 1:
                        ev.done(dve, "qg", v)
                        for h in range(H):
                            nc.vector.tensor_tensor(qgs[:, h], repeat(qg[:, s, h, :r], NB), own[:], ALU.mult)
                        ev.done(dve, "kw", v)
                        for b in range(NB):
                            nc.vector.tensor_scalar(kws[:, b], kw[:r, s], member[:, b:b + 1], None, ALU.mult)
                    ev.done(dve, "wt", v)
                    chain.link(nc.vector.tensor_tensor(wt[:r, :, :r], wt[:r, :, :r], repeat(up[:r, :r], H), ALU.mult))
                    ev.done(dve, "kq", v)
                    nc.vector.tensor_tensor(pt[:r, s, :, :r], heads(k_b, r, r), wt[:r, :, :r], ALU.mult).then_inc(ev["pt"], 1)

                def outputs(v, s, i, r, *_):
                    ev.done(dve, "num", v)
                    for h in range(H):
                        ins = nc.vector.tensor_copy(dn[:r, h:h + 1], head_b[h][:r, DV:W])
                    chain.link(ins)
                    chain.link(nc.vector.scalar_tensor_tensor(dn[:r], dn[:r], -1.0, dn[:r], ALU.mult, ALU.max))
                    chain.link(nc.vector.tensor_tensor(dn[:r], dn[:r], exps[:r, s, 1, :], ALU.max))
                    chain.link(nc.vector.reciprocal(rd[:r], dn[:r]))
                    ev.done(dve, "so", v)
                    ev.ago(dve, "sq", v, 1)
                    for h in range(H):
                        ins = nc.vector.scalar_tensor_tensor(ho[:r, h, :], head_b[h][:r, 0:DV], rd[:r, h:h + 1], to[:r, s, h, :],
                                                             ALU.mult, ALU.mult)
                    ins.then_inc(ev["ho"], 1)

                def state(v, s, i, r, n, up, la, ca, Ct, mp):
                    if n == 1:
                        ev.done(dve, "dC", v)
                        for h in range(H):
                            ins = nc.vector.scalar_tensor_tensor(C[:, h, 0, :], C[:, h, 0, :], dec[:, s, h, 0:1],
                                                                 head_b[h][:, :W], ALU.mult, ALU.add)
                        ins.then_inc(ev["C"], 1)
                        average(v, s, i, r)
                        return
                    average(v, s, i, r)
                    for b in range(NB):
                        dve.wait_ge(batch_dC, b + 1)
                        for h in range(H):
                            ins = nc.vector.scalar_tensor_tensor(Cs[:, h, b, :], Cs[:, h, b, :], dec[:, s, h, b:b + 1],
                                                                 head_b[h][:, :W], ALU.mult, ALU.add)
                        ins.then_inc(batch_C, 1)

                def average(v, s, i, r, *_):
                    ev.done(dve, "sq", v)
                    nc.vector.tensor_scalar(ss[:r, 4:8], ss[:r, 0:4], 1.0 / DV, EPS, ALU.mult, ALU.add).then_inc(ev["ms"], 1)

                def gated(v, s, i, r, *_):
                    ev.done(dve, "rr", v)
                    ev.done(dve, "zs", v)
                    dve.wait_ge(stored, v * 16 + 16)
                    for h in range(H):
                        ins = nc.vector.scalar_tensor_tensor(og[:r, h, :], ho[:r, h, :], rr[:r, h:h + 1], tz[:r, s, h, :],
                                                             ALU.mult, ALU.mult)
                    ins.then_inc(ev["og"], 1)

                def base(i):
                    if i is None:
                        base.first = chain.n
                    else:
                        chain.turn(i * (2 * 9) + base.first)

                interleaved(dve, [decays, maxima, spreads, products], [outputs, state, gated, None], base)

            @block.tensor
            def _(pe):
                ev.open(pe, "small crow mrow scrow qkt kq num dC")
                pe.wait_ge(consts_in, 16 * (NC - 1))
                pe.wait_ge(set_up, 4)
                mm = nc.tensor.matmul

                def turns(v, s, i, r, n, up, la, ca, Ct, mp):
                    ev.ago(pe, "qg", v, 1)
                    ev.ago(pe, "pt", v, 1)
                    pe.wait_ge(x_in[s], i * 32 + 32)
                    for h in range(H):
                        nc.tensor.transpose(q_b[:, h * r:(h + 1) * r], x[:r, s, h * P:(h + 1) * P], ident[:r, :r])
                        ins = nc.tensor.transpose(k_b[:, h * r:(h + 1) * r], x[:r, s, 512 + h * P:512 + (h + 1) * P], ident[:r, :r])
                    ins.then_inc(ev["qkt"], 1)
                    ev.done(pe, "gate", v)
                    mm(small_b[:r, 0:4], up[:r, :r], gt[:r, 0:4], start=True, stop=True).then_inc(ev["small"], 1)
                    ev.done(pe, "dgc", v)
                    mm(row_b[:r, :H * r], ones[:r, :r], dgc[:r, :, :r], start=True, stop=True).then_inc(ev["crow"], 1)

                def rows(v, s, i, r, n, up, la, ca, Ct, mp):
                    ev.done(pe, "qkc", v)
                    for h in range(H):
                        ins = mm(k_b[:r, h * r:(h + 1) * r], qk[:, 4 + h, :r], qk[:, h, :r], start=True, stop=True)
                    ins.then_inc(ev["kq"], 1)
                    ev.done(pe, "dgM", v)
                    mm(small_b[:, 4:8], ones[:r, :], gt[:r, 0:4], start=True, stop=True)
                    mm(small_b[:r, 8:12], la[:r, :r], M[:r], start=True, stop=True)
                    mm(row_b[:r, :H * r], ones[:r, :r], dgM[:r, :, :r], start=True, stop=True).then_inc(ev["mrow"], 1)
                    ev.done(pe, "dgs", v)
                    mm(q_b[:, :H * r], ones[:r, :], dgs[:r, :, :r], start=True, stop=True).then_inc(ev["scrow"], 1)

                def numerators(v, s, i, r, n, up, la, ca, Ct, mp):
                    ev.done(pe, "pt", v)
                    pe.wait_ge(va_in[s], i * 16 + 16)
                    ev.ago(pe, "C", v, 1)
                    for h in range(H):
                        for b in range(n):
                            mm(head_b[h][:r, :W], qg[:, s, h, :r] if n == 1 else qgs[:, h, b], Ct[:, h, b, :], start=(b == 0), stop=False)
                        ins = mm(head_b[h][:r, :W], pt[:r, s, h, :r], va[:r, s, h, :], start=False, stop=True)
                    ins.then_inc(ev["num"], 1)

                def updates(v, s, i, r, n, up, la, ca, Ct, mp):
                    ev.done(pe, "kw", v)
                    ev.done(pe, "ho", v)
                    for b in range(n):
                        if b:
                            pe.wait_ge(batch_C, b)
                        for h in range(H):
                            ins = mm(head_b[h][:, :W], kw[:r, s, h, :] if n == 1 else kws[:, b, h, :], va[:r, s, h, :], start=True, stop=True)
                        ins.then_inc(ev["dC"] if n == 1 else batch_dC, 1)

                interleaved(pe, [turns, None, rows, None], [numerators, updates, None, None])


def final_norm(nc, x, norm_d, y):
    N = 4
    with Phase(nc, "fin") as ph:
        xt, out = ph.sb("f_x", [P, N, D]), ph.sb("f_y", [P, N, D])
        junk, nw = ph.sb("f_junk", [P, 2, D]), ph.sb("f_nw", [P, D])
        ms, pw = ph.sb("f_ms", [P, N, 3]), ph.sb("f_pw", [P, 1])
        nw_in, set_up = ph.sem("nw_in"), ph.sem("set_up")
        x_in, stored = [ph.sem(f"x_in{s}") for s in range(N)], [ph.sem(f"stored{s}") for s in range(N)]
        squares, mean, rstd, normed = (ph.sem(n) for n in ("squares", "mean", "rstd", "normed"))
        with nc.Block() as block:

            @block.sync
            def _(sp):
                sp.dma_start(nw[:], norm_d.partition_broadcast(P)).then_inc(nw_in, 16)

                def load(v, s, i, r):
                    ph.hold(sp, normed, v + 1)
                    sp.dma_start(xt[:r, s, :], x[bass.ds(v * P, r), :]).then_inc(x_in[s], 16)

                def put(v, s, i, r):
                    ph.hold(sp, normed, v + N + 1)
                    sp.dma_start(y[bass.ds(v * P, r), :], out[:r, s, :]).then_inc(stored[s], 16)

                loads_and_stores(sp, load, put)
                for s in range(N):
                    sp.wait_ge(stored[s], 16 * (1 + NT // N + (s == 0)))

            @block.scalar
            def _(act):
                for s in range(N):
                    act.sem_inc(stored[s], 16)
                act.sem_inc(squares, 2)

                def tile(v, s, i, r=P):
                    act.wait_ge(x_in[s], i * 16 + 16)
                    act.wait_ge(normed, v + 1)
                    act.wait_ge(squares, v + 1)
                    nc.scalar.activation(junk[:r, s % 2, :], xt[:r, s, :], ACT.Square, accum_out=ms[:r, s, 0:1]).then_inc(squares, 1)

                turns_of(act, NT, N, tile)
                tile(NT, 0, NT // N, RS)

            @block.gpsimd
            def _(pool):
                nc.gpsimd.memset(pw[:], -0.5).then_inc(set_up, 1)
                pool.wait_ge(set_up, 1)

                def tile(v, s, i, r=P):
                    ph.hold(pool, mean, v + 1)
                    nc.gpsimd.tensor_tensor(ms[:r, s, 2:3], ms[:r, s, 1:2], pw[:r], ALU.pow).then_inc(rstd, 1)

                turns_of(pool, NT, N, tile)
                tile(NT, 0, NT // N, RS)

            @block.vector
            def _(dve):
                dve.sem_inc(normed, N)
                dve.wait_ge(nw_in, 16)

                def average(v, s, i, r=P):
                    dve.wait_ge(squares, v + 3)
                    nc.vector.tensor_scalar(ms[:r, s, 1:2], ms[:r, s, 0:1], 1.0 / D, EPS, ALU.mult, ALU.add).then_inc(mean, 1)

                def norm(v, s, i, r=P):
                    dve.wait_ge(rstd, v + 1)
                    dve.wait_ge(stored[s], i * 16 + 16)
                    nc.vector.scalar_tensor_tensor(out[:r, s, :], xt[:r, s, :], ms[:r, s, 2:3], nw[:r], ALU.mult, ALU.mult).then_inc(normed, 1)

                with dve.Fori(0, NT // N) as i:
                    for s in (0, 2):
                        for part in (average, norm):
                            part(i * N + s, s, i)
                            part(i * N + (s + 1), s + 1, i)
                average(NT, 0, NT // N, RS)
                norm(NT, 0, NT // N, RS)
def build(nc, a, o):
    def scratch(name, shape):
        return nc.dram_tensor(name, shape, F32, kind="Internal").ap()

    proj = scratch("proj", [ROWS, 5 * 512])
    conv_t, conv_s = scratch("conv_t", [CT * P, SEQ]), scratch("conv_s", [CT * P, RS])
    merged = scratch("merged", [ROWS, D])
    x1 = scratch("x1", [ROWS, D])
    proj2 = scratch("proj2", [ROWS, 4096])
    merged2 = scratch("merged2", [ROWS, D])
    x2 = scratch("x2", [ROWS, D])
    with ExitStack() as top:
        gates = top.enter_context(nc.sbuf_tensor("gates", [P, NT + 1, 8], F32))

        def resident(tag):
            st = ExitStack()
            hi = st.enter_context(nc.sbuf_tensor(tag + "act_hi", [P, KT, ROWS], F32R))
            lo = st.enter_context(nc.sbuf_tensor(tag + "act_lo", [P, KT, ROWS], F32R))
            return st, hi, lo

        st, hi, lo = resident("a1")
        with st:
            load_activations(nc, "a1", a["x"], hi, lo, a["ident"], a["norm_w"][0])
            project_conv(nc, hi, lo, a["w_conv"], a["conv_w"], a["conv_state"], conv_t, conv_s,
                         o["conv_p"], o["conv_s"])
            project_gates(nc, "e", hi, lo, a["w_gate_e"], a["gate_vec_e"], a["fold16"], gates, "gdn")
            project_rows(nc, "p1", hi, lo, a["w_rows_e"], proj, 5 * 512 // WB)
        gated_delta(nc, a, proj, conv_t, conv_s, gates, merged, o["gdn_p"], o["gdn_s"])
        with ExitStack() as st:
            def kept(name, shape):
                return st.enter_context(nc.sbuf_tensor(name, shape, F32))

            qT, kT = kept("qT", [P, H, ROWS]), kept("kT", [P, H, ROWS])
            V, G, nlam = kept("V", [P, NT + 1, 512]), kept("G", [P, NT + 1, 512]), kept("nlam", [P, 1])
            attention_inputs(nc, a, proj, o["k_rows"], o["v_rows"], qT, kT, V, G, nlam)
            prompt_attention(nc, a, merged, qT, kT, V, G, nlam)
            sample_attention(nc, a, merged, qT, kT, V, G, nlam)
        st, hi, lo = resident("a2")
        with st:
            load_activations(nc, "a2", merged, hi, lo, a["ident"])
            project_rows(nc, "p2", hi, lo, a["w_out_e"], x1, D // WB, residual=a["x"])

        st, hi, lo = resident("a3")
        with st:
            load_activations(nc, "a3", x1, hi, lo, a["ident"], a["norm_w"][1])
            project_gates(nc, "o", hi, lo, a["w_gate_o"], a["gate_vec_o"], a["fold16"], gates, "mlstm")
            project_rows(nc, "p3", hi, lo, a["w_rows_o"], proj2, 4096 // WB)
        mlstm(nc, a, proj2, gates, merged2, o["c_p"], o["c_s"], o["m_p"], o["m_s"])
        st, hi, lo = resident("a4")
        with st:
            load_activations(nc, "a4", merged2, hi, lo, a["ident"])
            project_rows(nc, "p4", hi, lo, a["w_out_o"], x2, D // WB, residual=x1)
        final_norm(nc, x2, a["final_w"], o["y"])


OUTS = {
    "y": (ROWS, D), "k_rows": (ROWS, 512), "v_rows": (ROWS, 512),
    "conv_p": (CT, P, CONV - 1), "conv_s": (CT, P, NB, CONV - 1),
    "gdn_p": (P, H, P), "gdn_s": (P, H, NB, P),
    "c_p": (P, H, DV + 1), "c_s": (P, H, NB, DV + 1), "m_p": (1, H), "m_s": (RS, H),
}


def constants():
    c = {"ident": np.eye(P, dtype=np.float32)}
    i, j = np.arange(P)[None, :], np.arange(P)[:, None]

    def masks(r, per, levels):
        i, j = np.arange(r)[None, :], np.arange(r)[:, None]
        same = i // per == j // per
        upper = ((j <= i) & same).astype(np.float32)
        level = [((i >> l) ^ 1 == j >> l) & (i > j) for l in range(levels)]
        last = (j == i // per * per + per - 1).astype(np.float32)
        return upper, np.stack(level, 1).astype(np.float32), same.astype(np.float32), last

    c["upper"], c["levels"], c["same"], c["last"] = masks(P, P, LEVELS)
    c["upper_s"], c["levels_s"], c["same_s"], c["last_s"] = masks(RS, DS, LEVELS_S)
    c["causal"] = np.where(j >= i, 0.0, NEG).astype(np.float32)
    c["causal_s"] = np.where(c["upper_s"].T > 0, 0.0, NEG).astype(np.float32)
    c["fold16"] = np.tile(np.eye(8, dtype=np.float32), (2, 1))
    member = np.zeros((RS, NB), np.float32)
    member[np.arange(RS), np.arange(RS) // DS] = 1
    c["own"] = np.repeat(member.T[None], 1, 0).reshape(NB, RS).copy()
    c["member"] = member
    row = np.arange(P)
    seq, hd, mp, q = row // 32, row // 8 % 4, row // 4 % 2, row % 4
    fold = np.zeros((P, 64), np.float32)
    fold[row, (seq * 4 + hd) * 4 + q] = 1
    c["fold"] = fold
    c["map2"] = np.stack([1.0 - mp, mp * 1.0], 1).astype(np.float32)
    new = np.arange(RS)
    ok = (new[None, :] // DS == seq[:, None]) & (new[None, :] % DS <= q[:, None])
    ok2 = (new[None, :] // DS == seq[:, None] + 4) & (new[None, :] % DS <= q[:, None])
    c["new_mask"] = np.stack([np.where(ok, 0, NEG), np.where(ok2, 0, NEG)], 1).astype(np.float32)
    inv = np.power(np.float32(500000.0), -np.arange(ROT, dtype=np.float32) / np.float32(ROT)).astype(np.float32)
    pos = np.concatenate([np.arange(SEQ), PAST + np.tile(np.arange(DS), NB)]).astype(np.float32)
    ang = (pos[:, None] * inv[None, :]).astype(np.float32)
    for name, f in (("cos", np.cos), ("sin", np.sin)):
        t = np.zeros(((NT + 1) * P, ROT), np.float32)
        t[:ROWS] = f(ang)
        c[name] = np.ascontiguousarray(t.reshape(NT + 1, P, ROT).transpose(1, 0, 2))
    return c


def laid_out(inputs):
    f = {k: np.asarray(v) for k, v in inputs.items()}
    blocks = lambda w, n: np.ascontiguousarray(
        w.reshape(KT, P, w.shape[1] // n, n).transpose(2, 1, 0, 3).reshape(-1, P, KT * n))
    we, wo = f["w_in_even"][0], f["w_in_odd"][0]
    a = {
        "x": np.concatenate([f["x_prompt"].reshape(SEQ, D), f["x_sample"].reshape(RS, D)]),
        "norm_w": f["norm_w"], "final_w": f["final_norm_w"],
        "w_conv": blocks(we[:, :1536], P),
        "w_rows_e": blocks(np.concatenate([we[:, 1536:2048], we[:, 2056:]], 1), WB),
        "w_gate_e": blocks(we[:, 2048:2056], 8)[0],
        "gate_vec_e": np.concatenate([f["a_log"][0], f["dt_bias"][0]]),
        "w_out_e": blocks(f["w_out_even"][0], WB),
        "w_rows_o": blocks(wo[:, :4096], WB), "w_gate_o": blocks(wo[:, 4096:], 8)[0],
        "gate_vec_o": np.concatenate([f["b_i"][0], f["b_f"][0]]),
        "w_out_o": blocks(f["w_out_odd"][0], WB),
        "conv_w": f["conv_w"][0].reshape(CONV, CT, P).transpose(2, 1, 0).reshape(P, CT * CONV),
        "conv_state": f["state_gdn_conv"][0].reshape(NB, CONV - 1, CT, P).transpose(2, 3, 0, 1),
        "gdn_state": f["state_gdn_s"][0].transpose(2, 1, 0, 3),
        "c_state": np.concatenate([f["state_mlstm_c"][0], f["state_mlstm_n"][0][..., None]], -1).transpose(2, 1, 0, 3),
        "m_state": np.repeat(f["state_mlstm_m"][0], DS, 0),
        "gdn_norm": f["gdn_norm_w"][0], "diff_norm": f["diff_norm_w"][0], "mlstm_norm": f["mlstm_norm_w"][0],
        "lambda_qk": f["lambda_qk"][0].reshape(-1),
        "pages": f["page_table"].reshape(1, -1),
        "cache_k": f["cache_k"][0].reshape(-1, 512), "cache_v": f["cache_v"][0].reshape(-1, 512),
    }
    return {k: np.ascontiguousarray(v) for k, v in a.items()}


def kernel(**inputs):
    import concourse.bacc as _bacc
    from concourse.bass_utils import run_bass_kernel_spmd as _run

    nc = _bacc.Bacc("TRN2", target_bir_lowering=False, num_devices=1)
    arrays, a, o = {}, {}, {}
    for name, x in {**laid_out(inputs), **constants()}.items():
        arrays[f"in_{name}"] = x
        a[name] = nc.dram_tensor(f"in_{name}", x.shape, mybir.dt.from_np(x.dtype), kind="ExternalInput").ap()
    for name, shape in OUTS.items():
        o[name] = nc.dram_tensor(f"out_{name}", shape, F32, kind="ExternalOutput").ap()
    build(nc, a, o)
    r = _run(nc, [arrays], core_ids=[0]).results[0]
    g = {name: r[f"out_{name}"] for name in OUTS}
    k, v = (g[n].reshape(ROWS, H, P) for n in ("k_rows", "v_rows"))
    cp = g["c_p"].transpose(1, 0, 2)
    cs = g["c_s"].transpose(2, 1, 0, 3)
    return (
        g["y"][:SEQ].reshape(1, SEQ, D), g["y"][SEQ:].reshape(NB, DS, D),
        k[:SEQ].reshape(1, 1, SEQ, H, P), v[:SEQ].reshape(1, 1, SEQ, H, P),
        k[SEQ:].reshape(1, NB, DS, H, P), v[SEQ:].reshape(1, NB, DS, H, P),
        g["conv_p"].transpose(2, 0, 1).reshape(1, 1, CONV - 1, CT * P),
        g["gdn_p"].transpose(1, 0, 2).reshape(1, 1, H, P, P),
        g["conv_s"].transpose(2, 3, 0, 1).reshape(1, NB, CONV - 1, CT * P),
        g["gdn_s"].transpose(2, 1, 0, 3).reshape(1, NB, H, P, P),
        cp[..., :DV].reshape(1, 1, H, P, DV), cp[..., DV].reshape(1, 1, H, P), g["m_p"].reshape(1, 1, H),
        cs[..., :DV].reshape(1, NB, H, P, DV), cs[..., DV].reshape(1, NB, H, P), g["m_s"][DS - 1::DS].reshape(1, NB, H),
    )
```
